# Optimizing a Trainium2 kernel written in Bass

```python
import jax
import jax.numpy as jnp
from jax import lax
import numpy as np
import math
import jax, jax.numpy as jnp

D_MODEL = 1024
BATCH = 1
SEQ = 256
DEPTH = 2

GRID_W = 64
MEM_LEN = 256
HEAD_DIM = 64
Q_BLOCK = 128
ROPE_THETA = 10000.0
LN_EPS = 1e-5
RMS_EPS = 1e-6
NA_HEADS = 4
NA_ROWS = 8
NA_COLS = 16
GQA_HEADS = 8
GQA_KV_HEADS = 2
GQA_GROUP = GQA_HEADS // GQA_KV_HEADS
MLA_HEADS = 4
MLA_Q_RANK = 256
MLA_KV_RANK = 128
MLA_NOPE = 64
MLA_ROPE = 32
MLA_V = 64
N_BRANCH = 3
A_WIDTH = NA_HEADS * HEAD_DIM
B_WIDTH = GQA_HEADS * HEAD_DIM
C_WIDTH = MLA_HEADS * MLA_V
IN_SPLITS = (A_WIDTH, A_WIDTH, A_WIDTH,
             B_WIDTH, GQA_KV_HEADS * HEAD_DIM, GQA_KV_HEADS * HEAD_DIM,
             MLA_Q_RANK, MLA_KV_RANK, MLA_ROPE,
             N_BRANCH * D_MODEL)
IN_COLS = sum(IN_SPLITS)
MEM_HEADS = 4
MEM_HEAD_DIM = D_MODEL // MEM_HEADS
D_FF = ((8 * D_MODEL // 3 + 127) // 128) * 128
N_EXPERTS = 8
TOP_K = 2
N_DENSE = (DEPTH + 1) // 2
N_MOE = DEPTH // 2
ALPHA = (2 * DEPTH) ** 0.25
BETA = (8 * DEPTH) ** -0.25


def layer_norm(x, g, b):
    xf = x.astype(jnp.float32)
    mu = jnp.mean(xf, axis=-1, keepdims=True)
    var = jnp.mean(jnp.square(xf - mu), axis=-1, keepdims=True)
    return ((xf - mu) * lax.rsqrt(var + LN_EPS) * g + b).astype(x.dtype)

def rms_norm(x, g):
    xf = x.astype(jnp.float32)
    return (xf * lax.rsqrt(jnp.mean(xf * xf, axis=-1, keepdims=True) + RMS_EPS) * g).astype(x.dtype)

def axial_rope_angles(seq, rot_dim):
    t = jnp.arange(seq)
    row = (t // GRID_W).astype(jnp.float32)
    col = (t % GRID_W).astype(jnp.float32)
    n = rot_dim // 4
    inv_freq = ROPE_THETA ** (-jnp.arange(n, dtype=jnp.float32) / n)
    ang = jnp.concatenate([row[:, None] * inv_freq, col[:, None] * inv_freq], axis=-1)
    return jnp.cos(ang), jnp.sin(ang)

def apply_rope(x, cos, sin):
    half = x.shape[-1] // 2
    xf = x.astype(jnp.float32)
    x1, x2 = xf[..., :half], xf[..., half:]
    c, s = cos[None, :, None, :], sin[None, :, None, :]
    return jnp.concatenate([x1 * c - x2 * s, x2 * c + x1 * s], axis=-1).astype(x.dtype)

def blocked_attention(q, k, v, scale):
    b, s, hkv, g, dk = q.shape
    nb = s // Q_BLOCK
    qb = q.reshape(b, nb, Q_BLOCK, hkv, g, dk).swapaxes(0, 1)

    def attend(q_blk):
        sc = jnp.einsum('bqhgd,bkhd->bhgqk', q_blk, k).astype(jnp.float32) * scale
        p = jax.nn.softmax(sc, axis=-1).astype(v.dtype)
        return jnp.einsum('bhgqk,bkhd->bqhgd', p, v)

    o = lax.map(attend, qb)
    return o.swapaxes(0, 1).reshape(b, s, hkv * g * v.shape[-1])

def neighborhood_attention(q, k, v, rpb):
    b, s, h, d = q.shape
    rows = s // GRID_W
    kr = min(NA_ROWS, rows)
    n_keys = kr * NA_COLS
    r = jnp.arange(rows)
    c = jnp.arange(GRID_W)
    key_r = jnp.clip(r - kr // 2, 0, rows - kr)[:, None] + jnp.arange(kr)
    key_c = jnp.clip(c - NA_COLS // 2, 0, GRID_W - NA_COLS)[:, None] + jnp.arange(NA_COLS)
    idx = (key_r[:, None, :, None] * GRID_W + key_c[None, :, None, :]).reshape(rows, GRID_W, n_keys)
    dr = key_r - r[:, None] + (NA_ROWS - 1)
    dc = key_c - c[:, None] + (NA_COLS - 1)
    bias = rpb[:, dr[:, None, :, None], dc[None, :, None, :]]
    bias = bias.reshape(h, rows, GRID_W, n_keys).transpose(1, 0, 2, 3)
    q_rows = q.reshape(b, rows, GRID_W, h, d).swapaxes(0, 1)
    scale = d ** -0.5

    def attend_row(args):
        q_r, idx_r, bias_r = args
        k_g = k[:, idx_r]
        v_g = v[:, idx_r]
        sc = jnp.einsum('bwhd,bwnhd->bhwn', q_r, k_g).astype(jnp.float32) * scale + bias_r.astype(jnp.float32)
        p = jax.nn.softmax(sc, axis=-1).astype(v.dtype)
        return jnp.einsum('bhwn,bwnhd->bwhd', p, v_g)

    o = lax.map(attend_row, (q_rows, idx, bias))
    return o.swapaxes(0, 1).reshape(b, s, h * d)

def hybrid_mixer(h, w_in, na_rpb, gqa_q_norm, gqa_k_norm, mla_q_norm, mla_kv_norm,
                 mla_w_uq, mla_w_ukv, w_proj_a, w_proj_b, w_proj_c, w_out, rope_b, rope_c):
    b, s, _ = h.shape
    z = h @ w_in
    (a_q, a_k, a_v, b_q, b_k, b_v, c_dq, c_dkv, c_kr, gate_logits) = jnp.split(
        z, np.cumsum(IN_SPLITS)[:-1].tolist(), axis=-1)

    ya = neighborhood_attention(a_q.reshape(b, s, NA_HEADS, HEAD_DIM),
                                a_k.reshape(b, s, NA_HEADS, HEAD_DIM),
                                a_v.reshape(b, s, NA_HEADS, HEAD_DIM), na_rpb)

    cos_b, sin_b = rope_b
    qb = apply_rope(rms_norm(b_q.reshape(b, s, GQA_HEADS, HEAD_DIM), gqa_q_norm), cos_b, sin_b)
    kb = apply_rope(rms_norm(b_k.reshape(b, s, GQA_KV_HEADS, HEAD_DIM), gqa_k_norm), cos_b, sin_b)
    vb = b_v.reshape(b, s, GQA_KV_HEADS, HEAD_DIM)
    yb = blocked_attention(qb.reshape(b, s, GQA_KV_HEADS, GQA_GROUP, HEAD_DIM), kb, vb, HEAD_DIM ** -0.5)

    cos_c, sin_c = rope_c
    qc = (rms_norm(c_dq, mla_q_norm) @ mla_w_uq).reshape(b, s, MLA_HEADS, MLA_NOPE + MLA_ROPE)
    q_nope, q_pe = qc[..., :MLA_NOPE], apply_rope(qc[..., MLA_NOPE:], cos_c, sin_c)
    kvc = (rms_norm(c_dkv, mla_kv_norm) @ mla_w_ukv).reshape(b, s, MLA_HEADS, MLA_NOPE + MLA_V)
    k_nope, vc = kvc[..., :MLA_NOPE], kvc[..., MLA_NOPE:]
    k_pe = apply_rope(c_kr[:, :, None, :], cos_c, sin_c)
    q_full = jnp.concatenate([q_nope, q_pe], axis=-1)[:, :, :, None, :]
    k_full = jnp.concatenate([k_nope, jnp.broadcast_to(k_pe, (b, s, MLA_HEADS, MLA_ROPE))], axis=-1)
    yc = blocked_attention(q_full, k_full, vc, (MLA_NOPE + MLA_ROPE) ** -0.5)

    gates = jax.nn.sigmoid(gate_logits.astype(jnp.float32)).astype(h.dtype).reshape(b, s, N_BRANCH, D_MODEL)
    merged = (gates[:, :, 0] * (ya @ w_proj_a)
              + gates[:, :, 1] * (yb @ w_proj_b)
              + gates[:, :, 2] * (yc @ w_proj_c))
    return merged @ w_out

def memory_cross_attention(h, mem, wq, wkv, wo):
    b, s, _ = h.shape
    m = mem.shape[1]
    q = (h @ wq).reshape(b, s, MEM_HEADS, MEM_HEAD_DIM)
    kv = (mem @ wkv).reshape(b, m, 2, MEM_HEADS, MEM_HEAD_DIM)
    k, v = kv[:, :, 0], kv[:, :, 1]
    sc = jnp.einsum('bqhd,bkhd->bhqk', q, k).astype(jnp.float32) * (MEM_HEAD_DIM ** -0.5)
    p = jax.nn.softmax(sc, axis=-1).astype(v.dtype)
    o = jnp.einsum('bhqk,bkhd->bqhd', p, v).reshape(b, s, D_MODEL)
    return o @ wo

def swiglu(t, w_gu, w_down):
    a, g = jnp.split(t @ w_gu, 2, axis=-1)
    return (jax.nn.silu(a) * g) @ w_down

def moe_swiglu(h, w_router, w_gu, w_down):
    b, s, d = h.shape
    t = h.reshape(b * s, d)
    logits = (t @ w_router).astype(jnp.float32)
    top_logit, top_idx = lax.top_k(logits, TOP_K)
    top_w = jax.nn.softmax(top_logit, axis=-1)
    gate = jnp.einsum('tk,tke->te', top_w,
                      jax.nn.one_hot(top_idx, N_EXPERTS, dtype=jnp.float32)).astype(h.dtype)
    out = jnp.zeros_like(t)
    for e in range(N_EXPERTS):
        out = out + gate[:, e:e + 1] * swiglu(t, w_gu[e], w_down[e])
    return out.reshape(b, s, d)

def first_inputs(seed: int = 0) -> dict:
    key = jax.random.key(seed)
    k = jax.random.split(key, 26)

    def nrm(kk, shape, std):
        return jax.random.normal(kk, shape, jnp.float32) * std

    def gain(kk, shape):
        return 1.0 + 0.05 * jax.random.normal(kk, shape, jnp.float32)

    return {
        'x': nrm(k[0], (BATCH, SEQ, D_MODEL), 1.0),
        'mem': nrm(k[1], (BATCH, MEM_LEN, D_MODEL), 1.0),
        'emb_ln_g': gain(k[2], (D_MODEL,)),
        'emb_ln_b': nrm(k[3], (D_MODEL,), 0.02),
        'w_in': nrm(k[4], (DEPTH, D_MODEL, IN_COLS), D_MODEL ** -0.5),
        'na_rpb': nrm(k[5], (DEPTH, NA_HEADS, 2 * NA_ROWS - 1, 2 * NA_COLS - 1), 0.1),
        'gqa_q_norm': gain(k[6], (DEPTH, HEAD_DIM)),
        'gqa_k_norm': gain(k[7], (DEPTH, HEAD_DIM)),
        'mla_q_norm': gain(k[8], (DEPTH, MLA_Q_RANK)),
        'mla_kv_norm': gain(k[9], (DEPTH, MLA_KV_RANK)),
        'mla_w_uq': nrm(k[10], (DEPTH, MLA_Q_RANK, MLA_HEADS * (MLA_NOPE + MLA_ROPE)), MLA_Q_RANK ** -0.5),
        'mla_w_ukv': nrm(k[11], (DEPTH, MLA_KV_RANK, MLA_HEADS * (MLA_NOPE + MLA_V)), MLA_KV_RANK ** -0.5),
        'w_proj_a': nrm(k[12], (DEPTH, A_WIDTH, D_MODEL), A_WIDTH ** -0.5),
        'w_proj_b': nrm(k[13], (DEPTH, B_WIDTH, D_MODEL), B_WIDTH ** -0.5),
        'w_proj_c': nrm(k[14], (DEPTH, C_WIDTH, D_MODEL), C_WIDTH ** -0.5),
        'w_out': nrm(k[15], (DEPTH, D_MODEL, D_MODEL), BETA * D_MODEL ** -0.5),
        'mem_wq': nrm(k[16], (DEPTH, D_MODEL, D_MODEL), D_MODEL ** -0.5),
        'mem_wkv': nrm(k[17], (DEPTH, D_MODEL, 2 * D_MODEL), D_MODEL ** -0.5),
        'mem_wo': nrm(k[18], (DEPTH, D_MODEL, D_MODEL), BETA * D_MODEL ** -0.5),
        'ln_g': gain(k[19], (DEPTH, 3, D_MODEL)),
        'ln_b': nrm(k[20], (DEPTH, 3, D_MODEL), 0.02),
        'ffn_w_gu': nrm(k[21], (N_DENSE, D_MODEL, 2 * D_FF), D_MODEL ** -0.5),
        'ffn_w_down': nrm(k[22], (N_DENSE, D_FF, D_MODEL), BETA * D_FF ** -0.5),
        'moe_router': nrm(k[23], (N_MOE, D_MODEL, N_EXPERTS), D_MODEL ** -0.5),
        'moe_w_gu': nrm(k[24], (N_MOE, N_EXPERTS, D_MODEL, 2 * D_FF), D_MODEL ** -0.5),
        'moe_w_down': nrm(k[25], (N_MOE, N_EXPERTS, D_FF, D_MODEL), BETA * D_FF ** -0.5),
    }

def first_block(x, mem, emb_ln_g, emb_ln_b, w_in, na_rpb, gqa_q_norm, gqa_k_norm, mla_q_norm,
              mla_kv_norm, mla_w_uq, mla_w_ukv, w_proj_a, w_proj_b, w_proj_c, w_out,
              mem_wq, mem_wkv, mem_wo, ln_g, ln_b, ffn_w_gu, ffn_w_down,
              moe_router, moe_w_gu, moe_w_down):
    s = x.shape[1]
    rope_b = axial_rope_angles(s, HEAD_DIM)
    rope_c = axial_rope_angles(s, MLA_ROPE)
    h = layer_norm(x, emb_ln_g, emb_ln_b)
    for l in range(DEPTH):
        mix = hybrid_mixer(h, w_in[l], na_rpb[l], gqa_q_norm[l], gqa_k_norm[l], mla_q_norm[l],
                           mla_kv_norm[l], mla_w_uq[l], mla_w_ukv[l], w_proj_a[l], w_proj_b[l],
                           w_proj_c[l], w_out[l], rope_b, rope_c)
        h = layer_norm(ALPHA * h + mix, ln_g[l, 0], ln_b[l, 0])
        xa = memory_cross_attention(h, mem, mem_wq[l], mem_wkv[l], mem_wo[l])
        h = layer_norm(ALPHA * h + xa, ln_g[l, 1], ln_b[l, 1])
        if l % 2 == 0:
            f = swiglu(h, ffn_w_gu[l // 2], ffn_w_down[l // 2])
        else:
            f = moe_swiglu(h, moe_router[l // 2], moe_w_gu[l // 2], moe_w_down[l // 2])
        h = layer_norm(ALPHA * h + f, ln_g[l, 2], ln_b[l, 2])
    return h


ROT_DIM = HEAD_DIM // 4
ROPE_THETA_2 = 500000.0
EPS = 1e-6
A_HEADS = 4
IDX_HEADS = 8
IDX_DIM = 64
INDEX_TOPK = 256
B_HEADS = 4
MOBA_BLOCK = 256
MOBA_TOPK = 3
MOBA_Q_CHUNK = 16
C_HEADS = 4
C_VDIM = 2 * HEAD_DIM
D_FF_2 = 2816

WIDTH_A = A_HEADS * HEAD_DIM
WIDTH_B = B_HEADS * HEAD_DIM
WIDTH_C = C_HEADS * C_VDIM
MIX_WIDTH = WIDTH_A + WIDTH_B + WIDTH_C
IN_SPLITS_2 = (A_HEADS * HEAD_DIM, HEAD_DIM, HEAD_DIM, IDX_HEADS * IDX_DIM, IDX_DIM, IDX_HEADS,
             B_HEADS * HEAD_DIM, B_HEADS * HEAD_DIM, B_HEADS * HEAD_DIM,
             C_HEADS * 2 * HEAD_DIM, C_HEADS * 2 * HEAD_DIM, C_HEADS * C_VDIM,
             D_MODEL, D_MODEL, D_MODEL)
IN_WIDTH = sum(IN_SPLITS_2)


def rmsnorm(x, g):
    xf = x.astype(jnp.float32)
    y = xf * lax.rsqrt(jnp.mean(xf * xf, axis=-1, keepdims=True) + EPS)
    return y.astype(x.dtype) * g

def rope_tables(positions):
    inv_freq = jnp.power(ROPE_THETA_2, -jnp.arange(0, ROT_DIM, 2, dtype=jnp.float32) / ROT_DIM)
    ang = positions.astype(jnp.float32)[..., None] * inv_freq
    return jnp.cos(ang), jnp.sin(ang)

def rope(x, cos, sin):
    shape = cos.shape[:2] + (1,) * (x.ndim - 3) + cos.shape[-1:]
    c = cos.reshape(shape).astype(x.dtype)
    s = sin.reshape(shape).astype(x.dtype)
    half = ROT_DIM // 2
    x1, x2 = x[..., :half], x[..., half:ROT_DIM]
    return jnp.concatenate([x1 * c - x2 * s, x2 * c + x1 * s, x[..., ROT_DIM:]], axis=-1)

def masked_softmax(scores, mask):
    return jax.nn.softmax(jnp.where(mask, scores.astype(jnp.float32), -jnp.inf), axis=-1)

def swiglu_2(h, w_gate, w_up, w_down):
    return (jax.nn.silu(h @ w_gate) * (h @ w_up)) @ w_down

def dsa_attention(q, k, v, qi, ki, wi):
    B, S = q.shape[:2]
    topk = min(INDEX_TOPK, S // 4)
    nb = S // Q_BLOCK
    s_pos = jnp.arange(S)
    b_idx = jnp.arange(B)[:, None, None]
    scale = HEAD_DIM ** -0.5

    def blk(t):
        return t.reshape((B, nb, Q_BLOCK) + t.shape[2:]).swapaxes(0, 1)

    def body(args):
        qb, qib, wib, start = args
        t = start + jnp.arange(Q_BLOCK)
        causal = s_pos[None, :] <= t[:, None]
        logits = jnp.einsum('bqhd,bsd->bqhs', qib, ki)
        iscore = jnp.einsum('bqhs,bqh->bqs', jax.nn.relu(logits).astype(jnp.float32), wib.astype(jnp.float32))
        iscore = jnp.where(causal[None], iscore, -jnp.inf)
        _, idx = lax.top_k(iscore, topk)
        k_sel = k[b_idx, idx]
        v_sel = v[b_idx, idx]
        sc = jnp.einsum('bqhd,bqkd->bhqk', qb, k_sel) * scale
        valid = (idx <= t[None, :, None])[:, None]
        p = masked_softmax(sc, valid).astype(v.dtype)
        return jnp.einsum('bhqk,bqkd->bqhd', p, v_sel)

    starts = jnp.arange(nb) * Q_BLOCK
    out = lax.map(body, (blk(q), blk(qi), blk(wi), starts))
    return out.swapaxes(0, 1).reshape(B, S, -1)

def moba_attention(q, k, v):
    B, S, H, d = q.shape
    nblk = -(-S // MOBA_BLOCK)
    pad = nblk * MOBA_BLOCK - S
    scale = d ** -0.5

    def to_blocks(t):
        t = jnp.pad(t, ((0, 0), (0, pad), (0, 0), (0, 0)))
        return t.reshape(B, nblk, MOBA_BLOCK, H, d).transpose(0, 3, 1, 2, 4)

    kbt, vbt = to_blocks(k), to_blocks(v)
    kmean = jnp.mean(kbt.astype(jnp.float32), axis=3).astype(k.dtype)
    n_sel = min(MOBA_TOPK, nblk)
    nc = S // MOBA_Q_CHUNK
    q_chunks = q.reshape(B, nc, MOBA_Q_CHUNK, H, d).transpose(1, 0, 3, 2, 4)
    b_idx = jnp.arange(B)[:, None, None, None]
    h_idx = jnp.arange(H)[None, :, None, None]
    blk_ids = jnp.arange(nblk)
    own_offsets = jnp.arange(MOBA_BLOCK)

    def body(args):
        qb, start = args
        t = start + jnp.arange(MOBA_Q_CHUNK)
        j = start // MOBA_BLOCK
        gate = jnp.einsum('bhqd,bhnd->bhqn', qb, kmean).astype(jnp.float32)
        gate = jnp.where(blk_ids < j, gate, -jnp.inf)
        _, sel = lax.top_k(gate, n_sel)
        sel_valid = sel < j
        k_sel = kbt[b_idx, h_idx, sel]
        v_sel = vbt[b_idx, h_idx, sel]
        s_sel = jnp.einsum('bhqd,bhqnkd->bhqnk', qb, k_sel) * scale
        s_sel = jnp.where(sel_valid[..., None], s_sel.astype(jnp.float32), -jnp.inf)
        s_sel = s_sel.reshape(B, H, MOBA_Q_CHUNK, n_sel * MOBA_BLOCK)
        k_own = lax.dynamic_index_in_dim(kbt, j, axis=2, keepdims=False)
        v_own = lax.dynamic_index_in_dim(vbt, j, axis=2, keepdims=False)
        s_own = jnp.einsum('bhqd,bhkd->bhqk', qb, k_own) * scale
        own_causal = (j * MOBA_BLOCK + own_offsets)[None, :] <= t[:, None]
        s_own = jnp.where(own_causal, s_own.astype(jnp.float32), -jnp.inf)
        p = jax.nn.softmax(jnp.concatenate([s_sel, s_own], axis=-1), axis=-1).astype(v.dtype)
        p_sel = p[..., :n_sel * MOBA_BLOCK].reshape(B, H, MOBA_Q_CHUNK, n_sel, MOBA_BLOCK)
        p_own = p[..., n_sel * MOBA_BLOCK:]
        return (jnp.einsum('bhqnk,bhqnkd->bhqd', p_sel, v_sel)
                + jnp.einsum('bhqk,bhkd->bhqd', p_own, v_own))

    starts = jnp.arange(nc) * MOBA_Q_CHUNK
    out = lax.map(body, (q_chunks, starts))
    return out.transpose(1, 0, 3, 2, 4).reshape(B, S, H * d)

def diff_attention(q, k, v, lam, lam_init, subln_g):
    B, S, H = q.shape[:3]
    nb = S // Q_BLOCK
    s_pos = jnp.arange(S)
    scale = HEAD_DIM ** -0.5
    q_blocks = q.reshape(B, nb, Q_BLOCK, H, 2, HEAD_DIM).swapaxes(0, 1)

    def body(args):
        qb, start = args
        t = start + jnp.arange(Q_BLOCK)
        causal = s_pos[None, :] <= t[:, None]
        sc = jnp.einsum('bqhcd,bshcd->bhcqs', qb, k) * scale
        p = masked_softmax(sc, causal)
        attn = (p[:, :, 0] - lam * p[:, :, 1]).astype(v.dtype)
        return jnp.einsum('bhqs,bshe->bqhe', attn, v)

    starts = jnp.arange(nb) * Q_BLOCK
    out = lax.map(body, (q_blocks, starts))
    out = out.swapaxes(0, 1).reshape(B, S, H, C_VDIM)
    out = rmsnorm(out, subln_g) * (1.0 - lam_init)
    return out.reshape(B, S, H * C_VDIM)

def hybrid_mixer_2(h, cos, sin, w_in, qk_g, lam_p, subln_g, w_branch, w_out, lam_init):
    B, S, _ = h.shape
    offsets = np.cumsum(IN_SPLITS_2)[:-1].tolist()
    proj = h @ w_in
    (qa, ka, va, qi, ki, wi, qb, kb, vb, qc, kc, vc, ga, gb, gc) = jnp.split(proj, offsets, axis=-1)
    qa = rope(rmsnorm(qa.reshape(B, S, A_HEADS, HEAD_DIM), qk_g[0]), cos, sin)
    ka = rope(rmsnorm(ka, qk_g[1]), cos, sin)
    qi = rope(qi.reshape(B, S, IDX_HEADS, IDX_DIM), cos, sin)
    ki = rope(ki, cos, sin)
    wi = wi * (IDX_HEADS * IDX_DIM) ** -0.5
    o_a = dsa_attention(qa, ka, va, qi, ki, wi)
    qb = rope(rmsnorm(qb.reshape(B, S, B_HEADS, HEAD_DIM), qk_g[2]), cos, sin)
    kb = rope(rmsnorm(kb.reshape(B, S, B_HEADS, HEAD_DIM), qk_g[3]), cos, sin)
    o_b = moba_attention(qb, kb, vb.reshape(B, S, B_HEADS, HEAD_DIM))
    qc = rope(rmsnorm(qc.reshape(B, S, C_HEADS, 2, HEAD_DIM), qk_g[4]), cos, sin)
    kc = rope(rmsnorm(kc.reshape(B, S, C_HEADS, 2, HEAD_DIM), qk_g[5]), cos, sin)
    lp = lam_p.astype(jnp.float32)
    lam = jnp.exp(jnp.sum(lp[0] * lp[1])) - jnp.exp(jnp.sum(lp[2] * lp[3])) + lam_init
    o_c = diff_attention(qc, kc, vc.reshape(B, S, C_HEADS, C_VDIM), lam, lam_init, subln_g)
    y_a = o_a @ w_branch[:WIDTH_A]
    y_b = o_b @ w_branch[WIDTH_A:WIDTH_A + WIDTH_B]
    y_c = o_c @ w_branch[WIDTH_A + WIDTH_B:]
    merged = jax.nn.sigmoid(ga) * y_a + jax.nn.sigmoid(gb) * y_b + jax.nn.sigmoid(gc) * y_c
    return merged @ w_out

def second_inputs(seed: int = 0) -> dict:
    key = jax.random.key(seed)
    ks = jax.random.split(key, 14)
    x = jax.random.normal(ks[0], (BATCH, SEQ, D_MODEL), jnp.float32)
    offset = jax.random.randint(ks[1], (BATCH, 1), 0, 4096, dtype=jnp.int32)
    positions = (offset + jnp.arange(SEQ, dtype=jnp.int32)[None, :]).astype(jnp.int32)
    norm_g = 1.0 + 0.02 * jax.random.normal(ks[2], (DEPTH, 3, D_MODEL), jnp.float32)
    w_in = jax.random.normal(ks[3], (DEPTH, D_MODEL, IN_WIDTH), jnp.float32) * D_MODEL ** -0.5
    qk_norm_g = 1.0 + 0.02 * jax.random.normal(ks[4], (DEPTH, 6, HEAD_DIM), jnp.float32)
    lambda_params = 0.1 * jax.random.normal(ks[5], (DEPTH, 4, HEAD_DIM), jnp.float32)
    diff_subln_g = 1.0 + 0.02 * jax.random.normal(ks[6], (DEPTH, C_VDIM), jnp.float32)
    w_branch = jnp.concatenate([
        jax.random.normal(ks[7], (DEPTH, WIDTH_A, D_MODEL), jnp.float32) * WIDTH_A ** -0.5,
        jax.random.normal(ks[8], (DEPTH, WIDTH_B, D_MODEL), jnp.float32) * WIDTH_B ** -0.5,
        jax.random.normal(ks[9], (DEPTH, WIDTH_C, D_MODEL), jnp.float32) * WIDTH_C ** -0.5], axis=1)
    w_out = jax.random.normal(ks[10], (DEPTH, D_MODEL, D_MODEL), jnp.float32) * D_MODEL ** -0.5
    ffn_w_gate = jax.random.normal(ks[11], (DEPTH, 2, D_MODEL, D_FF_2), jnp.float32) * D_MODEL ** -0.5
    ffn_w_up = jax.random.normal(ks[12], (DEPTH, 2, D_MODEL, D_FF_2), jnp.float32) * D_MODEL ** -0.5
    ffn_w_down = jax.random.normal(ks[13], (DEPTH, 2, D_FF_2, D_MODEL), jnp.float32) * D_FF_2 ** -0.5
    return {'x': x, 'positions': positions, 'norm_g': norm_g, 'w_in': w_in, 'qk_norm_g': qk_norm_g,
            'lambda_params': lambda_params, 'diff_subln_g': diff_subln_g, 'w_branch': w_branch,
            'w_out': w_out, 'ffn_w_gate': ffn_w_gate, 'ffn_w_up': ffn_w_up, 'ffn_w_down': ffn_w_down}

def second_block(x, positions, norm_g, w_in, qk_norm_g, lambda_params, diff_subln_g, w_branch,
              w_out, ffn_w_gate, ffn_w_up, ffn_w_down):
    cos, sin = rope_tables(positions)
    for layer in range(DEPTH):
        lam_init = 0.8 - 0.6 * math.exp(-0.3 * layer)
        x = x + 0.5 * swiglu_2(rmsnorm(x, norm_g[layer, 0]), ffn_w_gate[layer, 0], ffn_w_up[layer, 0], ffn_w_down[layer, 0])
        x = x + hybrid_mixer_2(rmsnorm(x, norm_g[layer, 1]), cos, sin, w_in[layer], qk_norm_g[layer],
                             lambda_params[layer], diff_subln_g[layer], w_branch[layer], w_out[layer], lam_init)
        x = x + 0.5 * swiglu_2(rmsnorm(x, norm_g[layer, 2]), ffn_w_gate[layer, 1], ffn_w_up[layer, 1], ffn_w_down[layer, 1])
    return x


def setup_inputs(seed=0):
    out = dict(first_inputs(seed))
    for name, value in second_inputs(seed + 1).items():
        if name != "x":
            out[name + "_2"] = value
    return out


def reference(
    x, mem, emb_ln_g, emb_ln_b, w_in, na_rpb, gqa_q_norm, gqa_k_norm, mla_q_norm, mla_kv_norm,
    mla_w_uq, mla_w_ukv, w_proj_a, w_proj_b, w_proj_c, w_out, mem_wq, mem_wkv, mem_wo, ln_g,
    ln_b, ffn_w_gu, ffn_w_down, moe_router, moe_w_gu, moe_w_down, positions_2, norm_g_2, w_in_2,
    qk_norm_g_2, lambda_params_2, diff_subln_g_2, w_branch_2, w_out_2, ffn_w_gate_2, ffn_w_up_2,
    ffn_w_down_2,
):
    x = first_block(
        x, mem, emb_ln_g, emb_ln_b, w_in, na_rpb, gqa_q_norm, gqa_k_norm, mla_q_norm,
        mla_kv_norm, mla_w_uq, mla_w_ukv, w_proj_a, w_proj_b, w_proj_c, w_out, mem_wq, mem_wkv,
        mem_wo, ln_g, ln_b, ffn_w_gu, ffn_w_down, moe_router, moe_w_gu, moe_w_down,
    )
    return second_block(
        x, positions_2, norm_g_2, w_in_2, qk_norm_g_2, lambda_params_2, diff_subln_g_2,
        w_branch_2, w_out_2, ffn_w_gate_2, ffn_w_up_2, ffn_w_down_2,
    )


_drawn_inputs = setup_inputs


def setup_inputs(seed=0):
    import zlib

    import numpy as np

    out = dict(_drawn_inputs(seed))
    spreads = {}
    factors = {'na_rpb': 2.678,
     'gqa_q_norm': 7.368,
     'gqa_k_norm': 7.962,
     'mla_q_norm': 4.23,
     'mla_kv_norm': 3.431,
     'qk_norm_g_2': 3.703,
     'diff_subln_g_2': 4.268}
    for name, (base, spread) in spreads.items():
        noise = np.random.default_rng([zlib.crc32(name.encode()), seed]).standard_normal(out[name].shape)
        drawn = base * np.exp(spread * noise) if base else spread * noise
        out[name] = jnp.asarray(drawn.astype(out[name].dtype))
    for name, factor in factors.items():
        out[name] = (out[name] * factor).astype(out[name].dtype)
    return out
```

```python
from contextlib import ExitStack
import numpy as np
import concourse.bass as bass
from concourse import mybir

F32, F32R, BF16 = mybir.dt.float32, mybir.dt.float32r, mybir.dt.bfloat16
I32, U32 = mybir.dt.int32, mybir.dt.uint32
ALU, ACT, AX = mybir.AluOpType, mybir.ActivationFunctionType, mybir.AxisListType

P = 128
SEQ, D = 256, 1024
NT = SEQ // P
KT = D // P
CH = 512
DEPTH = 2
ALPHA = (2 * DEPTH) ** 0.25
NEG = -1.0e30
GONE = -3.0e38

GRID_W, NA_ROWS, NA_COLS = 64, 8, 16
ROWS = SEQ // GRID_W
NA_HEADS, GQA_HEADS, GQA_KV, MLA_HEADS, MEM_HEADS, HD = 4, 8, 2, 4, 4, 64
NOPE, ROPE_C, VC = 64, 32, 64
QR, KVR = 256, 128
DFF = 2816
HCH = CH // 2
NFF = DFF // HCH
EXPERTS = 8
GATES = 3 * D

AQ, AK, AV = 0, 256, 512
BQ, BK, BV = 768, 1280, 1408
CDQ, CDKV, CKR, MAIN1 = 1536, 1792, 1920, 1952
A2Q, A2K, A2V, IQ, IK, IW = 0, 256, 320, 384, 896, 960
B2Q, B2K, B2V, C2Q, C2K, C2V, MAIN2 = 968, 1224, 1480, 1736, 2248, 2760, 3272
IDX_HEADS, TOPK = 8, 64
ROT2 = 16


class Chain:

    def __init__(self, eng, sem, seen):
        self.eng, self.sem, self.n, self.seen = eng, sem, 0, seen

    def wait(self, *tokens):
        for t in tokens:
            if t is None:
                continue
            sem, value = t
            if isinstance(value, int) and value <= self.seen.get(id(sem), 0):
                continue
            if isinstance(value, int):
                self.seen[id(sem)] = value
            self.eng.wait_ge(sem, value)

    def last(self):
        return (self.sem, self.n) if self.n else None

    def run(self, fn, *args, after=(), **kw):
        self.wait(*after, self.last())
        fn(*args, **kw).then_inc(self.sem, 1)
        self.n += 1
        return self.last()

    def mark(self, ins):
        ins.then_inc(self.sem, 1)
        self.n += 1
        return self.last()


def program(nc, A, C, out, stop=None):
    ctx = ExitStack()
    with ctx:
        def sb(name, shape, dt=F32):
            return ctx.enter_context(nc.sbuf_tensor(name, shape, dt))

        def sem(name):
            return ctx.enter_context(nc.semaphore(name))

        rawg = sb("raw_gu", [P, KT, CH])
        rawd = sb("raw_down", [P, 2, D])
        wh = sb("w_hi", [P, 2, KT, CH], F32R)
        wl = sb("w_lo", [P, 2, KT, CH], F32R)
        dh = sb("down_hi", [P, 2, D], F32R)
        dl = sb("down_lo", [P, 2, D], F32R)
        xh = sb("xT_hi", [P, KT, SEQ], F32R)
        xl = sb("xT_lo", [P, KT, SEQ], F32R)
        hh = sb("hiddenT_hi", [P, 2, SEQ], F32R)
        hl = sb("hiddenT_lo", [P, 2, SEQ], F32R)
        H = sb("residual", [P, NT, D])
        U = sb("token_scratch", [P, NT, D])
        Z = sb("projected", [P, NT, MAIN2])
        G = sb("gates", [P, NT, GATES])
        S = sb("scratch", [P, 5120])
        pb = sb("row_params", [P, 768])
        ident = sb("ident", [P, P])
        cmask = sb("causal", [P, NT, SEQ])
        ropeb = sb("rope_b", [P, NT, 2, HD])
        ropec = sb("rope_c", [P, NT, 2, ROPE_C])
        rope2 = sb("rope_2", [P, NT, 2, ROT2])
        cols = sb("col_params", [P, 54])
        mhalf = sb("minus_half", [P, 64])
        st = sb("stats", [P, NT, 2, 6])
        mv = sb("mean_var", [P, NT, 2])
        ss = sb("sums", [P, 64])
        rs = sb("rstd", [P, 64])
        zb = sb("zeros", [P, CH], BF16)
        lam = sb("lambda", [P, 8])
        rh, rl = sb("router_hi", [P, KT, EXPERTS], F32R), sb("router_lo", [P, KT, EXPERTS], F32R)
        gt = pb[:, 256:256 + NT * EXPERTS * NFF].rearrange("p (t n) -> p t n", t=NT)
        rw = pb[:, 448:448 + KT * EXPERTS].rearrange("p (k e) -> p k e", e=EXPERTS)
        lg = sb("router_stats", [P, 8, 8])
        iota = sb("expert_numbers", [P, EXPERTS])
        pos = sb("positions", [P, NT], I32)
        invf = sb("inverse_frequencies", [P, ROT2 // 2])

        QKT = S[:, 0:2048].rearrange("p (b k n) -> p b k n", b=2, k=2)
        SM = S[:, 2048:3072].rearrange("p (b t n) -> p b t n", b=2, t=2)
        PR = S[:, 3072:4096].rearrange("p (b t n) -> p b t n", b=2, t=2)
        PT = S[:, 4096:5120].rearrange("p (b k n) -> p b k n", b=2, k=2)
        SG = S[:, 2048:2560].rearrange("p (t n) -> p t n", t=2)
        HB = S[:, 2560:3072].rearrange("p (t n) -> p t n", t=2)
        GR, BR = S[:, 0:D], S[:, D:2 * D]
        nab = rawd[:, :, :].rearrange("p t (h n) -> p t h n", n=SEQ)
        ISC = rawd[:, 0, 0:NT * SEQ].rearrange("p (t n) -> p t n", t=NT)
        SEL = rawd[:, 1, 0:NT * SEQ].rearrange("p (t n) -> p t n", t=NT)

        bank = [ctx.enter_context(nc.psum_tensor(f"bank{i}", [P, CH], F32)) for i in range(8)]

        def halves(b):
            return bank[b][:, :].rearrange("p (a n) -> p a n", a=2)

        s_ld, s_ldd = sem("w_loaded"), sem("down_loaded")
        s_hi, s_lo, s_hid, s_lod = sem("w_hi_cut"), sem("w_lo_cut"), sem("down_hi_cut"), sem("down_lo_cut")
        s_mm, s_ev = sem("product_done"), sem("product_read")
        s_si, s_tr, s_hth, s_htl, s_dn = sem("silu"), sem("hidden_turned"), sem("hiddenT_hi_cut"), sem(
            "hiddenT_lo_cut"), sem("down_done")
        s_out = sem("stored")
        s_snap = sem("snap")
        small = [sem(f"small{i}") for i in range(8)]
        SP = Chain(nc.sync, sem("sp"), {})
        PE = Chain(nc.tensor, sem("pe"), {})
        DV = Chain(nc.vector, sem("dve"), {})
        AC = Chain(nc.scalar, sem("act"), {})
        PO = Chain(nc.gpsimd, sem("pool"), {})
        V, T, K, Q, Y = nc.vector, nc.tensor, nc.scalar, nc.gpsimd, nc.sync
        engines = (SP, PE, DV, AC, PO)

        class Count:
            pass
        c = Count()
        c.step = 0
        c.loads = 0
        c.ff = 0
        c.ffl = 0
        c.more, c.more_last = {}, 0
        c.small = 0
        c.snap = 0
        c.smallv = [0] * 8

        def at_least(chain, s, value):
            if isinstance(value, int):
                if value > 0:
                    chain.wait((s, value))
            else:
                chain.eng.wait_ge(s, value)

        def small_loads(pairs, after=()):
            k = c.small % 8
            PO.wait(*after, (small[k], c.smallv[k]) if c.smallv[k] else None)
            for dst, src in pairs:
                Q.dma_start(dst, src, allow_slow_non_contiguous=True).then_inc(small[k], 16)
            c.smallv[k] += 16 * len(pairs)
            c.small += 1
            return (small[k], c.smallv[k])

        def load_step(srcs, n=None):
            s = c.loads if n is None else n
            at_least(SP, s_lo, 2 * s)
            for dst, src in srcs:
                Y.dma_start(dst, src).then_inc(s_ld, 16)
            if n is None:
                c.more[s] = c.more.get(s - 1, c.more_last) + len(srcs) - 2
                c.more_last = c.more[s]
                c.loads += 1

        def linear_loads(w, c0, width):
            v = w.rearrange("(k p) n -> p k n", p=P)
            load_step([(rawg[:, 4 * u:4 * u + 4, 0:width], v[:, 4 * u:4 * u + 4, c0:c0 + width])
                       for u in range(2)])

        def cut(s, par, width=CH, at=None):
            more = 16 * c.more.get(s if at is None else at, c.more_last)
            for u in range(2):
                src = rawg[:, 4 * u:4 * u + 4, 0:width]
                hi = wh[:, par, 4 * u:4 * u + 4, 0:width]
                at_least(AC, s_ld, 32 * (s + 1) + more)
                at_least(AC, s_mm, 2 * (s - 1))
                K.copy(hi, src).then_inc(s_hi, 1)
                at_least(DV, s_hi, 2 * s + u + 1)
                V.tensor_tensor(wl[:, par, 4 * u:4 * u + 4, 0:width], src, hi.bitcast(F32),
                                ALU.subtract).then_inc(s_lo, 1)

        def three(acc, xk, wk, t, start, stop):
            (ah, al), (bh, bl) = xk, wk
            tok = slice(t * P, (t + 1) * P)
            T.matmul(acc, ah[:, tok], bh, start=start, stop=False)
            T.matmul(acc, ah[:, tok], bl, start=False, stop=False)
            return T.matmul(acc, al[:, tok], bh, start=False, stop=stop)

        def multiply(s, par, width=CH, groups=None):
            groups = groups or [(4, 5, range(KT))]
            for t in range(NT):
                at_least(PE, s_ev, 2 * s - 1 + t)
                for b in groups:
                    for k in b[2]:
                        if t == 0:
                            at_least(PE, s_lo, 2 * s + 1 + k // 4)
                        mm = three(bank[b[t]][:, 0:width], (xh[:, k, :], xl[:, k, :]),
                                   (wh[:, par, k, 0:width], wl[:, par, k, 0:width]), t,
                                   k == b[2][0], k == b[2][-1])
                mm.then_inc(s_mm, 1)

        def linear(n, evac, widths=None, next_width=CH, groups=None, last=False):
            base = c.step
            PE.wait(products_read())

            def one(i, j):
                s = base + i
                par = (base + j) % 2
                w_next = CH
                if isinstance(i, int):
                    w_next = widths[i + 1] if widths and i + 1 < n else (next_width if i + 1 == n else CH)
                if not (last and isinstance(i, int) and i == n - 1):
                    cut(s + 1, 1 - par, w_next, at=base + j + 1)
                multiply(s, par, widths[i] if widths and isinstance(i, int) else CH, groups)
                for t in range(NT):
                    evac(i, t, (s_mm, 2 * s + t + 1))

            pairs = (n - 2) // 2 if n >= 6 else 0
            if pairs:
                with nc.Fori(0, pairs) as r:
                    for j in range(2):
                        one(r * 2 + j, j)
                forget()
            for i in range(2 * pairs, n):
                one(i, i)
            c.step += n

        def products_read():
            return (s_ev, 2 * c.step)

        def forget():
            for e in engines:
                e.seen.clear()

        def turn(src, gain=None, after=()):
            done = {}
            PE.wait(*after)
            for r in range(KT // 2):
                b = 6 + r % 2
                for kk in range(2):
                    k = 2 * r + kk
                    for t in range(NT):
                        PE.wait(done.get(r - 2))
                        i = T.transpose(bank[b][:, kk * SEQ + t * P:kk * SEQ + (t + 1) * P],
                                        src[:, t, k * P:(k + 1) * P], ident[:, :])
                turned = PE.mark(i)
                if gain is None:
                    hi = AC.run(K.copy, xh[:, 2 * r:2 * r + 2, :], halves(b), after=[turned])
                    done[r] = DV.run(V.tensor_tensor, xl[:, 2 * r:2 * r + 2, :], halves(b),
                                     xh[:, 2 * r:2 * r + 2, :].bitcast(F32), ALU.subtract, after=[hi])
                else:
                    for k in (2 * r, 2 * r + 1):
                        hi = AC.run(K.activation, xh[:, k, :], halves(b)[:, k - 2 * r, :], ACT.Copy,
                                    scale=gain[:, k:k + 1], after=[turned])
                    for k in (2 * r, 2 * r + 1):
                        done[r] = DV.run(V.scalar_tensor_tensor, xl[:, k, :], halves(b)[:, k - 2 * r, :],
                                         gain[:, k:k + 1], xh[:, k, :].bitcast(F32), ALU.mult,
                                         ALU.subtract, after=[hi])
            return done[KT // 2 - 1]

        def ffn_loads(s, wa, wg, cc):
            load_step([(rawg[:, :, m * HCH:(m + 1) * HCH],
                        w.rearrange("(k p) n -> p k n", p=P)[:, :, bass.ds(cc * HCH, HCH)])
                       for m, w in enumerate((wa, wg))], n=s)

        def ffn_all_loads(wa, wg):
            if len(wa.shape) == 2:
                with nc.sync.Fori(0, NFF) as i:
                    ffn_loads(i + c.loads, wa, wg, i)
                c.loads += NFF
            else:
                with nc.sync.Fori(0, EXPERTS) as e:
                    with nc.sync.Fori(0, NFF) as i:
                        ffn_loads(e * NFF + i + c.loads, wa[e], wg[e], i)
                c.loads += EXPERTS * NFF
            SP.seen.clear()

        def ffn(n, wd, gate=None, after=(), last=False):
            s0, g0 = c.step, c.ff

            def load_down(i):
                at_least(AC, s_lod, g0 + i)
                K.dma_start(rawd[:, :, :], wd[bass.ds(i * HCH, HCH), :].rearrange("(k p) n -> p k n", p=P)
                            ).then_inc(s_ldd, 16)

            PE.wait(*after, products_read())
            DV.wait(*after)
            AC.wait(*after)
            load_down(0)
            for b in range(4):
                T.matmul(bank[b][:, :], zb[:, 0:P], zb[:, :], start=True, stop=False)

            def down(g, stop=False):
                at_least(PE, s_lod, g + 1)
                at_least(PE, s_htl, g + 1)
                for t in range(NT):
                    tok = slice(t * P, (t + 1) * P)
                    for k in range(2):
                        for xx, ww in ((hh, dh), (hh, dl), (hl, dh)):
                            for m in range(2):
                                mm = T.matmul(bank[2 * t + m][:, :], xx[:, k, tok], ww[:, k, m * CH:(m + 1) * CH],
                                              start=False, stop=stop and k == 1 and xx is hl)
                mm.then_inc(s_dn, 1)

            def slot(i, j, first=False, cut_next=True, more=True):
                s, g, par = s0 + i, g0 + i, (s0 + j) % 2
                if cut_next:
                    cut(s + 1, 1 - par, CH, at=s0 + j + 1)
                multiply(s, par)
                if not first:
                    down(g - 1)
                for t in range(NT):
                    at_least(AC, s_mm, 2 * s + t + 1)
                    at_least(AC, s_ev, 2 * s - 1 + t)
                    K.activation(SG[:, t, :], bank[4 + t][:, 0:HCH], ACT.Silu).then_inc(s_si, 1)
                    at_least(DV, s_si, 2 * g + t + 1)
                    at_least(DV, s_tr, g)
                    V.scalar_tensor_tensor(HB[:, t, :], SG[:, t, :], gate(i, t) if gate else 1.0,
                                           bank[4 + t][:, HCH:CH], ALU.mult, ALU.mult).then_inc(s_ev, 1)
                for t in range(NT):
                    at_least(PE, s_ev, 2 * s + t + 1)
                    at_least(PE, s_htl, g)
                    for k in range(2):
                        tr = T.transpose(bank[6][:, k * SEQ + t * P:k * SEQ + (t + 1) * P],
                                         HB[:, t, k * P:(k + 1) * P], ident[:, :])
                tr.then_inc(s_tr, 1)
                at_least(AC, s_ldd, 16 * (g + 1))
                at_least(AC, s_dn, g)
                K.copy(dh[:, :, :], rawd[:, :, :]).then_inc(s_hid, 1)
                at_least(DV, s_hid, g + 1)
                V.tensor_tensor(dl[:, :, :], rawd[:, :, :], dh[:, :, :].bitcast(F32), ALU.subtract).then_inc(s_lod, 1)
                at_least(AC, s_tr, g + 1)
                K.copy(hh[:, :, :], halves(6)).then_inc(s_hth, 1)
                at_least(DV, s_hth, g + 1)
                V.tensor_tensor(hl[:, :, :], halves(6), hh[:, :, :].bitcast(F32), ALU.subtract).then_inc(s_htl, 1)
                if more:
                    load_down(i + 1)

            AC.eng.preload_act_table(ACT.Silu)
            slot(0, 0, first=True)
            pairs = (n - 2) // 2
            with nc.Fori(0, pairs) as r:
                for j in range(2):
                    slot(r * 2 + (1 + j), 1 + j)
            forget()
            for i in range(1 + 2 * pairs, n):
                slot(i, i, cut_next=not (last and i == n - 1), more=i < n - 1)
            down(g0 + n - 1, stop=True)
            c.step += n
            c.ff += n
            return (s_dn, c.ff)

        def rsqrt(dst, src, after=()):
            return PO.run(Q.tensor_tensor, dst, src, mhalf[:, 0:src.shape[1]], ALU.pow, after=after)

        def layer_norm(g, b, after=()):
            rows = small_loads([(GR, g.partition_broadcast(P)), (BR, b.partition_broadcast(P))], after=after)
            DV.wait(*after)
            for t in range(NT):
                for m in range(2):
                    DV.run(V.bn_stats, st[:, t, m, :], U[:, t, m * CH:(m + 1) * CH])
                DV.run(V.bn_aggr, mv[:, t, :], st[:, t, :, :].rearrange("p a b -> p (a b)"))
                e = DV.run(V.tensor_scalar, ss[:, t:t + 1], mv[:, t, 1:2], 1e-5, None, ALU.add)
                r = rsqrt(rs[:, t:t + 1], ss[:, t:t + 1], after=[e])
                DV.run(V.tensor_scalar, H[:, t, :], U[:, t, :], mv[:, t, 0:1], rs[:, t:t + 1],
                       ALU.subtract, ALU.mult, after=[r])
                DV.run(V.tensor_tensor, H[:, t, :], H[:, t, :], GR, ALU.mult, after=[rows])
                DV.run(V.tensor_tensor, H[:, t, :], H[:, t, :], BR, ALU.add)
            return DV.last()

        def rms_rows(x, y, width, eps, col, after=()):
            DV.run(V.tensor_tensor_reduce, S[:, 0:width], x, x, 1.0, 0.0, ALU.mult, ALU.add,
                   ss[:, col:col + 1], after=after)
            e = DV.run(V.tensor_scalar, ss[:, col:col + 1], ss[:, col:col + 1], 1.0 / width, eps, ALU.mult, ALU.add)
            r = rsqrt(rs[:, col:col + 1], ss[:, col:col + 1], after=[e])
            return DV.run(V.tensor_scalar, y, x, rs[:, col:col + 1], None, ALU.mult, after=[r])

        def head_norm(c0, heads, gains):
            n = NT * heads
            for t in range(NT):
                x = Z[:, t, c0:c0 + heads * HD]
                sq = S[:, 0:heads * HD]
                DV.run(V.tensor_tensor, sq, x, x, ALU.mult)
                DV.run(V.tensor_reduce, ss[:, t * heads:(t + 1) * heads], sq.rearrange("p (h d) -> p h d", d=HD),
                       AX.X, ALU.add)
            e = DV.run(V.tensor_scalar, ss[:, 0:n], ss[:, 0:n], 1.0 / HD, 1e-6, ALU.mult, ALU.add)
            r = rsqrt(rs[:, 0:n], ss[:, 0:n], after=[e])
            for t in range(NT):
                x = Z[:, t, c0:c0 + heads * HD].rearrange("p (h d) -> p h d", d=HD)
                f = rs[:, t * heads:(t + 1) * heads].unsqueeze(2).to_broadcast([P, heads, HD])
                DV.run(V.tensor_tensor, x, x, f, ALU.mult, after=[r])
                for h0, nh, row in gains:
                    y = x[:, h0:h0 + nh, :]
                    DV.run(V.tensor_tensor, y, y, row.unsqueeze(1).to_broadcast([P, nh, HD]), ALU.mult)

        def rotate(x, heads, half, table):
            a = S[:, 0:heads * 2 * half].rearrange("p (h d) -> p h d", h=heads)
            b = S[:, 1024:1024 + heads * 2 * half].rearrange("p (h d) -> p h d", h=heads)
            cc = table[:, 0, :].unsqueeze(1).to_broadcast([P, heads, 2 * half])
            s1 = table[:, 1, 0:half].unsqueeze(1).to_broadcast([P, heads, half])
            s2 = table[:, 1, half:2 * half].unsqueeze(1).to_broadcast([P, heads, half])
            DV.run(V.tensor_tensor, a, x[:, :, 0:2 * half], cc, ALU.mult)
            DV.run(V.tensor_tensor, b[:, :, 0:half], x[:, :, half:2 * half], s1, ALU.mult)
            DV.run(V.tensor_tensor, b[:, :, half:2 * half], x[:, :, 0:half], s2, ALU.mult)
            return DV.run(V.tensor_tensor, x[:, :, 0:2 * half], a, b, ALU.add)

        def heads3(x, c0, heads, d=HD):
            return x[:, c0:c0 + heads * d].rearrange("p (h d) -> p h d", d=d)

        def attention(heads, after):
            for e in (PE, DV, AC):
                e.wait(*after)
            n = len(heads)
            qkc, sc, ex, rc, ptc, ov, of = {}, {}, {}, {}, {}, {}, {}

            def turn_qk(h):
                d = heads[h]
                for k in range(d["nk"]):
                    b = 6 + (h + k) % 2
                    PE.wait(qkc.get(h - 1 if d["nk"] == 2 else h - 2))
                    if d["nk"] == 2 and k == 0:
                        PE.wait(qkc.get(h - 1))
                    dk = d["dk"]
                    for j in range(2):
                        for t in range(NT):
                            i = T.transpose(bank[b][0:dk, (2 * j + t) * P:(2 * j + t + 1) * P],
                                            (d["q"], d["k"])[j](t, k), ident[:, :])
                    turned = PE.mark(i)
                    qkc[h] = AC.run(K.copy, QKT[0:dk, h % 2, k, :], bank[b][0:dk, :],
                                    after=[turned, sc.get(h - 2)])

            def score(h):
                d, b = heads[h], h % 2
                dk = d["dk"]
                PE.wait(qkc[h], ex.get(h - 2), rc.get(("m", h - 2)))
                for t in range(NT):
                    for k in range(d["nk"]):
                        i = T.matmul(halves(b)[:, t, :], QKT[0:dk, b, k, t * P:(t + 1) * P],
                                     QKT[0:dk, b, k, SEQ:2 * SEQ], start=k == 0, stop=k == d["nk"] - 1)
                sc[h] = PE.mark(i)
                x, f = halves(b), d["scale"]
                if d["bias"] is not None:
                    for t in range(NT):
                        DV.run(V.scalar_tensor_tensor, SM[:, b, t, :], halves(b)[:, t, :], f, d["bias"][:, t, :],
                               ALU.mult, ALU.add, after=[sc[h], ex.get(h - 2)])
                    x, f = SM[:, b, :, :], 1.0
                mx = ss[:, 4 * b:4 * b + 2]
                DV.run(V.tensor_reduce, mx, x, AX.X, ALU.max, after=[sc[h]])
                rc[("m", h)] = DV.run(V.tensor_scalar, rs[:, 4 * b:4 * b + 2], mx, -f, None, ALU.mult,
                                      after=[ex.get(h - 2)])
                for t in range(NT):
                    ex[h] = AC.run(K.activation, PR[:, b, t, :], x[:, t, :], ACT.Exp,
                                   bias=rs[:, 4 * b + t:4 * b + t + 1], scale=f,
                                   accum_out=ss[:, 8 + 4 * b + t:9 + 4 * b + t],
                                   after=[rc[("m", h)], ptc.get(("pe", h - 2)), rc.get(h - 2)])
                rc[h] = DV.run(V.reciprocal, rs[:, 8 + 4 * b:10 + 4 * b], ss[:, 8 + 4 * b:10 + 4 * b],
                               after=[ex[h]])

            def turn_p(h):
                b = h % 2
                PE.wait(ex[h], ptc.get(h - 2))
                for k in range(NT):
                    for t in range(NT):
                        i = T.transpose(halves(2 + b)[:, k, t * P:(t + 1) * P], PR[:, b, t, k * P:(k + 1) * P],
                                        ident[:, :])
                ptc[("pe", h)] = PE.mark(i)
                ptc[h] = DV.run(V.tensor_copy, PT[:, b, :, :], halves(2 + b), after=[ptc[("pe", h)], ov.get(h - 2)])

            def value(h):
                d, b = heads[h], h % 2
                dv = d["dv"]
                PE.wait(ptc[h], of.get(h - 2))
                for t in range(NT):
                    for k in range(NT):
                        i = T.matmul(halves(4 + b)[:, t, 0:dv], PT[:, b, k, t * P:(t + 1) * P], d["v"](k),
                                     start=k == 0, stop=k == 1)
                ov[h] = PE.mark(i)
                for t in range(NT):
                    r = rs[:, 8 + 4 * b + t:9 + 4 * b + t]
                    if d["weight"] is None:
                        of[h] = DV.run(V.tensor_scalar, d["out"](t), halves(4 + b)[:, t, 0:dv], r, None, ALU.mult,
                                       after=[ov[h]])
                    else:
                        DV.run(V.tensor_tensor, r, r, d["weight"], ALU.mult)
                        of[h] = DV.run(V.scalar_tensor_tensor, d["out"](t), halves(4 + b)[:, t, 0:dv], r,
                                       d["out"](t), ALU.mult, ALU.add, after=[ov[h]])

            for i in range(n + 3):
                if 0 <= i - 3 < n:
                    value(i - 3)
                if 0 <= i - 2 < n:
                    turn_p(i - 2)
                if 0 <= i - 1 < n:
                    score(i - 1)
                if i < n:
                    turn_qk(i)
            return DV.last()

        def head(q, k, v, out_, scale, dk=HD, dv=HD, nk=1, bias=None, weight=None):
            return dict(q=q, k=k, v=v, out=out_, scale=scale, dk=dk, dv=dv, nk=nk, bias=bias, weight=weight)

        def zc(c0, w=HD):
            return lambda t, k=0: Z[:, t, c0 + k * w:c0 + (k + 1) * w]

        def uc(c0, w=HD):
            return lambda t: U[:, t, c0:c0 + w]

        def to_tokens(dst, widths=None):
            def evac(i, t, done):
                w = widths[i] if widths and isinstance(i, int) else CH
                at_least(DV, *done)
                V.tensor_copy(dst[:, t, bass.ds(i * CH, w)], bank[4 + t][:, 0:w]).then_inc(s_ev, 1)
            return evac

        def to_gates(i, t, done):
            at_least(AC, *done)
            K.activation(G[:, t, bass.ds(i * CH, CH)], bank[4 + t][:, :], ACT.Sigmoid).then_inc(s_ev, 1)

        def add_residual(i, t, done):
            at_least(DV, *done)
            V.scalar_tensor_tensor(U[:, t, i * CH:(i + 1) * CH], H[:, t, i * CH:(i + 1) * CH], ALPHA,
                                   bank[4 + t][:, :], ALU.mult, ALU.add).then_inc(s_ev, 1)

        def add_to_h(i, t, done):
            at_least(DV, *done)
            V.tensor_tensor(H[:, t, i * CH:(i + 1) * CH], H[:, t, i * CH:(i + 1) * CH], bank[4 + t][:, :],
                            ALU.add).then_inc(s_ev, 1)

        def merge(i, t, done):
            at_least(DV, *done)
            cs = slice(i * CH, (i + 1) * CH)
            tmp = S[:, 0:CH]
            DV.run(V.tensor_tensor, U[:, t, cs], bank[3 * t][:, :], G[:, t, cs], ALU.mult)
            for b in (1, 2):
                DV.run(V.tensor_tensor, tmp, bank[3 * t + b][:, :], G[:, t, b * D + i * CH:b * D + (i + 1) * CH],
                       ALU.mult)
                if b == 1:
                    DV.run(V.tensor_tensor, U[:, t, cs], U[:, t, cs], tmp, ALU.add)
            DV.wait(DV.last())
            V.tensor_tensor(U[:, t, cs], U[:, t, cs], tmp, ALU.add).then_inc(s_ev, 1)

        def all_idle():
            return [e.last() for e in (PE, AC, DV, PO)] + [products_read()]

        def snapshot(name, l, src):
            if stop is None or f"{name}{l}" not in stop:
                return
            AC.wait(*all_idle())
            AC.eng.dma_start(stop[f"{name}{l}"].rearrange("a (t p) n -> p (a t) n", p=P), src[:, :, :]).then_inc(s_snap, 16)
            c.snap += 16
            for e in (AC, DV, PE):
                e.wait((s_snap, c.snap))

        def store_and_end(src):
            SP.wait(*all_idle())
            o = out.rearrange("a (t p) n -> p (a t) n", p=P)
            Y.dma_start(o, src).then_inc(s_out, 16)
            Y.wait_ge(s_out, 16)

        def route(m):
            w = small_loads([(rw[:, :, :], A["moe_router"][m].rearrange("(k p) e -> p k e", p=P))])
            hi = DV.run(V.tensor_copy, rh[:, :, :], rw[:, :, :], after=[w])
            DV.run(V.tensor_tensor, rl[:, :, :], rw[:, :, :], rh[:, :, :].bitcast(F32), ALU.subtract)
            PE.wait(DV.last())
            for t in range(NT):
                for k in range(KT):
                    i = three(bank[7][:, t * 8:(t + 1) * 8], (xh[:, k, :], xl[:, k, :]), (rh[:, k, :], rl[:, k, :]), t,
                              k == 0, k == KT - 1)
            scored = PE.mark(i)
            for t in range(NT):
                L, top, idx, num, e, g, g2 = (lg[:, j, :] for j in range(7))
                DV.run(V.tensor_copy, L, bank[7][:, t * 8:(t + 1) * 8], after=[scored])
                DV.run(V.max, top, L)
                DV.run(V.max_index, idx.bitcast(U32), top, L)
                DV.run(V.tensor_copy, num, idx.bitcast(U32))
                d = DV.run(V.tensor_tensor, e[:, 0:1], top[:, 1:2], top[:, 0:1], ALU.subtract)
                x = AC.run(K.activation, e[:, 1:2], e[:, 0:1], ACT.Exp, after=[d])
                DV.run(V.tensor_scalar, e[:, 2:3], e[:, 1:2], 1.0, None, ALU.add, after=[x])
                DV.run(V.reciprocal, e[:, 3:4], e[:, 2:3])
                DV.run(V.tensor_tensor, e[:, 4:5], e[:, 1:2], e[:, 3:4], ALU.mult)
                DV.run(V.tensor_scalar, g, iota[:, :], num[:, 0:1], e[:, 3:4], ALU.is_equal, ALU.mult)
                DV.run(V.tensor_scalar, g2, iota[:, :], num[:, 1:2], e[:, 4:5], ALU.is_equal, ALU.mult)
                DV.run(V.tensor_tensor, g, g, g2, ALU.add)
                DV.run(V.tensor_copy, gt[:, t, :].rearrange("p (e c) -> p e c", c=NFF),
                       g.unsqueeze(2).to_broadcast([P, EXPERTS, NFF]))

        def angles():
            load = small_loads([(pos[:, :], A["positions_2"].rearrange("a (t p) -> p (a t)", p=P)),
                                (invf[:, :], C["inv_freq"])], after=[DV.last()])
            n = NT * ROT2 // 2
            x, k, y, z = (S[:, 3072 + j * n:3072 + (j + 1) * n] for j in range(4))
            pf = lam[:, 0:NT]
            two_pi = 2 * np.pi
            c1 = 6.28125
            c2 = float(np.round((two_pi - c1) * 2 ** 20) / 2 ** 20)
            c3 = float(two_pi - c1 - c2)
            magic = 1.5 * 2.0 ** 23
            DV.run(V.tensor_copy, pf, pos[:, :], after=[load])
            for t in range(NT):
                DV.run(V.tensor_scalar, x[:, t * 8:(t + 1) * 8], invf[:, :], pf[:, t:t + 1], None, ALU.mult)
            DV.run(V.tensor_scalar, k, x, 1.0 / two_pi, magic, ALU.mult, ALU.add)
            DV.run(V.tensor_scalar, k, k, -magic, None, ALU.add)
            for part in (c1, c2, c3):
                DV.run(V.scalar_tensor_tensor, x, k, -part, x, ALU.mult, ALU.add)
            DV.run(V.tensor_scalar, y, x, float(np.pi / 2), None, ALU.add)
            DV.run(V.tensor_scalar, z, y, float(np.pi), None, ALU.is_gt)
            DV.run(V.scalar_tensor_tensor, y, z, -two_pi, y, ALU.mult, ALU.add)
            lim = 3.1415925
            for v in (x, y):
                DV.run(V.tensor_scalar, v, v, lim, -lim, ALU.min, ALU.max)
            AC.run(K.activation, k, x, ACT.Sin, after=[DV.last()])
            sc_ = AC.run(K.activation, z, y, ACT.Sin)
            for t in range(NT):
                sn, cs = k[:, t * 8:(t + 1) * 8], z[:, t * 8:(t + 1) * 8]
                DV.run(V.tensor_copy, rope2[:, t, 0, 0:8], cs, after=[sc_])
                DV.run(V.tensor_copy, rope2[:, t, 0, 8:16], cs)
                DV.run(V.tensor_scalar, rope2[:, t, 1, 0:8], sn, -1.0, None, ALU.mult)
                DV.run(V.tensor_copy, rope2[:, t, 1, 8:16], sn)

        def half_ffn_loads(l, j):
            ffn_all_loads(A["ffn_w_gate_2"][l, j], A["ffn_w_up_2"][l, j])

        def half_ffn(l, j, last=False):
            idle = all_idle()
            for t in range(NT):
                rms_rows(H[:, t, :], U[:, t, :], D, 1e-6, t, after=idle)
            PE.wait(turn(U, gain=cols[:, (3 * l + 2 * j) * KT:(3 * l + 2 * j + 1) * KT], after=all_idle()))
            done = ffn(NFF, A["ffn_w_down_2"][l, j], after=all_idle(), last=last)
            for t in range(NT):
                for m in range(2):
                    cs = slice(m * CH, (m + 1) * CH)
                    DV.run(V.scalar_tensor_tensor, H[:, t, cs], bank[2 * t + m][:, :], 0.5, H[:, t, cs],
                           ALU.mult, ALU.add, after=[done])

        def select_keys():
            for e in (PE, DV, AC):
                e.wait(*all_idle())
            turned, scored, relu, used = {}, {}, {}, {}
            DV.run(V.tensor_copy, ISC[:, :, :], cmask[:, :, :])
            for i in range(IDX_HEADS + 1):
                if i < IDX_HEADS:
                    PE.wait(turned.get(i - 2))
                    for j in range(2):
                        for t in range(NT):
                            c0 = IQ + i * HD if j == 0 else IK
                            tr = T.transpose(bank[6 + i % 2][0:HD, (2 * j + t) * P:(2 * j + t + 1) * P],
                                             Z[:, t, c0:c0 + HD], ident[:, :])
                    m = PE.mark(tr)
                    turned[i] = AC.run(K.copy, QKT[0:HD, i % 2, 0, :], bank[6 + i % 2][0:HD, :],
                                       after=[m, scored.get(i - 2)])
                h = i - 1
                if h >= 0:
                    b = h % 2
                    PE.wait(turned[h], relu.get(h - 2))
                    for t in range(NT):
                        mm = T.matmul(halves(b)[:, t, :], QKT[0:HD, b, 0, t * P:(t + 1) * P],
                                      QKT[0:HD, b, 0, SEQ:2 * SEQ], start=True, stop=True)
                    scored[h] = PE.mark(mm)
                    relu[h] = AC.run(K.activation, PR[:, b, :, :], halves(b), ACT.Relu,
                                     after=[scored[h], used.get(h - 2)])
                    for t in range(NT):
                        used[h] = DV.run(V.scalar_tensor_tensor, ISC[:, t, :], PR[:, b, t, :],
                                         Z[:, t, IW + h:IW + h + 1], ISC[:, t, :], ALU.mult, ALU.add,
                                         after=[relu[h]])
            for r in range(TOPK // 8):
                for t in range(NT):
                    DV.run(V.max, ss[:, 8 * t:8 * t + 8], ISC[:, t, :])
                    DV.run(V.match_replace, ISC[:, t, :], ss[:, 8 * t:8 * t + 8], ISC[:, t, :], GONE)
            DV.run(V.tensor_scalar, SEL, ISC, GONE / 2, NEG, ALU.is_gt, ALU.mult)
            DV.run(V.tensor_tensor, SEL, SEL, cmask[:, :, :], ALU.add)


        DV.run(V.memset, mhalf[:, :], -0.5)
        DV.run(V.memset, zb[:, :], 0.0)
        consts = small_loads([(ident[:, :], C["ident"]), (cmask[:, :, :], C["causal"]),
                              (ropeb[:, :, :, :], C["rope_b"]), (ropec[:, :, :, :], C["rope_c"]),
                              (iota[:, :], C["iota"])])
        crow = G[:, 0, 0:P]
        crows = small_loads([
            (G[0:48, 0, 0:P], A["norm_g_2"].rearrange("l j (k p) -> (l j k) p", p=P)),
            (G[48:52, 0, 0:P], A["mla_q_norm"].rearrange("l (k p) -> (l k) p", p=P)),
            (G[52:54, 0, 0:P], A["mla_kv_norm"])])
        xin = small_loads([(U[:, :, :], A["x"].rearrange("a (t p) n -> p (a t) n", p=P))])
        ROW_LN, ROW_Q, ROW_KV = 0, 48, 52


        W1 = [CH, CH, CH, MAIN1 - 3 * CH]
        W2 = [CH] * 6 + [MAIN2 - 6 * CH]

        def stream(w, c0, widths, skip=0):
            for i, width in enumerate(widths):
                if i >= skip:
                    linear_loads(w, c0, width)
                c0 += width

        def stream_branches(wa, wb, wc):
            for m in range(2):
                cs = slice(m * CH, (m + 1) * CH)
                load_step([(rawg[:, k0:k1, :], w[(k0 - r) * P:(k1 - r) * P, cs].rearrange("(k p) n -> p k n", p=P))
                           for w, k0, k1, r in ((wa, 0, 2, 0), (wb, 2, 4, 2), (wb, 4, 6, 2), (wc, 6, 8, 6))])

        BRANCHES1 = [(0, 3, range(0, 2)), (1, 4, range(2, 6)), (2, 5, range(6, 8))]
        BRANCHES2 = [(0, 3, range(0, 2)), (1, 4, range(2, 4)), (2, 5, range(4, 8))]

        linear_loads(A["w_in"][0], 0, CH)
        cut(0, 0)
        PE.wait(crows, consts)
        turned = PE.mark(T.transpose(bank[0][:, 0:54], G[0:54, 0, 0:P], ident[0:54, 0:54]))
        DV.run(V.tensor_copy, cols[:, :], bank[0][:, 0:54], after=[turned])
        layer_norm(A["emb_ln_g"], A["emb_ln_b"], after=[xin])

        for l in range(DEPTH):
            idle = all_idle()
            rowp = small_loads([(pb[:, 0:HD], A["gqa_q_norm"][l].partition_broadcast(P)),
                                (pb[:, HD:2 * HD], A["gqa_k_norm"][l].partition_broadcast(P))], after=idle)
            loads = []
            for t in range(NT):
                for half in range(2):
                    r = 2 * t + half
                    w = 2 * NA_COLS - 1
                    src = A["na_rpb"]
                    off = (l * NA_HEADS * (2 * NA_ROWS - 1) + NA_ROWS - 1 - r) * w + NA_COLS - GRID_W
                    for h in range(NA_HEADS):
                        loads.append((nab[half * 64:(half + 1) * 64, t, h, :].rearrange("p (r c) -> p r c", c=GRID_W),
                                      bass.AP(src.tensor, off + h * (2 * NA_ROWS - 1) * w,
                                              [[1, GRID_W], [w, ROWS], [1, GRID_W]])))
            wmask = S[:, 4096:4096 + SEQ]
            flip = S[:, 4096 + SEQ:4096 + SEQ + P]
            loads += [(wmask, C["window"]), (flip, C["flip"])]
            biases = small_loads(loads, after=idle + ([(s_lod, c.ff)] if c.ff else []))
            WUQ = S[:, 2816:3584].rearrange("p (k n) -> p k n", k=2)
            WUKV = S[:, 3584:4096]
            latw = small_loads([(WUQ, A["mla_w_uq"][l].rearrange("(k p) n -> p k n", p=P)),
                                (WUKV, A["mla_w_ukv"][l])], after=idle)
            stream(A["w_in"][l], 0, W1, skip=1 if l == 0 else 0)
            stream(A["w_in"][l], MAIN1, [CH] * 6)
            stream_branches(A["w_proj_a"][l], A["w_proj_b"][l], A["w_proj_c"][l])
            stream(A["w_out"][l], 0, [CH] * 2)
            stream(A["mem_wkv"][l], 0, [CH] * 4)
            stream(A["mem_wq"][l], 0, [CH] * 2)
            stream(A["mem_wo"][l], 0, [CH] * 2)

            xt = turn(H, after=[DV.last()])
            PE.wait(xt)
            linear(4, to_tokens(Z, W1), widths=W1)
            AC.eng.preload_act_table(ACT.Sigmoid)
            linear(6, to_gates)
            zdone = products_read()
            DV.wait(zdone)

            PE.wait(biases)
            for t in range(NT):
                for j in range(2):
                    pair = nab[:, t, 2 * j:2 * j + 2, :]
                    m = PE.mark(T.matmul(halves(2 * t + j), flip, pair, start=True, stop=True))
                    DV.run(V.tensor_tensor, pair, halves(2 * t + j), wmask.unsqueeze(1).to_broadcast([P, 2, SEQ]),
                           ALU.add, after=[m])
            DV.wait(rowp)
            head_norm(BQ, GQA_HEADS + GQA_KV, [(0, GQA_HEADS, pb[:, 0:HD]), (GQA_HEADS, GQA_KV, pb[:, HD:2 * HD])])
            for t in range(NT):
                rotate(heads3(Z[:, t, :], BQ, GQA_HEADS + GQA_KV), GQA_HEADS + GQA_KV, HD // 2, ropeb[:, t, :, :])
            for t in range(NT):
                rms_rows(Z[:, t, CDQ:CDQ + QR], Z[:, t, CDQ:CDQ + QR], QR, 1e-6, t)
                rms_rows(Z[:, t, CDKV:CDKV + KVR], Z[:, t, CDKV:CDKV + KVR], KVR, 1e-6, t)
            PE.wait(DV.last())
            CQT = S[:, 2048:2560].rearrange("p (k n) -> p k n", k=2)
            CKT = S[:, 2560:2816]
            for t in range(NT):
                for k in range(2):
                    T.transpose(halves(6)[:, k, t * P:(t + 1) * P], Z[:, t, CDQ + k * P:CDQ + (k + 1) * P], ident[:, :])
                i = T.transpose(halves(7)[:, 0, t * P:(t + 1) * P], Z[:, t, CDKV:CDKV + P], ident[:, :])
            turned = PE.mark(i)
            for k in range(2):
                DV.run(V.tensor_scalar, CQT[:, k, :], halves(6)[:, k, :],
                       cols[:, ROW_Q + 2 * l + k:ROW_Q + 2 * l + k + 1], None, ALU.mult, after=[turned])
            DV.run(V.tensor_scalar, CKT, halves(7)[:, 0, :], cols[:, ROW_KV + l:ROW_KV + l + 1], None, ALU.mult)
            PE.wait(DV.last(), latw)
            QC, KVC, KF = MAIN1, MAIN1 + 384, MAIN1 + 384 + 512
            for t in range(NT):
                for k in range(2):
                    T.matmul(bank[t][:, 0:384], CQT[:, k, t * P:(t + 1) * P], WUQ[:, k, :], start=k == 0, stop=k == 1)
                i = T.matmul(bank[2 + t][:, :], CKT[:, t * P:(t + 1) * P], WUKV, start=True, stop=True)
            up = PE.mark(i)
            for t in range(NT):
                DV.run(V.tensor_copy, Z[:, t, QC:QC + 384], bank[t][:, 0:384], after=[up])
                DV.run(V.tensor_copy, Z[:, t, KVC:KVC + 512], bank[2 + t][:, :])
                rotate(heads3(Z[:, t, :], QC, MLA_HEADS, 96)[:, :, NOPE:], MLA_HEADS, ROPE_C // 2, ropec[:, t, :, :])
                rotate(heads3(Z[:, t, :], CKR, 1, ROPE_C), 1, ROPE_C // 2, ropec[:, t, :, :])
                kf = heads3(Z[:, t, :], KF, MLA_HEADS, 96)
                DV.run(V.tensor_copy, kf[:, :, 0:NOPE], heads3(Z[:, t, :], KVC, MLA_HEADS, 128)[:, :, 0:NOPE])
                DV.run(V.tensor_copy, kf[:, :, NOPE:],
                       heads3(Z[:, t, :], CKR, 1, ROPE_C).to_broadcast([P, MLA_HEADS, ROPE_C]))
            hs = [head(zc(AQ + h * HD), zc(AK + h * HD), zc(AV + h * HD), uc(h * HD), HD ** -0.5,
                       bias=nab[:, :, h, :]) for h in range(NA_HEADS)]
            hs += [head(zc(BQ + h * HD), zc(BK + h // 4 * HD), zc(BV + h // 4 * HD), uc(256 + h * HD), HD ** -0.5)
                   for h in range(GQA_HEADS)]
            hs += [head(zc(QC + h * 96, 96), zc(KF + h * 96, 96), zc(KVC + h * 128 + NOPE), uc(768 + h * VC),
                        (NOPE + ROPE_C) ** -0.5, dk=96) for h in range(MLA_HEADS)]
            attention(hs, after=all_idle())
            wgu = A["ffn_w_gu"] if l % 2 == 0 else A["moe_w_gu"]
            ffn_all_loads(*(wgu[l // 2][..., m * DFF:(m + 1) * DFF] for m in range(2)))
            snapshot("heads", l, U)

            PE.wait(turn(U, after=all_idle()))
            linear(2, merge, groups=BRANCHES1)
            PE.wait(turn(U, after=all_idle()))
            linear(2, add_residual)
            layer_norm(A["ln_g"][l, 0], A["ln_b"][l, 0], after=all_idle())
            snapshot("mix", l, H)

            mem = small_loads([(U[:, :, :], A["mem"].rearrange("a (t p) n -> p (a t) n", p=P))], after=all_idle())
            PE.wait(turn(U, after=[mem] + all_idle()))
            linear(4, to_tokens(Z))
            PE.wait(turn(H, after=all_idle()))
            linear(2, to_tokens(G))
            w = D // MEM_HEADS

            def mem_head(h):
                return head(lambda t, k: G[:, t, h * w + k * P:h * w + (k + 1) * P],
                            lambda t, k: Z[:, t, h * w + k * P:h * w + (k + 1) * P],
                            lambda t: Z[:, t, D + h * w:D + (h + 1) * w], uc(h * w, w), w ** -0.5, dk=P, dv=w, nk=2)
            attention([mem_head(h) for h in range(MEM_HEADS)], after=all_idle())
            PE.wait(turn(U, after=all_idle()))
            linear(2, add_residual)
            layer_norm(A["ln_g"][l, 1], A["ln_b"][l, 1], after=all_idle())
            snapshot("mem", l, H)

            idle = all_idle()
            PE.wait(turn(H, after=idle))
            if l % 2 == 0:
                done = ffn(NFF, A["ffn_w_down"][l // 2], after=all_idle())
            else:
                route(l // 2)
                done = ffn(EXPERTS * NFF, A["moe_w_down"][l // 2].rearrange("e f n -> (e f) n"), gate=lambda i, t: gt[:, t, bass.ds(i, 1)], after=all_idle())
            for t in range(NT):
                for m in range(2):
                    cs = slice(m * CH, (m + 1) * CH)
                    DV.run(V.scalar_tensor_tensor, U[:, t, cs], H[:, t, cs], ALPHA, bank[2 * t + m][:, :],
                           ALU.mult, ALU.add, after=[done])
            layer_norm(A["ln_g"][l, 2], A["ln_b"][l, 2], after=all_idle())
            snapshot("ffn", l, H)

        angles()
        for l in range(DEPTH):
            last = l == DEPTH - 1
            half_ffn_loads(l, 0)
            half_ffn(l, 0)
            snapshot("ffn2", l, H)
            idle = all_idle()
            rowp = small_loads([(pb[:, 0:6 * HD], A["qk_norm_g_2"][l].rearrange("a b -> (a b)").partition_broadcast(P)),
                                (pb[:, 384:512], A["diff_subln_g_2"][l].partition_broadcast(P)),
                                (pb[:, 512:768], A["lambda_params_2"][l].rearrange("a b -> (a b)").partition_broadcast(P))],
                               after=idle)
            stream(A["w_in_2"][l], 0, W2)
            stream(A["w_in_2"][l], MAIN2, [CH] * 6)
            stream(A["w_branch_2"][l], 0, [CH] * 2)
            stream(A["w_out_2"][l], 0, [CH] * 2)
            for t in range(NT):
                rms_rows(H[:, t, :], U[:, t, :], D, 1e-6, t, after=idle)
            PE.wait(turn(U, gain=cols[:, (3 * l + 1) * KT:(3 * l + 2) * KT], after=all_idle()))
            linear(7, to_tokens(Z, W2), widths=W2)
            AC.eng.preload_act_table(ACT.Sigmoid)
            linear(6, to_gates)
            DV.wait(products_read(), rowp)

            def gain(j):
                return pb[:, j * HD:(j + 1) * HD]
            head_norm(A2Q, 5, [(0, 4, gain(0)), (4, 1, gain(1))])
            head_norm(B2Q, 8, [(0, 4, gain(2)), (4, 4, gain(3))])
            head_norm(C2Q, 16, [(0, 8, gain(4)), (8, 8, gain(5))])
            for t in range(NT):
                for c0, nh in ((A2Q, 5), (IQ, 9), (B2Q, 8), (C2Q, 16)):
                    rotate(heads3(Z[:, t, :], c0, nh), nh, ROT2 // 2, rope2[:, t, :, :])
                DV.run(V.tensor_scalar, Z[:, t, IW:IW + IDX_HEADS], Z[:, t, IW:IW + IDX_HEADS],
                       (IDX_HEADS * HD) ** -0.5, None, ALU.mult)
            init = 0.8 - 0.6 * float(np.exp(-0.3 * l))
            for j in range(2):
                DV.run(V.tensor_tensor_reduce, S[:, 0:HD], pb[:, 512 + 2 * j * HD:512 + (2 * j + 1) * HD],
                       pb[:, 512 + (2 * j + 1) * HD:512 + (2 * j + 2) * HD], 1.0, 0.0, ALU.mult, ALU.add,
                       lam[:, j:j + 1])
            e = AC.run(K.activation, lam[:, 2:4], lam[:, 0:2], ACT.Exp, after=[DV.last()])
            DV.run(V.tensor_tensor, lam[:, 4:5], lam[:, 3:4], lam[:, 2:3], ALU.subtract, after=[e])
            DV.run(V.tensor_scalar, lam[:, 4:5], lam[:, 4:5], -init, None, ALU.add)
            select_keys()
            hs = [head(zc(A2Q + h * HD), zc(A2K), zc(A2V), uc(h * HD), HD ** -0.5, bias=SEL) for h in range(4)]
            hs += [head(zc(B2Q + h * HD), zc(B2K + h * HD), zc(B2V + h * HD), uc(256 + h * HD), HD ** -0.5,
                        bias=cmask) for h in range(4)]
            hs += [head(zc(C2Q + (2 * h + j) * HD), zc(C2K + (2 * h + j) * HD), zc(C2V + h * P, P),
                        uc(512 + h * P, P), HD ** -0.5, dv=P, bias=cmask, weight=lam[:, 4:5] if j else None)
                   for h in range(4) for j in range(2)]
            attention(hs, after=all_idle())
            half_ffn_loads(l, 1)
            for t in range(NT):
                x = U[:, t, 512:D].rearrange("p (h d) -> p h d", d=P)
                sq = S[:, 0:512]
                DV.run(V.tensor_tensor, sq, U[:, t, 512:D], U[:, t, 512:D], ALU.mult)
                DV.run(V.tensor_reduce, ss[:, 4 * t:4 * t + 4], sq.rearrange("p (h d) -> p h d", d=P), AX.X, ALU.add)
            e = DV.run(V.tensor_scalar, ss[:, 0:8], ss[:, 0:8], 1.0 / P, 1e-6, ALU.mult, ALU.add)
            r = rsqrt(rs[:, 0:8], ss[:, 0:8], after=[e])
            DV.run(V.tensor_scalar, pb[:, 384:512], pb[:, 384:512], 1.0 - init, None, ALU.mult)
            for t in range(NT):
                x = U[:, t, 512:D].rearrange("p (h d) -> p h d", d=P)
                DV.run(V.tensor_tensor, x, x, rs[:, 4 * t:4 * t + 4].unsqueeze(2).to_broadcast([P, 4, P]), ALU.mult,
                       after=[r])
                DV.run(V.tensor_tensor, x, x, pb[:, 384:512].unsqueeze(1).to_broadcast([P, 4, P]), ALU.mult)
            snapshot("heads2", l, U)
            PE.wait(turn(U, after=all_idle()))
            linear(2, merge, groups=BRANCHES2)
            PE.wait(turn(U, after=all_idle()))
            linear(2, add_to_h)
            snapshot("mix2", l, H)
            half_ffn(l, 1, last=last)
        store_and_end(H[:, :, :])


INPUTS = ["x", "mem", "emb_ln_g", "emb_ln_b", "w_in", "na_rpb", "gqa_q_norm", "gqa_k_norm", "mla_q_norm",
          "mla_kv_norm", "mla_w_uq", "mla_w_ukv", "w_proj_a", "w_proj_b", "w_proj_c", "w_out", "mem_wq", "mem_wkv",
          "mem_wo", "ln_g", "ln_b", "ffn_w_gu", "ffn_w_down", "moe_router", "moe_w_gu", "moe_w_down",
          "positions_2", "norm_g_2", "w_in_2", "qk_norm_g_2", "lambda_params_2", "diff_subln_g_2", "w_branch_2",
          "w_out_2", "ffn_w_gate_2", "ffn_w_up_2", "ffn_w_down_2"]


def shape_constants():
    f = np.float32
    t = np.arange(SEQ)
    row, col = (t // GRID_W).astype(f), (t % GRID_W).astype(f)

    def axial(dim):
        n = dim // 4
        inv = (f(10000.0) ** (-np.arange(n, dtype=f) / f(n))).astype(f)
        ang = np.concatenate([row[:, None] * inv, col[:, None] * inv], axis=1)
        c, s = np.cos(ang).astype(f), np.sin(ang).astype(f)
        tab = np.stack([np.concatenate([c, c], 1), np.concatenate([-s, s], 1)], axis=1)
        return np.ascontiguousarray(tab.reshape(NT, P, 2, dim).transpose(1, 0, 2, 3))
    causal = np.where(t[None, :] <= t[:, None], 0.0, NEG).astype(f).reshape(NT, P, SEQ).transpose(1, 0, 2)
    c = np.arange(GRID_W)
    first = np.clip(c - NA_COLS // 2, 0, GRID_W - NA_COLS)[:, None]
    window = np.where((c[None, :] >= first) & (c[None, :] < first + NA_COLS), 0.0, NEG).astype(f)
    inv2 = (500000.0 ** (-np.arange(0, ROT2, 2) / ROT2)).astype(f)
    return {"ident": np.eye(P, dtype=f), "causal": np.ascontiguousarray(causal), "rope_b": axial(HD),
            "rope_c": axial(ROPE_C), "flip": np.kron(np.eye(P // GRID_W, dtype=f), np.eye(GRID_W, dtype=f)[::-1]),
            "window": np.tile(window, (P // GRID_W, ROWS)),
            "inv_freq": np.tile(inv2, (P, 1)), "iota": np.tile(np.arange(EXPERTS, dtype=f), (P, 1))}


def kernel(**inputs):
    import concourse.bacc as bacc
    from concourse.bass_utils import run_bass_kernel_spmd
    nc = bacc.Bacc("TRN2", target_bir_lowering=False, num_devices=1, dynamic_dma_scratch_size=4096)
    arrays = {}

    def given(name, a):
        a = np.ascontiguousarray(a)
        arrays[name] = a
        return nc.dram_tensor(name, a.shape, mybir.dt.from_np(a.dtype), kind="ExternalInput").ap()
    A = {name: given(f"in_{name}", inputs[name]) for name in INPUTS}
    C = {name: given(f"const_{name}", a) for name, a in shape_constants().items()}
    out = nc.dram_tensor("out", (1, SEQ, D), F32, kind="ExternalOutput").ap()
    program(nc, A, C, out)
    return run_bass_kernel_spmd(nc, [arrays], core_ids=[0]).results[0]["out"]
```

```python
from contextlib import ExitStack
import numpy as np
import concourse.bass as bass
from concourse import mybir

F32, F32R, BF16 = mybir.dt.float32, mybir.dt.float32r, mybir.dt.bfloat16
I32, U32 = mybir.dt.int32, mybir.dt.uint32
ALU, ACT, AX = mybir.AluOpType, mybir.ActivationFunctionType, mybir.AxisListType

P = 128
SEQ, D = 256, 1024
NT = SEQ // P
KT = D // P
CH = 512
DEPTH = 2
ALPHA = (2 * DEPTH) ** 0.25
NEG = -1.0e30
GONE = -3.0e38

GRID_W, NA_ROWS, NA_COLS = 64, 8, 16
ROWS = SEQ // GRID_W
NA_HEADS, GQA_HEADS, GQA_KV, MLA_HEADS, MEM_HEADS, HD = 4, 8, 2, 4, 4, 64
NOPE, ROPE_C, VC = 64, 32, 64
QR, KVR = 256, 128
DFF = 2816
HCH = CH // 2
NFF = DFF // HCH
EXPERTS = 8
GATES = 3 * D

AQ, AK, AV = 0, 256, 512
BQ, BK, BV = 768, 1280, 1408
CDQ, CDKV, CKR, MAIN1 = 1536, 1792, 1920, 1952
A2Q, A2K, A2V, IQ, IK, IW = 0, 256, 320, 384, 896, 960
B2Q, B2K, B2V, C2Q, C2K, C2V, MAIN2 = 968, 1224, 1480, 1736, 2248, 2760, 3272
IDX_HEADS, TOPK = 8, 64
ROT2 = 16


class Chain:

    def __init__(self, eng, sem, seen):
        self.eng, self.sem, self.n, self.seen = eng, sem, 0, seen

    def wait(self, *tokens):
        for t in tokens:
            if t is None:
                continue
            sem, value = t
            if isinstance(value, int) and value <= self.seen.get(id(sem), 0):
                continue
            if isinstance(value, int):
                self.seen[id(sem)] = value
            self.eng.wait_ge(sem, value)

    def last(self):
        return (self.sem, self.n) if self.n else None

    def run(self, fn, *args, after=(), **kw):
        self.wait(*after, self.last())
        fn(*args, **kw).then_inc(self.sem, 1)
        self.n += 1
        return self.last()

    def mark(self, ins):
        ins.then_inc(self.sem, 1)
        self.n += 1
        return self.last()


def program(nc, A, C, out, stop=None):
    ctx = ExitStack()
    with ctx:
        def sb(name, shape, dt=F32):
            return ctx.enter_context(nc.sbuf_tensor(name, shape, dt))

        def sem(name):
            return ctx.enter_context(nc.semaphore(name))

        rawg = sb("raw_gu", [P, KT, CH])
        rawd = sb("raw_down", [P, 2, D])
        wh = sb("w_hi", [P, 2, KT, CH], F32R)
        wl = sb("w_lo", [P, 2, KT, CH], F32R)
        dh = sb("down_hi", [P, 2, D], F32R)
        dl = sb("down_lo", [P, 2, D], F32R)
        xh = sb("xT_hi", [P, KT, SEQ], F32R)
        xl = sb("xT_lo", [P, KT, SEQ], F32R)
        hh = sb("hiddenT_hi", [P, 2, SEQ], F32R)
        hl = sb("hiddenT_lo", [P, 2, SEQ], F32R)
        H = sb("residual", [P, NT, D])
        U = sb("token_scratch", [P, NT, D])
        z_offset = nc.sbuf_base
        Z = sb("projected", [P, NT, MAIN2])
        g_offset = nc.sbuf_base
        G = sb("gates", [P, NT, GATES])
        S = sb("scratch", [P, 5120])
        pb = sb("row_params", [P, 768])
        ident = sb("ident", [P, P])
        cmask = sb("causal", [P, NT, SEQ])
        ropeb = sb("rope_b", [P, NT, 2, HD])
        ropec = sb("rope_c", [P, NT, 2, ROPE_C])
        rope2 = sb("rope_2", [P, NT, 2, ROT2])
        cols = sb("col_params", [P, 54])
        mhalf = sb("minus_half", [P, 64])
        st = sb("stats", [P, NT, 2, 6])
        mv = sb("mean_var", [P, NT, 2])
        ss = sb("sums", [P, 64])
        rs = sb("rstd", [P, 64])
        zb = sb("zeros", [P, CH], BF16)
        lam = sb("lambda", [P, 8])
        rh, rl = sb("router_hi", [P, KT, EXPERTS], F32R), sb("router_lo", [P, KT, EXPERTS], F32R)
        flag = sb("again", [P, 1], I32)
        rw = pb[:, 448:448 + KT * EXPERTS].rearrange("p (k e) -> p k e", e=EXPERTS)
        lg = sb("router_stats", [P, 8, 8])
        iota = sb("expert_numbers", [P, EXPERTS])
        pos = sb("positions", [P, NT], I32)
        invf = sb("inverse_frequencies", [P, ROT2 // 2])

        QKT = S[:, 0:2048].rearrange("p (b k n) -> p b k n", b=2, k=2)
        SM = S[:, 2048:3072].rearrange("p (b t n) -> p b t n", b=2, t=2)
        PR = S[:, 3072:4096].rearrange("p (b t n) -> p b t n", b=2, t=2)
        PT = S[:, 4096:5120].rearrange("p (b k n) -> p b k n", b=2, k=2)
        SG = S[:, 2048:2560].rearrange("p (t n) -> p t n", t=2)
        HB = S[:, 2560:3072].rearrange("p (t n) -> p t n", t=2)
        GR, BR = S[:, 0:D], S[:, D:2 * D]
        nab = rawd[:, :, :].rearrange("p t (h n) -> p t h n", n=SEQ)
        ISC = rawd[:, 0, 0:NT * SEQ].rearrange("p (t n) -> p t n", t=NT)
        SEL = rawd[:, 1, 0:NT * SEQ].rearrange("p (t n) -> p t n", t=NT)

        bank = [ctx.enter_context(nc.psum_tensor(f"bank{i}", [P, CH], F32)) for i in range(8)]

        def halves(b):
            return bank[b][:, :].rearrange("p (a n) -> p a n", a=2)

        s_ld, s_ldd = [sem("w_loaded0"), sem("w_loaded1")], sem("down_loaded")
        s_hi, s_lo, s_hid, s_lod = sem("w_hi_cut"), sem("w_lo_cut"), sem("down_hi_cut"), sem("down_lo_cut")
        s_mm, s_ev = sem("product_done"), sem("product_read")
        s_si, s_tr, s_hth, s_htl, s_dn = sem("silu"), sem("hidden_turned"), sem("hiddenT_hi_cut"), sem(
            "hiddenT_lo_cut"), sem("down_done")
        s_out = sem("stored")
        s_snap = sem("snap")
        s_again = sem("ranks_lowered")
        small = [sem(f"small{i}") for i in range(8)]
        SP = Chain(nc.sync, sem("sp"), {})
        PE = Chain(nc.tensor, sem("pe"), {})
        DV = Chain(nc.vector, sem("dve"), {})
        AC = Chain(nc.scalar, sem("act"), {})
        PO = Chain(nc.gpsimd, sem("pool"), {})
        V, T, K, Q, Y = nc.vector, nc.tensor, nc.scalar, nc.gpsimd, nc.sync
        engines = (SP, PE, DV, AC, PO)

        class Count:
            pass
        c = Count()
        c.step = 0
        c.loads = 0
        c.ff = 0
        c.ffl = 0
        c.small = 0
        c.snap = 0
        c.smallv = [0] * 8

        def at_least(chain, s, value):
            if isinstance(value, int):
                if value > 0:
                    chain.wait((s, value))
            else:
                chain.eng.wait_ge(s, value)

        def small_loads(pairs, after=()):
            k = c.small % 8
            PO.wait(*after, (small[k], c.smallv[k]) if c.smallv[k] else None)
            for dst, src in pairs:
                Q.dma_start(dst, src, allow_slow_non_contiguous=True).then_inc(small[k], 16)
            c.smallv[k] += 16 * len(pairs)
            c.small += 1
            return (small[k], c.smallv[k])

        def load_step(srcs, n=None):
            s = c.loads if n is None else n
            for u in range(2):
                at_least(SP, s_lo, 2 * s - 1 + u)
                for dst, src in srcs[2 * u:2 * u + 2]:
                    Y.dma_start(dst, src).then_inc(s_ld[u], 16)
            if n is None:
                c.loads += 1

        def linear_loads(w, c0, width):
            v = w.rearrange("(k p) n -> p k n", p=P)
            load_step([(rawg[:, k:k + 2, 0:width], v[:, k:k + 2, c0:c0 + width]) for k in range(0, KT, 2)])

        def cut(s, par, width=CH):
            for u in range(2):
                src = rawg[:, 4 * u:4 * u + 4, 0:width]
                hi = wh[:, par, 4 * u:4 * u + 4, 0:width]
                at_least(AC, s_ld[u], 32 * (s + 1))
                at_least(AC, s_mm, 2 * (s - 1))
                K.copy(hi, src).then_inc(s_hi, 1)
                at_least(DV, s_hi, 2 * s + u + 1)
                V.tensor_tensor(wl[:, par, 4 * u:4 * u + 4, 0:width], src, hi.bitcast(F32),
                                ALU.subtract).then_inc(s_lo, 1)

        def three(acc, xk, wk, t, start, stop):
            (ah, al), (bh, bl) = xk, wk
            tok = slice(t * P, (t + 1) * P)
            T.matmul(acc, ah[:, tok], bh, start=start, stop=False)
            T.matmul(acc, ah[:, tok], bl, start=False, stop=False)
            return T.matmul(acc, al[:, tok], bh, start=False, stop=stop)

        def multiply(s, par, width=CH, groups=None):
            groups = groups or [(4, 5, range(KT))]
            for t in range(NT):
                at_least(PE, s_ev, 2 * s - 1 + t)
                for b in groups:
                    for k in b[2]:
                        if t == 0:
                            at_least(PE, s_lo, 2 * s + 1 + k // 4)
                        mm = three(bank[b[t]][:, 0:width], (xh[:, k, :], xl[:, k, :]),
                                   (wh[:, par, k, 0:width], wl[:, par, k, 0:width]), t,
                                   k == b[2][0], k == b[2][-1])
                mm.then_inc(s_mm, 1)

        def linear(n, evac, widths=None, next_width=CH, groups=None, last=False):
            base = c.step
            PE.wait(products_read())

            def one(i, j):
                s = base + i
                par = (base + j) % 2
                w_next = CH
                if isinstance(i, int):
                    w_next = widths[i + 1] if widths and i + 1 < n else (next_width if i + 1 == n else CH)
                if not (last and isinstance(i, int) and i == n - 1):
                    cut(s + 1, 1 - par, w_next)
                multiply(s, par, widths[i] if widths and isinstance(i, int) else CH, groups)
                for t in range(NT):
                    evac(i, t, (s_mm, 2 * s + t + 1))

            pairs = (n - 2) // 2 if n >= 6 else 0
            if pairs:
                with nc.Fori(0, pairs) as r:
                    for j in range(2):
                        one(r * 2 + j, j)
                forget()
            for i in range(2 * pairs, n):
                one(i, i)
            c.step += n

        def products_read():
            return (s_ev, 2 * c.step)

        def forget():
            for e in engines:
                e.seen.clear()

        def turn(src, gain=None, after=()):
            done = {}
            PE.wait(*after)
            for r in range(KT // 2):
                b = 6 + r % 2
                for kk in range(2):
                    k = 2 * r + kk
                    for t in range(NT):
                        PE.wait(done.get(r - 2))
                        i = T.transpose(bank[b][:, kk * SEQ + t * P:kk * SEQ + (t + 1) * P],
                                        src[:, t, k * P:(k + 1) * P], ident[:, :])
                turned = PE.mark(i)
                if gain is None:
                    hi = AC.run(K.copy, xh[:, 2 * r:2 * r + 2, :], halves(b), after=[turned])
                    done[r] = DV.run(V.tensor_tensor, xl[:, 2 * r:2 * r + 2, :], halves(b),
                                     xh[:, 2 * r:2 * r + 2, :].bitcast(F32), ALU.subtract, after=[hi])
                else:
                    for k in (2 * r, 2 * r + 1):
                        hi = AC.run(K.activation, xh[:, k, :], halves(b)[:, k - 2 * r, :], ACT.Copy,
                                    scale=gain[:, k:k + 1], after=[turned])
                    for k in (2 * r, 2 * r + 1):
                        done[r] = DV.run(V.scalar_tensor_tensor, xl[:, k, :], halves(b)[:, k - 2 * r, :],
                                         gain[:, k:k + 1], xh[:, k, :].bitcast(F32), ALU.mult,
                                         ALU.subtract, after=[hi])
            return done[KT // 2 - 1]

        def ffn_loads(s, wa, wg, cc):
            load_step([(rawg[:, 4 * u:4 * u + 4, m * HCH:(m + 1) * HCH],
                        w.rearrange("(k p) n -> p k n", p=P)[:, 4 * u:4 * u + 4, bass.ds(cc * HCH, HCH)])
                       for u in range(2) for m, w in enumerate((wa, wg))], n=s)

        def ffn_all_loads(wa, wg):
            with nc.sync.Fori(0, NFF) as i:
                ffn_loads(i + c.loads, wa, wg, i)
            c.loads += NFF
            SP.seen.clear()

        def ffn(n, wd, gate=None, after=(), last=False):
            s0, g0 = c.step, c.ff

            def load_down(i):
                at_least(AC, s_lod, g0 + i)
                K.dma_start(rawd[:, :, :], wd[bass.ds(i * HCH, HCH), :].rearrange("(k p) n -> p k n", p=P)
                            ).then_inc(s_ldd, 16)

            PE.wait(*after, products_read())
            DV.wait(*after)
            AC.wait(*after)
            load_down(0)
            for b in range(4):
                T.matmul(bank[b][:, :], zb[:, 0:P], zb[:, :], start=True, stop=False)

            def down(g, stop=False):
                at_least(PE, s_lod, g + 1)
                at_least(PE, s_htl, g + 1)
                for t in range(NT):
                    tok = slice(t * P, (t + 1) * P)
                    for k in range(2):
                        for xx, ww in ((hh, dh), (hh, dl), (hl, dh)):
                            for m in range(2):
                                mm = T.matmul(bank[2 * t + m][:, :], xx[:, k, tok], ww[:, k, m * CH:(m + 1) * CH],
                                              start=False, stop=stop and k == 1 and xx is hl)
                mm.then_inc(s_dn, 1)

            def slot(i, j, first=False, cut_next=True, more=True):
                s, g, par = s0 + i, g0 + i, (s0 + j) % 2
                if cut_next:
                    cut(s + 1, 1 - par)
                multiply(s, par)
                if not first:
                    down(g - 1)
                for t in range(NT):
                    at_least(AC, s_mm, 2 * s + t + 1)
                    at_least(AC, s_ev, 2 * s - 1 + t)
                    K.activation(SG[:, t, :], bank[4 + t][:, 0:HCH], ACT.Silu).then_inc(s_si, 1)
                    at_least(DV, s_si, 2 * g + t + 1)
                    at_least(DV, s_tr, g)
                    V.scalar_tensor_tensor(HB[:, t, :], SG[:, t, :], gate(i, t) if gate else 1.0,
                                           bank[4 + t][:, HCH:CH], ALU.mult, ALU.mult).then_inc(s_ev, 1)
                for t in range(NT):
                    at_least(PE, s_ev, 2 * s + t + 1)
                    at_least(PE, s_htl, g)
                    for k in range(2):
                        tr = T.transpose(bank[6][:, k * SEQ + t * P:k * SEQ + (t + 1) * P],
                                         HB[:, t, k * P:(k + 1) * P], ident[:, :])
                tr.then_inc(s_tr, 1)
                at_least(AC, s_ldd, 16 * (g + 1))
                at_least(AC, s_dn, g)
                K.copy(dh[:, :, :], rawd[:, :, :]).then_inc(s_hid, 1)
                at_least(DV, s_hid, g + 1)
                V.tensor_tensor(dl[:, :, :], rawd[:, :, :], dh[:, :, :].bitcast(F32), ALU.subtract).then_inc(s_lod, 1)
                at_least(AC, s_tr, g + 1)
                K.copy(hh[:, :, :], halves(6)).then_inc(s_hth, 1)
                at_least(DV, s_hth, g + 1)
                V.tensor_tensor(hl[:, :, :], halves(6), hh[:, :, :].bitcast(F32), ALU.subtract).then_inc(s_htl, 1)
                if more:
                    load_down(i + 1)

            AC.eng.preload_act_table(ACT.Silu)
            slot(0, 0, first=True)
            pairs = (n - 2) // 2
            with nc.Fori(0, pairs) as r:
                for j in range(2):
                    slot(r * 2 + (1 + j), 1 + j)
            forget()
            for i in range(1 + 2 * pairs, n):
                slot(i, i, cut_next=not (last and i == n - 1), more=i < n - 1)
            down(g0 + n - 1, stop=True)
            c.step += n
            c.ff += n
            return (s_dn, c.ff)

        def rsqrt(dst, src, after=()):
            return PO.run(Q.tensor_tensor, dst, src, mhalf[:, 0:src.shape[1]], ALU.pow, after=after)

        def layer_norm(g, b, after=()):
            rows = small_loads([(GR, g.partition_broadcast(P)), (BR, b.partition_broadcast(P))], after=after)
            DV.wait(*after)
            for t in range(NT):
                for m in range(2):
                    DV.run(V.bn_stats, st[:, t, m, :], U[:, t, m * CH:(m + 1) * CH])
                DV.run(V.bn_aggr, mv[:, t, :], st[:, t, :, :].rearrange("p a b -> p (a b)"))
                e = DV.run(V.tensor_scalar, ss[:, t:t + 1], mv[:, t, 1:2], 1e-5, None, ALU.add)
                r = rsqrt(rs[:, t:t + 1], ss[:, t:t + 1], after=[e])
                DV.run(V.tensor_scalar, H[:, t, :], U[:, t, :], mv[:, t, 0:1], rs[:, t:t + 1],
                       ALU.subtract, ALU.mult, after=[r])
                DV.run(V.tensor_tensor, H[:, t, :], H[:, t, :], GR, ALU.mult, after=[rows])
                DV.run(V.tensor_tensor, H[:, t, :], H[:, t, :], BR, ALU.add)
            return DV.last()

        def rms_rows(x, y, width, eps, col, after=()):
            DV.run(V.tensor_tensor_reduce, S[:, 0:width], x, x, 1.0, 0.0, ALU.mult, ALU.add,
                   ss[:, col:col + 1], after=after)
            e = DV.run(V.tensor_scalar, ss[:, col:col + 1], ss[:, col:col + 1], 1.0 / width, eps, ALU.mult, ALU.add)
            r = rsqrt(rs[:, col:col + 1], ss[:, col:col + 1], after=[e])
            return DV.run(V.tensor_scalar, y, x, rs[:, col:col + 1], None, ALU.mult, after=[r])

        def head_norm(c0, heads, gains):
            n = NT * heads
            for t in range(NT):
                x = Z[:, t, c0:c0 + heads * HD]
                sq = S[:, 0:heads * HD]
                DV.run(V.tensor_tensor, sq, x, x, ALU.mult)
                DV.run(V.tensor_reduce, ss[:, t * heads:(t + 1) * heads], sq.rearrange("p (h d) -> p h d", d=HD),
                       AX.X, ALU.add)
            e = DV.run(V.tensor_scalar, ss[:, 0:n], ss[:, 0:n], 1.0 / HD, 1e-6, ALU.mult, ALU.add)
            r = rsqrt(rs[:, 0:n], ss[:, 0:n], after=[e])
            for t in range(NT):
                x = Z[:, t, c0:c0 + heads * HD].rearrange("p (h d) -> p h d", d=HD)
                f = rs[:, t * heads:(t + 1) * heads].unsqueeze(2).to_broadcast([P, heads, HD])
                DV.run(V.tensor_tensor, x, x, f, ALU.mult, after=[r])
                for h0, nh, row in gains:
                    y = x[:, h0:h0 + nh, :]
                    DV.run(V.tensor_tensor, y, y, row.unsqueeze(1).to_broadcast([P, nh, HD]), ALU.mult)

        def rotate(x, heads, half, table):
            a = S[:, 0:heads * 2 * half].rearrange("p (h d) -> p h d", h=heads)
            b = S[:, 1024:1024 + heads * 2 * half].rearrange("p (h d) -> p h d", h=heads)
            cc = table[:, 0, :].unsqueeze(1).to_broadcast([P, heads, 2 * half])
            s1 = table[:, 1, 0:half].unsqueeze(1).to_broadcast([P, heads, half])
            s2 = table[:, 1, half:2 * half].unsqueeze(1).to_broadcast([P, heads, half])
            DV.run(V.tensor_tensor, a, x[:, :, 0:2 * half], cc, ALU.mult)
            DV.run(V.tensor_tensor, b[:, :, 0:half], x[:, :, half:2 * half], s1, ALU.mult)
            DV.run(V.tensor_tensor, b[:, :, half:2 * half], x[:, :, 0:half], s2, ALU.mult)
            return DV.run(V.tensor_tensor, x[:, :, 0:2 * half], a, b, ALU.add)

        def heads3(x, c0, heads, d=HD):
            return x[:, c0:c0 + heads * d].rearrange("p (h d) -> p h d", d=d)

        def attention(heads, after):
            for e in (PE, DV, AC):
                e.wait(*after)
            n = len(heads)
            qkc, sc, ex, rc, ptc, ov, of = {}, {}, {}, {}, {}, {}, {}

            def turn_qk(h):
                d = heads[h]
                for k in range(d["nk"]):
                    b = 6 + (h + k) % 2
                    PE.wait(qkc.get(h - 1 if d["nk"] == 2 else h - 2))
                    if d["nk"] == 2 and k == 0:
                        PE.wait(qkc.get(h - 1))
                    dk = d["dk"]
                    for j in range(2):
                        for t in range(NT):
                            i = T.transpose(bank[b][0:dk, (2 * j + t) * P:(2 * j + t + 1) * P],
                                            (d["q"], d["k"])[j](t, k), ident[:, :])
                    turned = PE.mark(i)
                    qkc[h] = AC.run(K.copy, QKT[0:dk, h % 2, k, :], bank[b][0:dk, :],
                                    after=[turned, sc.get(h - 2)])

            def score(h):
                d, b = heads[h], h % 2
                dk = d["dk"]
                PE.wait(qkc[h], ex.get(h - 2), rc.get(("m", h - 2)))
                for t in range(NT):
                    for k in range(d["nk"]):
                        i = T.matmul(halves(b)[:, t, :], QKT[0:dk, b, k, t * P:(t + 1) * P],
                                     QKT[0:dk, b, k, SEQ:2 * SEQ], start=k == 0, stop=k == d["nk"] - 1)
                sc[h] = PE.mark(i)
                x, f = halves(b), d["scale"]
                if d["bias"] is not None:
                    for t in range(NT):
                        DV.run(V.scalar_tensor_tensor, SM[:, b, t, :], halves(b)[:, t, :], f, d["bias"][:, t, :],
                               ALU.mult, ALU.add, after=[sc[h], ex.get(h - 2)])
                    x, f = SM[:, b, :, :], 1.0
                mx = ss[:, 4 * b:4 * b + 2]
                DV.run(V.tensor_reduce, mx, x, AX.X, ALU.max, after=[sc[h]])
                rc[("m", h)] = DV.run(V.tensor_scalar, rs[:, 4 * b:4 * b + 2], mx, -f, None, ALU.mult,
                                      after=[ex.get(h - 2)])
                for t in range(NT):
                    ex[h] = AC.run(K.activation, PR[:, b, t, :], x[:, t, :], ACT.Exp,
                                   bias=rs[:, 4 * b + t:4 * b + t + 1], scale=f,
                                   accum_out=ss[:, 8 + 4 * b + t:9 + 4 * b + t],
                                   after=[rc[("m", h)], ptc.get(("pe", h - 2)), rc.get(h - 2)])
                rc[h] = DV.run(V.reciprocal, rs[:, 8 + 4 * b:10 + 4 * b], ss[:, 8 + 4 * b:10 + 4 * b],
                               after=[ex[h]])

            def turn_p(h):
                b = h % 2
                PE.wait(ex[h], ptc.get(h - 2))
                for k in range(NT):
                    for t in range(NT):
                        i = T.transpose(halves(2 + b)[:, k, t * P:(t + 1) * P], PR[:, b, t, k * P:(k + 1) * P],
                                        ident[:, :])
                ptc[("pe", h)] = PE.mark(i)
                ptc[h] = DV.run(V.tensor_copy, PT[:, b, :, :], halves(2 + b), after=[ptc[("pe", h)], ov.get(h - 2)])

            def value(h):
                d, b = heads[h], h % 2
                dv = d["dv"]
                PE.wait(ptc[h], of.get(h - 2))
                for t in range(NT):
                    for k in range(NT):
                        i = T.matmul(halves(4 + b)[:, t, 0:dv], PT[:, b, k, t * P:(t + 1) * P], d["v"](k),
                                     start=k == 0, stop=k == 1)
                ov[h] = PE.mark(i)
                for t in range(NT):
                    r = rs[:, 8 + 4 * b + t:9 + 4 * b + t]
                    if d["weight"] is None:
                        of[h] = DV.run(V.tensor_scalar, d["out"](t), halves(4 + b)[:, t, 0:dv], r, None, ALU.mult,
                                       after=[ov[h]])
                    else:
                        DV.run(V.tensor_tensor, r, r, d["weight"], ALU.mult)
                        of[h] = DV.run(V.scalar_tensor_tensor, d["out"](t), halves(4 + b)[:, t, 0:dv], r,
                                       d["out"](t), ALU.mult, ALU.add, after=[ov[h]])

            for i in range(n + 3):
                if 0 <= i - 3 < n:
                    value(i - 3)
                if 0 <= i - 2 < n:
                    turn_p(i - 2)
                if 0 <= i - 1 < n:
                    score(i - 1)
                if i < n:
                    turn_qk(i)
            return DV.last()

        def head(q, k, v, out_, scale, dk=HD, dv=HD, nk=1, bias=None, weight=None):
            return dict(q=q, k=k, v=v, out=out_, scale=scale, dk=dk, dv=dv, nk=nk, bias=bias, weight=weight)

        def zc(c0, w=HD):
            return lambda t, k=0: Z[:, t, c0 + k * w:c0 + (k + 1) * w]

        def uc(c0, w=HD):
            return lambda t: U[:, t, c0:c0 + w]

        def to_tokens(dst, widths=None):
            def evac(i, t, done):
                w = widths[i] if widths and isinstance(i, int) else CH
                at_least(DV, *done)
                V.tensor_copy(dst[:, t, bass.ds(i * CH, w)], bank[4 + t][:, 0:w]).then_inc(s_ev, 1)
            return evac

        def to_gates(i, t, done):
            at_least(AC, *done)
            K.activation(G[:, t, bass.ds(i * CH, CH)], bank[4 + t][:, :], ACT.Sigmoid).then_inc(s_ev, 1)

        def add_residual(i, t, done):
            at_least(DV, *done)
            V.scalar_tensor_tensor(U[:, t, i * CH:(i + 1) * CH], H[:, t, i * CH:(i + 1) * CH], ALPHA,
                                   bank[4 + t][:, :], ALU.mult, ALU.add).then_inc(s_ev, 1)

        def add_to_h(i, t, done):
            at_least(DV, *done)
            V.tensor_tensor(H[:, t, i * CH:(i + 1) * CH], H[:, t, i * CH:(i + 1) * CH], bank[4 + t][:, :],
                            ALU.add).then_inc(s_ev, 1)

        def merge(i, t, done):
            at_least(DV, *done)
            cs = slice(i * CH, (i + 1) * CH)
            tmp = S[:, 0:CH]
            DV.run(V.tensor_tensor, U[:, t, cs], bank[3 * t][:, :], G[:, t, cs], ALU.mult)
            for b in (1, 2):
                DV.run(V.tensor_tensor, tmp, bank[3 * t + b][:, :], G[:, t, b * D + i * CH:b * D + (i + 1) * CH],
                       ALU.mult)
                if b == 1:
                    DV.run(V.tensor_tensor, U[:, t, cs], U[:, t, cs], tmp, ALU.add)
            DV.wait(DV.last())
            V.tensor_tensor(U[:, t, cs], U[:, t, cs], tmp, ALU.add).then_inc(s_ev, 1)

        def all_idle():
            return [e.last() for e in (PE, AC, DV, PO)] + [products_read()]

        def snapshot(name, l, src):
            if stop is None or f"{name}{l}" not in stop:
                return
            AC.wait(*all_idle())
            AC.eng.dma_start(stop[f"{name}{l}"].rearrange("a (t p) n -> p (a t) n", p=P), src[:, :, :]).then_inc(s_snap, 16)
            c.snap += 16
            for e in (AC, DV, PE):
                e.wait((s_snap, c.snap))

        def store_and_end(src):
            SP.wait(*all_idle())
            o = out.rearrange("a (t p) n -> p (a t) n", p=P)
            Y.dma_start(o, src).then_inc(s_out, 16)
            Y.wait_ge(s_out, 16)

        at_z, at_g = z_offset, g_offset

        def over(name, shape, offset):
            return nc.alloc_sbuf_tensor_at(name, shape, F32R, offset=offset)
        HH = over("tokens_hi", [P, NT, D], at_z)
        HL = over("tokens_lo", [P, NT, D], at_z + 4 * NT * D)
        SEL_R = over("gather", [P, 2, NT, P], at_z + 8 * NT * D)
        SEL_T = over("scatter", [P, 2, SEQ], at_z + 8 * NT * D + 2048)
        YH = over("expert_out_hi", [P, D], at_g)
        YL = over("expert_out_lo", [P, D], at_g + 4 * D)
        Gf = G[:, :, :].rearrange("p t n -> p (t n)")
        rawg2 = Gf[:, 2 * D:2 * D + KT * CH].rearrange("p (k n) -> p k n", n=CH)
        rawd2 = S[:, 3072:5120].rearrange("p (k n) -> p k n", n=D)
        RAWG, RAWD = (rawg, rawg2), (rawd, rawd2)
        before, ones, slot_no = S[:, 0:P], S[:, P:2 * P], S[:, 2 * P:3 * P]
        rank = S[:, 384:400].rearrange("p (t e) -> p t e", t=NT)
        chose = S[:, 400:416].rearrange("p (t e) -> p t e", t=NT)
        g8 = S[:, 416:432].rearrange("p (t e) -> p t e", t=NT)
        gslot = S[:, 432:434]
        total, many = S[:, 440:448], S[:, 450:451]

        def route(m):
            w = small_loads([(rw[:, :, :], A["moe_router"][m].rearrange("(k p) e -> p k e", p=P)),
                             (before, C["before"]), (ones, C["ones"]), (slot_no, C["slots"])], after=all_idle())
            DV.run(V.tensor_copy, rh[:, :, :], rw[:, :, :], after=[w])
            DV.run(V.tensor_tensor, rl[:, :, :], rw[:, :, :], rh[:, :, :].bitcast(F32), ALU.subtract)
            PE.wait(DV.last())
            for t in range(NT):
                for k in range(KT):
                    i = three(bank[7][:, t * 8:(t + 1) * 8], (xh[:, k, :], xl[:, k, :]), (rh[:, k, :], rl[:, k, :]), t,
                              k == 0, k == KT - 1)
            scored = PE.mark(i)
            L, top, idx, num, e, g2 = (lg[:, j, :] for j in range(6))
            for t in range(NT):
                g = g8[:, t, :]
                DV.run(V.tensor_copy, L, bank[7][:, t * 8:(t + 1) * 8], after=[scored])
                DV.run(V.max, top, L)
                DV.run(V.max_index, idx.bitcast(U32), top, L)
                DV.run(V.tensor_copy, num, idx.bitcast(U32))
                d = DV.run(V.tensor_tensor, e[:, 0:1], top[:, 1:2], top[:, 0:1], ALU.subtract)
                x = AC.run(K.activation, e[:, 1:2], e[:, 0:1], ACT.Exp, after=[d])
                DV.run(V.tensor_scalar, e[:, 2:3], e[:, 1:2], 1.0, None, ALU.add, after=[x])
                DV.run(V.reciprocal, e[:, 3:4], e[:, 2:3])
                DV.run(V.tensor_tensor, e[:, 4:5], e[:, 1:2], e[:, 3:4], ALU.mult)
                DV.run(V.tensor_scalar, g, iota[:, :], num[:, 0:1], e[:, 3:4], ALU.is_equal, ALU.mult)
                DV.run(V.tensor_scalar, g2, iota[:, :], num[:, 1:2], e[:, 4:5], ALU.is_equal, ALU.mult)
                DV.run(V.tensor_tensor, g, g, g2, ALU.add)
                DV.run(V.tensor_scalar, chose[:, t, :], iota[:, :], num[:, 0:1], None, ALU.is_equal)
                DV.run(V.tensor_scalar, g2, iota[:, :], num[:, 1:2], None, ALU.is_equal)
                DV.run(V.tensor_tensor, chose[:, t, :], chose[:, t, :], g2, ALU.add)
            PE.wait(DV.last())
            T.matmul(bank[7][:, 0:8], before, chose[:, 0, :], start=True, stop=True)
            T.matmul(bank[7][:, 8:16], ones, chose[:, 0, :], start=True, stop=False)
            T.matmul(bank[7][:, 8:16], before, chose[:, 1, :], start=False, stop=True)
            T.matmul(bank[7][:, 16:24], ones, chose[:, 0, :], start=True, stop=False)
            i = T.matmul(bank[7][:, 16:24], ones, chose[:, 1, :], start=False, stop=True)
            ranked = PE.mark(i)
            DV.run(V.tensor_copy, S[:, 384:400], bank[7][:, 0:16], after=[ranked])
            DV.run(V.tensor_copy, total, bank[7][:, 16:24])
            DV.run(V.tensor_reduce, many, total, AX.X, ALU.max)
            DV.run(V.tensor_scalar, many, many, P + 0.5, None, ALU.is_gt)
            DV.run(V.tensor_copy, flag[:, :], many)
            for t in range(NT):
                DV.run(V.tensor_scalar, U[:, t, :], H[:, t, :], ALPHA, None, ALU.mult)
            for t in range(NT):
                hi = AC.run(K.copy, HH[:, t, :], H[:, t, :], after=[DV.last()])
                DV.run(V.tensor_tensor, HL[:, t, :], H[:, t, :], HH[:, t, :].bitcast(F32), ALU.subtract, after=[hi])

        names = ["ld0", "ld1", "ldd0", "ldd1", "hi", "lo", "hid", "lod", "mm", "ev", "si", "tr", "hth", "htl", "dn", "sel", "ga", "xhi",
                 "xlo", "tp", "st", "gs", "yh", "yl", "sc", "ua"]
        passes = [{x: sem(f"moe{q}_{x}") for x in names} for q in range(2)]

        def at(eng, s, value):
            if not isinstance(value, int) or value > 0:
                eng.wait_ge(s, value)

        def moe_loads(q, wgu):
            def load(e, j, f, fp):
                n = e * NFF + f
                par = (j + fp) % 2
                at(Y, q["lo"], 2 * n - 2)
                for m in range(2):
                    Y.dma_start(RAWG[par][:, :, m * HCH:(m + 1) * HCH],
                                wgu[e].rearrange("(k p) n -> p k n", p=P)[:, :, bass.ds(f * HCH + m * DFF, HCH)]
                                ).then_inc(q[f"ld{par}"], 16)

            def expert(e, j):
                load(e, j, 0, 0)
                if isinstance(e, int) and e == 0:
                    load(e, j, 1, 1)
                    load(e, j, 2, 2)
                with nc.sync.Fori(1 if isinstance(e, int) and e == 0 else 0, NFF // 2) as r:
                    for fp in (1, 2):
                        load(e, j, r * 2 + fp, fp)
            expert(0, 0)
            expert(1, 1)
            with nc.sync.Fori(1, EXPERTS // 2) as r:
                for j in range(2):
                    expert(r * 2 + j, j)
            SP.seen.clear()

        def moe_pass(q, wd):
            s = q

            def load_down(n, par):
                at(K, s["lod"], n - 1)
                K.dma_start(RAWD[par][:, :, :], wd[bass.ds(n * HCH, HCH), :].rearrange("(k p) n -> p k n", p=P)
                            ).then_inc(s[f"ldd{par}"], 16)

            def cut_up(n, par):
                for u in range(2):
                    src, hi, lo = (x[:, 4 * u:4 * u + 4, :] for x in (RAWG[par], wh[:, par, :, :], wl[:, par, :, :]))
                    at(K, s[f"ld{par}"], 16 * (n - par) + 32)
                    at(K, s["mm"], n - 1)
                    K.copy(hi, src).then_inc(s["hi"], 1)
                    at(V, s["hi"], 2 * n + u + 1)
                    V.tensor_tensor(lo, src, hi.bitcast(F32), ALU.subtract).then_inc(s["lo"], 1)

            def down_products(n, par, j):
                at(T, s["lod"], n + 1)
                at(T, s["htl"], n + 1)
                tok = slice(par * P, (par + 1) * P)
                for k in range(2):
                    for xx, ww in ((hh, dh), (hh, dl), (hl, dh)):
                        for m in range(2):
                            mm = T.matmul(bank[2 * j + m][:, :], xx[:, k, tok], ww[:, k, m * CH:(m + 1) * CH],
                                          start=False, stop=False, skip_group_check=True)
                mm.then_inc(s["dn"], 1)

            def slot(e, j, f, fp, prev, cut_next=True, between=(), after=()):
                n = e * NFF + f
                par = (j + fp) % 2
                if cut_next:
                    cut_up(n + 1, 1 - par)
                if fp == 0:
                    at(T, s["xlo"], 2 * e + 2)
                at(T, s["ev"], n - 1)
                for k in range(KT):
                    if k % 4 == 0:
                        at(T, s["lo"], 2 * n + k // 4 + 1)
                    mm = three(bank[4 + par][:, :], (xh[:, k, :], xl[:, k, :]), (wh[:, par, k, :], wl[:, par, k, :]), j,
                               k == 0, k == KT - 1)
                mm.then_inc(s["mm"], 1)
                if prev is not None:
                    down_products(n - 1, 1 - par, prev)
                for piece in between:
                    piece()
                at(K, s["mm"], n + 1)
                at(K, s["ev"], n - 1)
                K.activation(SG[:, par, :], bank[4 + par][:, 0:HCH], ACT.Silu).then_inc(s["si"], 1)
                at(V, s["si"], n + 1)
                at(V, s["tr"], n - 1)
                if fp == 0:
                    at(V, s["gs"], e + 1)
                V.scalar_tensor_tensor(HB[:, par, :], SG[:, par, :], gslot[:, j:j + 1], bank[4 + par][:, HCH:CH],
                                       ALU.mult, ALU.mult).then_inc(s["ev"], 1)
                at(T, s["ev"], n + 1)
                at(T, s["htl"], n)
                for k in range(2):
                    tr = T.transpose(bank[6][:, k * P:(k + 1) * P], HB[:, par, k * P:(k + 1) * P], ident[:, :])
                tr.then_inc(s["tr"], 1)
                at(K, s[f"ldd{par}"], 8 * (n - par) + 16)
                at(K, s["dn"], n)
                K.copy(dh[:, :, :], RAWD[par][:, :, :]).then_inc(s["hid"], 1)
                at(V, s["hid"], n + 1)
                V.tensor_tensor(dl[:, :, :], RAWD[par][:, :, :], dh[:, :, :].bitcast(F32), ALU.subtract
                                ).then_inc(s["lod"], 1)
                tok = slice(par * P, (par + 1) * P)
                src = bank[6][:, 0:2 * P].rearrange("p (k n) -> p k n", k=2)
                at(K, s["tr"], n + 1)
                K.copy(hh[:, :, tok], src).then_inc(s["hth"], 1)
                at(V, s["hth"], n + 1)
                V.tensor_tensor(hl[:, :, tok], src, hh[:, :, tok].bitcast(F32), ALU.subtract).then_inc(s["htl"], 1)
                for piece in after:
                    piece()
                if cut_next:
                    load_down(n + 1, 1 - par)

            def choose(e, j):
                at(V, s["tp"], e - 1)
                for t in range(NT):
                    i = V.tensor_scalar(SEL_R[:, j, t, :], slot_no, rank[:, t, bass.ds(e, 1)], chose[:, t, bass.ds(e, 1)],
                                        ALU.is_equal, ALU.mult)
                i.then_inc(s["sel"], 1)

            def gather(e, j, h):
                at(T, s["sel"], e + 1)
                at(T, s["gs"], e)
                at(T, s["xlo"], 2 * e + h)
                for kk in range(4):
                    ks = slice((4 * h + kk) * P, (4 * h + kk + 1) * P)
                    for t in range(NT):
                        for x in (HH, HL):
                            i = T.matmul(bank[7][:, kk * P:(kk + 1) * P], x[:, t, ks], SEL_R[:, j, t, :],
                                         start=t == 0 and x is HH, stop=t == 1 and x is HL)
                i.then_inc(s["ga"], 1)

            def cut_gathered(e, j, h):
                src = bank[7][:, :].rearrange("p (k n) -> p k n", n=P)
                xs = (slice(None), slice(4 * h, 4 * h + 4), slice(j * P, (j + 1) * P))
                at(K, s["ga"], 2 * e + h + 1)
                K.copy(xh[xs], src).then_inc(s["xhi"], 1)
                at(V, s["xhi"], 2 * e + h + 1)
                V.tensor_tensor(xl[xs], src, xh[xs].bitcast(F32), ALU.subtract).then_inc(s["xlo"], 1)

            def turn_choice(e, j):
                at(T, s["xlo"], 2 * e + 2)
                for t in range(NT):
                    T.transpose(bank[7][:, t * P:(t + 1) * P], SEL_R[:, j, t, :].bitcast(F32), ident[:, :])
                for t in range(NT):
                    i = T.matmul(bank[7][:, SEQ:SEQ + 1], SEL_R[:, j, t, :].bitcast(F32), g8[:, t, bass.ds(e, 1)],
                                 start=t == 0, stop=t == 1)
                i.then_inc(s["tp"], 1)

            def keep_choice(e, j):
                at(K, s["tp"], e + 1)
                at(K, s["sc"], 2 * e - 2)
                K.copy(SEL_T[:, j, :], bank[7][:, 0:SEQ]).then_inc(s["st"], 1)
                at(V, s["st"], e + 1)
                V.tensor_copy(gslot[:, j:j + 1], bank[7][:, SEQ:SEQ + 1]).then_inc(s["gs"], 1)

            def open_sums(e, j):
                at(T, s["ua"], 2 * e - 2)
                for m in range(2):
                    T.matmul(bank[2 * j + m][:, :], zb[:, 0:P], zb[:, :], start=True, stop=False,
                             skip_group_check=True)

            def cut_sums(e, j):
                for m in range(2):
                    cs = slice(m * CH, (m + 1) * CH)
                    at(K, s["dn"], e * NFF + NFF)
                    at(K, s["sc"], 2 * e)
                    K.copy(YH[:, cs], bank[2 * j + m][:, :]).then_inc(s["yh"], 1)
                    at(V, s["yh"], 2 * e + m + 1)
                    V.tensor_tensor(YL[:, cs], bank[2 * j + m][:, :], YH[:, cs].bitcast(F32), ALU.subtract
                                    ).then_inc(s["yl"], 1)

            def scatter(e, j, t):
                at(T, s["yl"], 2 * e + 2)
                at(T, s["st"], e + 1)
                at(T, s["ua"], 2 * e + t)
                for m in range(2):
                    cs = slice(m * CH, (m + 1) * CH)
                    T.matmul(bank[2 * j + m][:, :], SEL_T[:, j, t * P:(t + 1) * P], YH[:, cs], start=True, stop=False)
                    i = T.matmul(bank[2 * j + m][:, :], SEL_T[:, j, t * P:(t + 1) * P], YL[:, cs], start=False, stop=True)
                i.then_inc(s["sc"], 1)

            def add(e, j, t):
                at(V, s["sc"], 2 * e + t + 1)
                at(V, s["ua"], 2 * e + t)
                for m in range(2):
                    cs = slice(m * CH, (m + 1) * CH)
                    i = V.tensor_tensor(U[:, t, cs], U[:, t, cs], bank[2 * j + m][:, :], ALU.add)
                i.then_inc(s["ua"], 1)

            def expert(e, j, first=False, last=False):
                b, a = ([[] for _ in range(4)] for _ in range(2))
                k = 1 - j
                if not first:
                    a[0].append(lambda: cut_sums(e - 1, k))
                    for t in range(NT):
                        b[1 + t].append(lambda t=t: scatter(e - 1, k, t))
                        a[1 + t].append(lambda t=t: add(e - 1, k, t))
                if not last:
                    a[0].append(lambda: choose(e + 1, k))
                    for h in range(2):
                        b[1 + h].append(lambda h=h: gather(e + 1, k, h))
                        a[1 + h].append(lambda h=h: cut_gathered(e + 1, k, h))
                    b[3].append(lambda: turn_choice(e + 1, k))
                    a[3].append(lambda: keep_choice(e + 1, k))
                slot(e, j, 0, 0, None if first else k, after=a[0])
                open_sums(e, j)
                for f in (1, 2, 3):
                    slot(e, j, f, f, j, between=b[f], after=a[f])
                slot(e, j, 4, 4, j)
                with nc.Fori(2, NFF // 2 - (1 if last else 0)) as r:
                    for fp in (1, 2):
                        slot(e, j, r * 2 + fp, fp, j)
                if last:
                    slot(e, j, NFF - 2, 1, j)
                    slot(e, j, NFF - 1, 2, j, cut_next=False)

            K.preload_act_table(ACT.Silu)
            load_down(0, 0)
            cut_up(0, 0)
            choose(0, 0)
            for h in range(2):
                gather(0, 0, h)
                cut_gathered(0, 0, h)
            turn_choice(0, 0)
            keep_choice(0, 0)
            expert(0, 0, first=True)
            expert(1, 1)
            with nc.Fori(1, EXPERTS // 2 - 1) as r:
                for j in range(2):
                    expert(r * 2 + j, j)
            expert(EXPERTS - 2, 0)
            expert(EXPERTS - 1, 1, last=True)
            down_products(EXPERTS * NFF - 1, (EXPERTS * NFF - 1) % 2, 1)
            cut_sums(EXPERTS - 1, 1)
            for t in range(NT):
                scatter(EXPERTS - 1, 1, t)
                add(EXPERTS - 1, 1, t)

        def moe(m, g_free):
            wgu = A["moe_w_gu"][m]
            wd = A["moe_w_down"][m].rearrange("e f n -> (e f) n")
            everything = [(s, v) for q in passes for s, v in ((q["ua"], 2 * EXPERTS), (q["dn"], EXPERTS * NFF))]
            SP.wait((s_lo, 2 * c.loads), *g_free)
            moe_loads(passes[0], wgu)
            for e in (PE, DV, AC):
                e.wait(*all_idle())
            moe_pass(passes[0], wd)
            for e in (PE, DV, AC, SP, PO):
                for x, v in everything[:2]:
                    e.eng.wait_ge(x, v)
                e.wait(*all_idle())
            again = nc.values_load(flag[0:1, 0:1], min_val=0, max_val=1)
            with nc.If(again > 0):
                V.tensor_scalar(S[:, 384:400], S[:, 384:400], -float(P), None, ALU.add).then_inc(s_again, 1)
                for e in (V, T, K, Y, Q):
                    e.wait_ge(s_again, 1)
                moe_loads(passes[1], wgu)
                moe_pass(passes[1], wd)
                for e in (PE, DV, AC, SP, PO):
                    for x, v in everything[2:]:
                        e.eng.wait_ge(x, v)
            forget()

        def angles():
            load = small_loads([(pos[:, :], A["positions_2"].rearrange("a (t p) -> p (a t)", p=P)),
                                (invf[:, :], C["inv_freq"])], after=[DV.last()])
            n = NT * ROT2 // 2
            x, k, y, z = (S[:, 3072 + j * n:3072 + (j + 1) * n] for j in range(4))
            pf = lam[:, 0:NT]
            two_pi = 2 * np.pi
            c1 = 6.28125
            c2 = float(np.round((two_pi - c1) * 2 ** 20) / 2 ** 20)
            c3 = float(two_pi - c1 - c2)
            magic = 1.5 * 2.0 ** 23
            DV.run(V.tensor_copy, pf, pos[:, :], after=[load])
            for t in range(NT):
                DV.run(V.tensor_scalar, x[:, t * 8:(t + 1) * 8], invf[:, :], pf[:, t:t + 1], None, ALU.mult)
            DV.run(V.tensor_scalar, k, x, 1.0 / two_pi, magic, ALU.mult, ALU.add)
            DV.run(V.tensor_scalar, k, k, -magic, None, ALU.add)
            for part in (c1, c2, c3):
                DV.run(V.scalar_tensor_tensor, x, k, -part, x, ALU.mult, ALU.add)
            DV.run(V.tensor_scalar, y, x, float(np.pi / 2), None, ALU.add)
            DV.run(V.tensor_scalar, z, y, float(np.pi), None, ALU.is_gt)
            DV.run(V.scalar_tensor_tensor, y, z, -two_pi, y, ALU.mult, ALU.add)
            lim = 3.1415925
            for v in (x, y):
                DV.run(V.tensor_scalar, v, v, lim, -lim, ALU.min, ALU.max)
            AC.run(K.activation, k, x, ACT.Sin, after=[DV.last()])
            sc_ = AC.run(K.activation, z, y, ACT.Sin)
            for t in range(NT):
                sn, cs = k[:, t * 8:(t + 1) * 8], z[:, t * 8:(t + 1) * 8]
                DV.run(V.tensor_copy, rope2[:, t, 0, 0:8], cs, after=[sc_])
                DV.run(V.tensor_copy, rope2[:, t, 0, 8:16], cs)
                DV.run(V.tensor_scalar, rope2[:, t, 1, 0:8], sn, -1.0, None, ALU.mult)
                DV.run(V.tensor_copy, rope2[:, t, 1, 8:16], sn)

        def half_ffn_loads(l, j):
            ffn_all_loads(A["ffn_w_gate_2"][l, j], A["ffn_w_up_2"][l, j])

        def half_ffn(l, j, last=False):
            idle = all_idle()
            for t in range(NT):
                rms_rows(H[:, t, :], U[:, t, :], D, 1e-6, t, after=idle)
            PE.wait(turn(U, gain=cols[:, (3 * l + 2 * j) * KT:(3 * l + 2 * j + 1) * KT], after=all_idle()))
            done = ffn(NFF, A["ffn_w_down_2"][l, j], after=all_idle(), last=last)
            for t in range(NT):
                for m in range(2):
                    cs = slice(m * CH, (m + 1) * CH)
                    DV.run(V.scalar_tensor_tensor, H[:, t, cs], bank[2 * t + m][:, :], 0.5, H[:, t, cs],
                           ALU.mult, ALU.add, after=[done])

        def select_keys():
            for e in (PE, DV, AC):
                e.wait(*all_idle())
            turned, scored, relu, used = {}, {}, {}, {}
            DV.run(V.tensor_copy, ISC[:, :, :], cmask[:, :, :])
            for i in range(IDX_HEADS + 1):
                if i < IDX_HEADS:
                    PE.wait(turned.get(i - 2))
                    for j in range(2):
                        for t in range(NT):
                            c0 = IQ + i * HD if j == 0 else IK
                            tr = T.transpose(bank[6 + i % 2][0:HD, (2 * j + t) * P:(2 * j + t + 1) * P],
                                             Z[:, t, c0:c0 + HD], ident[:, :])
                    m = PE.mark(tr)
                    turned[i] = AC.run(K.copy, QKT[0:HD, i % 2, 0, :], bank[6 + i % 2][0:HD, :],
                                       after=[m, scored.get(i - 2)])
                h = i - 1
                if h >= 0:
                    b = h % 2
                    PE.wait(turned[h], relu.get(h - 2))
                    for t in range(NT):
                        mm = T.matmul(halves(b)[:, t, :], QKT[0:HD, b, 0, t * P:(t + 1) * P],
                                      QKT[0:HD, b, 0, SEQ:2 * SEQ], start=True, stop=True)
                    scored[h] = PE.mark(mm)
                    relu[h] = AC.run(K.activation, PR[:, b, :, :], halves(b), ACT.Relu,
                                     after=[scored[h], used.get(h - 2)])
                    for t in range(NT):
                        used[h] = DV.run(V.scalar_tensor_tensor, ISC[:, t, :], PR[:, b, t, :],
                                         Z[:, t, IW + h:IW + h + 1], ISC[:, t, :], ALU.mult, ALU.add,
                                         after=[relu[h]])
            for r in range(TOPK // 8):
                for t in range(NT):
                    DV.run(V.max, ss[:, 8 * t:8 * t + 8], ISC[:, t, :])
                    DV.run(V.match_replace, ISC[:, t, :], ss[:, 8 * t:8 * t + 8], ISC[:, t, :], GONE)
            DV.run(V.tensor_scalar, SEL, ISC, GONE / 2, NEG, ALU.is_gt, ALU.mult)
            DV.run(V.tensor_tensor, SEL, SEL, cmask[:, :, :], ALU.add)


        DV.run(V.memset, mhalf[:, :], -0.5)
        DV.run(V.memset, zb[:, :], 0.0)
        consts = small_loads([(ident[:, :], C["ident"]), (cmask[:, :, :], C["causal"]),
                              (ropeb[:, :, :, :], C["rope_b"]), (ropec[:, :, :, :], C["rope_c"]),
                              (iota[:, :], C["iota"])])
        crow = G[:, 0, 0:P]
        crows = small_loads([
            (G[0:48, 0, 0:P], A["norm_g_2"].rearrange("l j (k p) -> (l j k) p", p=P)),
            (G[48:52, 0, 0:P], A["mla_q_norm"].rearrange("l (k p) -> (l k) p", p=P)),
            (G[52:54, 0, 0:P], A["mla_kv_norm"])])
        xin = small_loads([(U[:, :, :], A["x"].rearrange("a (t p) n -> p (a t) n", p=P))])
        ROW_LN, ROW_Q, ROW_KV = 0, 48, 52


        W1 = [CH, CH, CH, MAIN1 - 3 * CH]
        W2 = [CH] * 6 + [MAIN2 - 6 * CH]

        def stream(w, c0, widths, skip=0):
            for i, width in enumerate(widths):
                if i >= skip:
                    linear_loads(w, c0, width)
                c0 += width

        def stream_branches(wa, wb, wc):
            for m in range(2):
                cs = slice(m * CH, (m + 1) * CH)
                load_step([(rawg[:, k0:k1, :], w[(k0 - r) * P:(k1 - r) * P, cs].rearrange("(k p) n -> p k n", p=P))
                           for w, k0, k1, r in ((wa, 0, 2, 0), (wb, 2, 4, 2), (wb, 4, 6, 2), (wc, 6, 8, 6))])

        BRANCHES1 = [(0, 3, range(0, 2)), (1, 4, range(2, 6)), (2, 5, range(6, 8))]
        BRANCHES2 = [(0, 3, range(0, 2)), (1, 4, range(2, 4)), (2, 5, range(4, 8))]

        linear_loads(A["w_in"][0], 0, CH)
        cut(0, 0)
        PE.wait(crows, consts)
        turned = PE.mark(T.transpose(bank[0][:, 0:54], G[0:54, 0, 0:P], ident[0:54, 0:54]))
        DV.run(V.tensor_copy, cols[:, :], bank[0][:, 0:54], after=[turned])
        layer_norm(A["emb_ln_g"], A["emb_ln_b"], after=[xin])

        for l in range(DEPTH):
            idle = all_idle()
            rowp = small_loads([(pb[:, 0:HD], A["gqa_q_norm"][l].partition_broadcast(P)),
                                (pb[:, HD:2 * HD], A["gqa_k_norm"][l].partition_broadcast(P))], after=idle)
            loads = []
            for t in range(NT):
                for half in range(2):
                    r = 2 * t + half
                    w = 2 * NA_COLS - 1
                    src = A["na_rpb"]
                    off = (l * NA_HEADS * (2 * NA_ROWS - 1) + NA_ROWS - 1 - r) * w + NA_COLS - GRID_W
                    for h in range(NA_HEADS):
                        loads.append((nab[half * 64:(half + 1) * 64, t, h, :].rearrange("p (r c) -> p r c", c=GRID_W),
                                      bass.AP(src.tensor, off + h * (2 * NA_ROWS - 1) * w,
                                              [[1, GRID_W], [w, ROWS], [1, GRID_W]])))
            wmask = S[:, 4096:4096 + SEQ]
            flip = S[:, 4096 + SEQ:4096 + SEQ + P]
            loads += [(wmask, C["window"]), (flip, C["flip"])]
            biases = small_loads(loads, after=idle + ([(s_lod, c.ff)] if c.ff else []))
            WUQ = S[:, 2816:3584].rearrange("p (k n) -> p k n", k=2)
            WUKV = S[:, 3584:4096]
            latw = small_loads([(WUQ, A["mla_w_uq"][l].rearrange("(k p) n -> p k n", p=P)),
                                (WUKV, A["mla_w_ukv"][l])], after=idle)
            stream(A["w_in"][l], 0, W1, skip=1 if l == 0 else 0)
            stream(A["w_in"][l], MAIN1, [CH] * 6)
            stream_branches(A["w_proj_a"][l], A["w_proj_b"][l], A["w_proj_c"][l])
            stream(A["w_out"][l], 0, [CH] * 2)
            stream(A["mem_wkv"][l], 0, [CH] * 4)
            stream(A["mem_wq"][l], 0, [CH] * 2)
            stream(A["mem_wo"][l], 0, [CH] * 2)

            xt = turn(H, after=[DV.last()])
            PE.wait(xt)
            linear(4, to_tokens(Z, W1), widths=W1)
            AC.eng.preload_act_table(ACT.Sigmoid)
            linear(6, to_gates)
            zdone = products_read()
            DV.wait(zdone)

            PE.wait(biases)
            for t in range(NT):
                for j in range(2):
                    pair = nab[:, t, 2 * j:2 * j + 2, :]
                    m = PE.mark(T.matmul(halves(2 * t + j), flip, pair, start=True, stop=True))
                    DV.run(V.tensor_tensor, pair, halves(2 * t + j), wmask.unsqueeze(1).to_broadcast([P, 2, SEQ]),
                           ALU.add, after=[m])
            DV.wait(rowp)
            head_norm(BQ, GQA_HEADS + GQA_KV, [(0, GQA_HEADS, pb[:, 0:HD]), (GQA_HEADS, GQA_KV, pb[:, HD:2 * HD])])
            for t in range(NT):
                rotate(heads3(Z[:, t, :], BQ, GQA_HEADS + GQA_KV), GQA_HEADS + GQA_KV, HD // 2, ropeb[:, t, :, :])
            for t in range(NT):
                rms_rows(Z[:, t, CDQ:CDQ + QR], Z[:, t, CDQ:CDQ + QR], QR, 1e-6, t)
                rms_rows(Z[:, t, CDKV:CDKV + KVR], Z[:, t, CDKV:CDKV + KVR], KVR, 1e-6, t)
            PE.wait(DV.last())
            CQT = S[:, 2048:2560].rearrange("p (k n) -> p k n", k=2)
            CKT = S[:, 2560:2816]
            for t in range(NT):
                for k in range(2):
                    T.transpose(halves(6)[:, k, t * P:(t + 1) * P], Z[:, t, CDQ + k * P:CDQ + (k + 1) * P], ident[:, :])
                i = T.transpose(halves(7)[:, 0, t * P:(t + 1) * P], Z[:, t, CDKV:CDKV + P], ident[:, :])
            turned = PE.mark(i)
            for k in range(2):
                DV.run(V.tensor_scalar, CQT[:, k, :], halves(6)[:, k, :],
                       cols[:, ROW_Q + 2 * l + k:ROW_Q + 2 * l + k + 1], None, ALU.mult, after=[turned])
            DV.run(V.tensor_scalar, CKT, halves(7)[:, 0, :], cols[:, ROW_KV + l:ROW_KV + l + 1], None, ALU.mult)
            PE.wait(DV.last(), latw)
            QC, KVC, KF = MAIN1, MAIN1 + 384, MAIN1 + 384 + 512
            for t in range(NT):
                for k in range(2):
                    T.matmul(bank[t][:, 0:384], CQT[:, k, t * P:(t + 1) * P], WUQ[:, k, :], start=k == 0, stop=k == 1)
                i = T.matmul(bank[2 + t][:, :], CKT[:, t * P:(t + 1) * P], WUKV, start=True, stop=True)
            up = PE.mark(i)
            for t in range(NT):
                DV.run(V.tensor_copy, Z[:, t, QC:QC + 384], bank[t][:, 0:384], after=[up])
                DV.run(V.tensor_copy, Z[:, t, KVC:KVC + 512], bank[2 + t][:, :])
                rotate(heads3(Z[:, t, :], QC, MLA_HEADS, 96)[:, :, NOPE:], MLA_HEADS, ROPE_C // 2, ropec[:, t, :, :])
                rotate(heads3(Z[:, t, :], CKR, 1, ROPE_C), 1, ROPE_C // 2, ropec[:, t, :, :])
                kf = heads3(Z[:, t, :], KF, MLA_HEADS, 96)
                DV.run(V.tensor_copy, kf[:, :, 0:NOPE], heads3(Z[:, t, :], KVC, MLA_HEADS, 128)[:, :, 0:NOPE])
                DV.run(V.tensor_copy, kf[:, :, NOPE:],
                       heads3(Z[:, t, :], CKR, 1, ROPE_C).to_broadcast([P, MLA_HEADS, ROPE_C]))
            hs = [head(zc(AQ + h * HD), zc(AK + h * HD), zc(AV + h * HD), uc(h * HD), HD ** -0.5,
                       bias=nab[:, :, h, :]) for h in range(NA_HEADS)]
            hs += [head(zc(BQ + h * HD), zc(BK + h // 4 * HD), zc(BV + h // 4 * HD), uc(256 + h * HD), HD ** -0.5)
                   for h in range(GQA_HEADS)]
            hs += [head(zc(QC + h * 96, 96), zc(KF + h * 96, 96), zc(KVC + h * 128 + NOPE), uc(768 + h * VC),
                        (NOPE + ROPE_C) ** -0.5, dk=96) for h in range(MLA_HEADS)]
            attention(hs, after=all_idle())
            if l % 2 == 0:
                ffn_all_loads(*(A["ffn_w_gu"][l // 2][:, m * DFF:(m + 1) * DFF] for m in range(2)))
            snapshot("heads", l, U)

            PE.wait(turn(U, after=all_idle()))
            linear(2, merge, groups=BRANCHES1)
            PE.wait(turn(U, after=all_idle()))
            linear(2, add_residual)
            layer_norm(A["ln_g"][l, 0], A["ln_b"][l, 0], after=all_idle())
            snapshot("mix", l, H)

            mem = small_loads([(U[:, :, :], A["mem"].rearrange("a (t p) n -> p (a t) n", p=P))], after=all_idle())
            PE.wait(turn(U, after=[mem] + all_idle()))
            linear(4, to_tokens(Z))
            PE.wait(turn(H, after=all_idle()))
            linear(2, to_tokens(G))
            w = D // MEM_HEADS

            def mem_head(h):
                return head(lambda t, k: G[:, t, h * w + k * P:h * w + (k + 1) * P],
                            lambda t, k: Z[:, t, h * w + k * P:h * w + (k + 1) * P],
                            lambda t: Z[:, t, D + h * w:D + (h + 1) * w], uc(h * w, w), w ** -0.5, dk=P, dv=w, nk=2)
            attention([mem_head(h) for h in range(MEM_HEADS)], after=all_idle())
            g_free = all_idle()
            PE.wait(turn(U, after=all_idle()))
            linear(2, add_residual, last=l % 2 == 1)
            layer_norm(A["ln_g"][l, 1], A["ln_b"][l, 1], after=all_idle())
            snapshot("mem", l, H)

            idle = all_idle()
            PE.wait(turn(H, after=idle))
            if l % 2 == 0:
                done = ffn(NFF, A["ffn_w_down"][l // 2], after=all_idle())
                for t in range(NT):
                    for m in range(2):
                        cs = slice(m * CH, (m + 1) * CH)
                        DV.run(V.scalar_tensor_tensor, U[:, t, cs], H[:, t, cs], ALPHA, bank[2 * t + m][:, :],
                               ALU.mult, ALU.add, after=[done])
            else:
                route(l // 2)
                moe(l // 2, g_free)
                half_ffn_loads(0, 0)
                cut(c.step, c.step % 2)
            layer_norm(A["ln_g"][l, 2], A["ln_b"][l, 2], after=all_idle())
            snapshot("ffn", l, H)

        angles()
        for l in range(DEPTH):
            last = l == DEPTH - 1
            if l > 0:
                half_ffn_loads(l, 0)
            half_ffn(l, 0)
            snapshot("ffn2", l, H)
            idle = all_idle()
            rowp = small_loads([(pb[:, 0:6 * HD], A["qk_norm_g_2"][l].rearrange("a b -> (a b)").partition_broadcast(P)),
                                (pb[:, 384:512], A["diff_subln_g_2"][l].partition_broadcast(P)),
                                (pb[:, 512:768], A["lambda_params_2"][l].rearrange("a b -> (a b)").partition_broadcast(P))],
                               after=idle)
            stream(A["w_in_2"][l], 0, W2)
            stream(A["w_in_2"][l], MAIN2, [CH] * 6)
            stream(A["w_branch_2"][l], 0, [CH] * 2)
            stream(A["w_out_2"][l], 0, [CH] * 2)
            for t in range(NT):
                rms_rows(H[:, t, :], U[:, t, :], D, 1e-6, t, after=idle)
            PE.wait(turn(U, gain=cols[:, (3 * l + 1) * KT:(3 * l + 2) * KT], after=all_idle()))
            linear(7, to_tokens(Z, W2), widths=W2)
            AC.eng.preload_act_table(ACT.Sigmoid)
            linear(6, to_gates)
            DV.wait(products_read(), rowp)

            def gain(j):
                return pb[:, j * HD:(j + 1) * HD]
            head_norm(A2Q, 5, [(0, 4, gain(0)), (4, 1, gain(1))])
            head_norm(B2Q, 8, [(0, 4, gain(2)), (4, 4, gain(3))])
            head_norm(C2Q, 16, [(0, 8, gain(4)), (8, 8, gain(5))])
            for t in range(NT):
                for c0, nh in ((A2Q, 5), (IQ, 9), (B2Q, 8), (C2Q, 16)):
                    rotate(heads3(Z[:, t, :], c0, nh), nh, ROT2 // 2, rope2[:, t, :, :])
                DV.run(V.tensor_scalar, Z[:, t, IW:IW + IDX_HEADS], Z[:, t, IW:IW + IDX_HEADS],
                       (IDX_HEADS * HD) ** -0.5, None, ALU.mult)
            init = 0.8 - 0.6 * float(np.exp(-0.3 * l))
            for j in range(2):
                DV.run(V.tensor_tensor_reduce, S[:, 0:HD], pb[:, 512 + 2 * j * HD:512 + (2 * j + 1) * HD],
                       pb[:, 512 + (2 * j + 1) * HD:512 + (2 * j + 2) * HD], 1.0, 0.0, ALU.mult, ALU.add,
                       lam[:, j:j + 1])
            e = AC.run(K.activation, lam[:, 2:4], lam[:, 0:2], ACT.Exp, after=[DV.last()])
            DV.run(V.tensor_tensor, lam[:, 4:5], lam[:, 3:4], lam[:, 2:3], ALU.subtract, after=[e])
            DV.run(V.tensor_scalar, lam[:, 4:5], lam[:, 4:5], -init, None, ALU.add)
            select_keys()
            hs = [head(zc(A2Q + h * HD), zc(A2K), zc(A2V), uc(h * HD), HD ** -0.5, bias=SEL) for h in range(4)]
            hs += [head(zc(B2Q + h * HD), zc(B2K + h * HD), zc(B2V + h * HD), uc(256 + h * HD), HD ** -0.5,
                        bias=cmask) for h in range(4)]
            hs += [head(zc(C2Q + (2 * h + j) * HD), zc(C2K + (2 * h + j) * HD), zc(C2V + h * P, P),
                        uc(512 + h * P, P), HD ** -0.5, dv=P, bias=cmask, weight=lam[:, 4:5] if j else None)
                   for h in range(4) for j in range(2)]
            attention(hs, after=all_idle())
            half_ffn_loads(l, 1)
            for t in range(NT):
                x = U[:, t, 512:D].rearrange("p (h d) -> p h d", d=P)
                sq = S[:, 0:512]
                DV.run(V.tensor_tensor, sq, U[:, t, 512:D], U[:, t, 512:D], ALU.mult)
                DV.run(V.tensor_reduce, ss[:, 4 * t:4 * t + 4], sq.rearrange("p (h d) -> p h d", d=P), AX.X, ALU.add)
            e = DV.run(V.tensor_scalar, ss[:, 0:8], ss[:, 0:8], 1.0 / P, 1e-6, ALU.mult, ALU.add)
            r = rsqrt(rs[:, 0:8], ss[:, 0:8], after=[e])
            DV.run(V.tensor_scalar, pb[:, 384:512], pb[:, 384:512], 1.0 - init, None, ALU.mult)
            for t in range(NT):
                x = U[:, t, 512:D].rearrange("p (h d) -> p h d", d=P)
                DV.run(V.tensor_tensor, x, x, rs[:, 4 * t:4 * t + 4].unsqueeze(2).to_broadcast([P, 4, P]), ALU.mult,
                       after=[r])
                DV.run(V.tensor_tensor, x, x, pb[:, 384:512].unsqueeze(1).to_broadcast([P, 4, P]), ALU.mult)
            snapshot("heads2", l, U)
            PE.wait(turn(U, after=all_idle()))
            linear(2, merge, groups=BRANCHES2)
            PE.wait(turn(U, after=all_idle()))
            linear(2, add_to_h)
            snapshot("mix2", l, H)
            half_ffn(l, 1, last=last)
        store_and_end(H[:, :, :])


INPUTS = ["x", "mem", "emb_ln_g", "emb_ln_b", "w_in", "na_rpb", "gqa_q_norm", "gqa_k_norm", "mla_q_norm",
          "mla_kv_norm", "mla_w_uq", "mla_w_ukv", "w_proj_a", "w_proj_b", "w_proj_c", "w_out", "mem_wq", "mem_wkv",
          "mem_wo", "ln_g", "ln_b", "ffn_w_gu", "ffn_w_down", "moe_router", "moe_w_gu", "moe_w_down",
          "positions_2", "norm_g_2", "w_in_2", "qk_norm_g_2", "lambda_params_2", "diff_subln_g_2", "w_branch_2",
          "w_out_2", "ffn_w_gate_2", "ffn_w_up_2", "ffn_w_down_2"]


def shape_constants():
    f = np.float32
    t = np.arange(SEQ)
    row, col = (t // GRID_W).astype(f), (t % GRID_W).astype(f)

    def axial(dim):
        n = dim // 4
        inv = (f(10000.0) ** (-np.arange(n, dtype=f) / f(n))).astype(f)
        ang = np.concatenate([row[:, None] * inv, col[:, None] * inv], axis=1)
        c, s = np.cos(ang).astype(f), np.sin(ang).astype(f)
        tab = np.stack([np.concatenate([c, c], 1), np.concatenate([-s, s], 1)], axis=1)
        return np.ascontiguousarray(tab.reshape(NT, P, 2, dim).transpose(1, 0, 2, 3))
    causal = np.where(t[None, :] <= t[:, None], 0.0, NEG).astype(f).reshape(NT, P, SEQ).transpose(1, 0, 2)
    c = np.arange(GRID_W)
    first = np.clip(c - NA_COLS // 2, 0, GRID_W - NA_COLS)[:, None]
    window = np.where((c[None, :] >= first) & (c[None, :] < first + NA_COLS), 0.0, NEG).astype(f)
    inv2 = (500000.0 ** (-np.arange(0, ROT2, 2) / ROT2)).astype(f)
    return {"ident": np.eye(P, dtype=f), "causal": np.ascontiguousarray(causal), "rope_b": axial(HD),
            "rope_c": axial(ROPE_C), "flip": np.kron(np.eye(P // GRID_W, dtype=f), np.eye(GRID_W, dtype=f)[::-1]),
            "window": np.tile(window, (P // GRID_W, ROWS)),
            "inv_freq": np.tile(inv2, (P, 1)), "before": np.triu(np.ones((P, P), f), 1), "ones": np.ones((P, P), f),
            "slots": np.tile(np.arange(P, dtype=f), (P, 1)), "iota": np.tile(np.arange(EXPERTS, dtype=f), (P, 1))}


def kernel(**inputs):
    import concourse.bacc as bacc
    from concourse.bass_utils import run_bass_kernel_spmd
    nc = bacc.Bacc("TRN2", target_bir_lowering=False, num_devices=1, dynamic_dma_scratch_size=4096)
    arrays = {}

    def given(name, a):
        a = np.ascontiguousarray(a)
        arrays[name] = a
        return nc.dram_tensor(name, a.shape, mybir.dt.from_np(a.dtype), kind="ExternalInput").ap()
    A = {name: given(f"in_{name}", inputs[name]) for name in INPUTS}
    C = {name: given(f"const_{name}", a) for name, a in shape_constants().items()}
    out = nc.dram_tensor("out", (1, SEQ, D), F32, kind="ExternalOutput").ap()
    program(nc, A, C, out)
    return run_bass_kernel_spmd(nc, [arrays], core_ids=[0]).results[0]["out"]
```

```python
from contextlib import ExitStack
import numpy as np
import concourse.bass as bass
from concourse import mybir

F32, F32R, BF16 = mybir.dt.float32, mybir.dt.float32r, mybir.dt.bfloat16
I32, U32 = mybir.dt.int32, mybir.dt.uint32
ALU, ACT, AX = mybir.AluOpType, mybir.ActivationFunctionType, mybir.AxisListType

P = 128
SEQ, D = 256, 1024
NT = SEQ // P
KT = D // P
CH = 512
DEPTH = 2
ALPHA = (2 * DEPTH) ** 0.25
NEG = -1.0e30
GONE = -3.0e38

GRID_W, NA_ROWS, NA_COLS = 64, 8, 16
ROWS = SEQ // GRID_W
NA_HEADS, GQA_HEADS, GQA_KV, MLA_HEADS, MEM_HEADS, HD = 4, 8, 2, 4, 4, 64
NOPE, ROPE_C, VC = 64, 32, 64
QR, KVR = 256, 128
DFF = 2816
HCH = CH // 2
NFF = DFF // HCH
EXPERTS = 8
GATES = 3 * D

AQ, AK, AV = 0, 256, 512
BQ, BK, BV = 768, 1280, 1408
CDQ, CDKV, CKR, MAIN1 = 1536, 1792, 1920, 1952
A2Q, A2K, A2V, IQ, IK, IW = 0, 256, 320, 384, 896, 960
B2Q, B2K, B2V, C2Q, C2K, C2V, MAIN2 = 968, 1224, 1480, 1736, 2248, 2760, 3272
IDX_HEADS, TOPK = 8, 64
ROT2 = 16


class Chain:

    def __init__(self, eng, sem, seen):
        self.eng, self.sem, self.n, self.seen = eng, sem, 0, seen

    def wait(self, *tokens):
        for t in tokens:
            if t is None:
                continue
            sem, value = t
            if isinstance(value, int) and value <= self.seen.get(id(sem), 0):
                continue
            if isinstance(value, int):
                self.seen[id(sem)] = value
            self.eng.wait_ge(sem, value)

    def last(self):
        return (self.sem, self.n) if self.n else None

    def run(self, fn, *args, after=(), **kw):
        self.wait(*after, self.last())
        fn(*args, **kw).then_inc(self.sem, 1)
        self.n += 1
        return self.last()

    def mark(self, ins):
        ins.then_inc(self.sem, 1)
        self.n += 1
        return self.last()


def program(nc, A, C, out):
    ctx = ExitStack()
    with ctx:
        def sb(name, shape, dt=F32):
            return ctx.enter_context(nc.sbuf_tensor(name, shape, dt))

        def sem(name):
            return ctx.enter_context(nc.semaphore(name))

        rawg = sb("raw_gu", [P, KT, CH])
        rawd = sb("raw_down", [P, 2, D])
        wh = sb("w_hi", [P, 2, KT, CH], F32R)
        wl = sb("w_lo", [P, 2, KT, CH], F32R)
        dh = sb("down_hi", [P, 2, D], F32R)
        dl = sb("down_lo", [P, 2, D], F32R)
        xh = sb("xT_hi", [P, KT, SEQ], F32R)
        xl = sb("xT_lo", [P, KT, SEQ], F32R)
        hh = sb("hiddenT_hi", [P, 2, SEQ], F32R)
        hl = sb("hiddenT_lo", [P, 2, SEQ], F32R)
        H = sb("residual", [P, NT, D])
        U = sb("token_scratch", [P, NT, D])
        z_offset = nc.sbuf_base
        Z = sb("projected", [P, NT, MAIN2])
        g_offset = nc.sbuf_base
        G = sb("gates", [P, NT, GATES])
        S = sb("scratch", [P, 5120])
        pb = sb("row_params", [P, 768])
        ident = sb("ident", [P, P])
        cmask = sb("causal", [P, NT, SEQ])
        ropeb = sb("rope_b", [P, NT, 2, HD])
        ropec = sb("rope_c", [P, NT, 2, ROPE_C])
        rope2 = sb("rope_2", [P, NT, 2, ROT2])
        cols = sb("col_params", [P, 54])
        mhalf = sb("minus_half", [P, 64])
        st = sb("stats", [P, NT, 2, 6])
        mv = sb("mean_var", [P, NT, 2])
        ss = sb("sums", [P, 64])
        rs = sb("rstd", [P, 64])
        zb = sb("zeros", [P, CH], BF16)
        lam = sb("lambda", [P, 8])
        rh, rl = sb("router_hi", [P, KT, EXPERTS], F32R), sb("router_lo", [P, KT, EXPERTS], F32R)
        flag = sb("again", [P, 1], I32)
        rw = pb[:, 448:448 + KT * EXPERTS].rearrange("p (k e) -> p k e", e=EXPERTS)
        lg = sb("router_stats", [P, 8, 8])
        iota = sb("expert_numbers", [P, EXPERTS])
        pos = sb("positions", [P, NT], I32)
        invf = sb("inverse_frequencies", [P, ROT2 // 2])

        QKH, QKL = (x[:, :, :].rearrange("p (b k j) n -> p b k (j n)", b=2, k=2) for x in (xh, xl))
        SM = S[:, 2048:3072].rearrange("p (b t n) -> p b t n", b=2, t=2)
        PR = S[:, 3072:4096].rearrange("p (b t n) -> p b t n", b=2, t=2)
        PT = S[:, 4096:5120].rearrange("p (b k n) -> p b k n", b=2, k=2)
        MEM = G[:, :, 2 * D:3 * D]
        SG = S[:, 2048:2560].rearrange("p (t n) -> p t n", t=2)
        HB = S[:, 2560:3072].rearrange("p (t n) -> p t n", t=2)
        GR, BR = S[:, 0:D], S[:, D:2 * D]
        nab = rawd[:, :, :].rearrange("p t (h n) -> p t h n", n=SEQ)
        ISC = rawd[:, 0, 0:NT * SEQ].rearrange("p (t n) -> p t n", t=NT)
        SEL = rawd[:, 1, 0:NT * SEQ].rearrange("p (t n) -> p t n", t=NT)

        bank = [ctx.enter_context(nc.psum_tensor(f"bank{i}", [P, CH], F32)) for i in range(8)]

        def halves(b):
            return bank[b][:, :].rearrange("p (a n) -> p a n", a=2)

        s_ld, s_ldd = [sem("w_loaded0"), sem("w_loaded1")], sem("down_loaded")
        s_hi, s_lo, s_hid, s_lod = sem("w_hi_cut"), sem("w_lo_cut"), sem("down_hi_cut"), sem("down_lo_cut")
        s_mm, s_ev = sem("product_done"), sem("product_read")
        s_si, s_tr, s_hth, s_htl, s_dn = sem("silu"), sem("hidden_turned"), sem("hiddenT_hi_cut"), sem(
            "hiddenT_lo_cut"), sem("down_done")
        s_out = sem("stored")
        s_again = sem("ranks_lowered")
        small = [sem(f"small{i}") for i in range(8)]
        SP = Chain(nc.sync, sem("sp"), {})
        PE = Chain(nc.tensor, sem("pe"), {})
        DV = Chain(nc.vector, sem("dve"), {})
        AC = Chain(nc.scalar, sem("act"), {})
        PO = Chain(nc.gpsimd, sem("pool"), {})
        V, T, K, Q, Y = nc.vector, nc.tensor, nc.scalar, nc.gpsimd, nc.sync
        engines = (SP, PE, DV, AC, PO)

        class Count:
            pass
        c = Count()
        c.step = 0
        c.loads = 0
        c.ff = 0
        c.ffl = 0
        c.small = 0
        c.smallv = [0] * 8

        def at_least(chain, s, value):
            if isinstance(value, int):
                if value > 0:
                    chain.wait((s, value))
            else:
                chain.eng.wait_ge(s, value)

        def small_loads(pairs, after=()):
            k = c.small % 8
            PO.wait(*after, (small[k], c.smallv[k]) if c.smallv[k] else None)
            for dst, src in pairs:
                Q.dma_start(dst, src, allow_slow_non_contiguous=True).then_inc(small[k], 16)
            c.smallv[k] += 16 * len(pairs)
            c.small += 1
            return (small[k], c.smallv[k])

        def load_step(srcs, n=None):
            s = c.loads if n is None else n
            for u in range(2):
                at_least(SP, s_lo, 2 * s - 1 + u)
                for dst, src in srcs[2 * u:2 * u + 2]:
                    Y.dma_start(dst, src).then_inc(s_ld[u], 16)
            if n is None:
                c.loads += 1

        def linear_loads(w, c0, width):
            v = w.rearrange("(k p) n -> p k n", p=P)
            load_step([(rawg[:, k:k + 2, 0:width], v[:, k:k + 2, c0:c0 + width]) for k in range(0, KT, 2)])

        def cut(s, par, width=CH):
            for u in range(2):
                src = rawg[:, 4 * u:4 * u + 4, 0:width]
                hi = wh[:, par, 4 * u:4 * u + 4, 0:width]
                at_least(AC, s_ld[u], 32 * (s + 1))
                at_least(AC, s_mm, 2 * (s - 1))
                K.copy(hi, src).then_inc(s_hi, 1)
                at_least(DV, s_hi, 2 * s + u + 1)
                V.tensor_tensor(wl[:, par, 4 * u:4 * u + 4, 0:width], src, hi.bitcast(F32),
                                ALU.subtract).then_inc(s_lo, 1)

        def three(acc, xk, wk, t, start, stop):
            (ah, al), (bh, bl) = xk, wk
            tok = slice(t * P, (t + 1) * P)
            T.matmul(acc, ah[:, tok], bh, start=start, stop=False)
            T.matmul(acc, ah[:, tok], bl, start=False, stop=False)
            return T.matmul(acc, al[:, tok], bh, start=False, stop=stop)

        def multiply(s, par, width=CH, groups=None):
            groups = groups or [(4, 5, range(KT))]
            for t in range(NT):
                at_least(PE, s_ev, 2 * s - 1 + t)
                for b in groups:
                    for k in b[2]:
                        if t == 0:
                            at_least(PE, s_lo, 2 * s + 1 + k // 4)
                        mm = three(bank[b[t]][:, 0:width], (xh[:, k, :], xl[:, k, :]),
                                   (wh[:, par, k, 0:width], wl[:, par, k, 0:width]), t,
                                   k == b[2][0], k == b[2][-1])
                mm.then_inc(s_mm, 1)

        def linear(n, evac, widths=None, next_width=CH, groups=None, last=False, beside=None):
            base = c.step
            PE.wait(products_read())

            def one(i, j):
                s = base + i
                par = (base + j) % 2
                w_next = CH
                if isinstance(i, int):
                    w_next = widths[i + 1] if widths and i + 1 < n else (next_width if i + 1 == n else CH)
                if not (last and isinstance(i, int) and i == n - 1):
                    cut(s + 1, 1 - par, w_next)
                multiply(s, par, widths[i] if widths and isinstance(i, int) else CH, groups)
                for t in range(NT):
                    evac(i, t, (s_mm, 2 * s + t + 1))

            pairs = (n - 2) // 2 if n >= 6 and not beside else 0
            if pairs:
                with nc.Fori(0, pairs) as r:
                    for j in range(2):
                        one(r * 2 + j, j)
                forget()
            for i in range(2 * pairs, n):
                one(i, i)
                if beside:
                    next(beside, None)
            c.step += n
            now(beside or ())

        def now(work):
            for _ in work:
                pass

        def products_read():
            return (s_ev, 2 * c.step)

        def forget():
            for e in engines:
                e.seen.clear()

        def turn(src, gain=None, after=(), prepare=None):
            done, ready = {}, {}
            PE.wait(*after)
            if prepare:
                ready[0] = prepare(0)
            for r in range(KT // 2):
                if prepare:
                    if r + 1 < KT // 2:
                        ready[r + 1] = prepare(r + 1)
                    PE.wait(*ready[r])
                b = 6 + r % 2
                for kk in range(2):
                    k = 2 * r + kk
                    for t in range(NT):
                        PE.wait(done.get(r - 2))
                        i = T.transpose(bank[b][:, kk * SEQ + t * P:kk * SEQ + (t + 1) * P],
                                        src[:, t, k * P:(k + 1) * P], ident[:, :])
                turned = PE.mark(i)
                if gain is None:
                    hi = AC.run(K.copy, xh[:, 2 * r:2 * r + 2, :], halves(b), after=[turned])
                    done[r] = DV.run(V.tensor_tensor, xl[:, 2 * r:2 * r + 2, :], halves(b),
                                     xh[:, 2 * r:2 * r + 2, :].bitcast(F32), ALU.subtract, after=[hi])
                else:
                    for k in (2 * r, 2 * r + 1):
                        hi = AC.run(K.activation, xh[:, k, :], halves(b)[:, k - 2 * r, :], ACT.Copy,
                                    scale=gain[:, k:k + 1], after=[turned])
                    for k in (2 * r, 2 * r + 1):
                        done[r] = DV.run(V.scalar_tensor_tensor, xl[:, k, :], halves(b)[:, k - 2 * r, :],
                                         gain[:, k:k + 1], xh[:, k, :].bitcast(F32), ALU.mult,
                                         ALU.subtract, after=[hi])
            return done[KT // 2 - 1]

        def ffn_loads(s, wa, wg, cc):
            load_step([(rawg[:, 4 * u:4 * u + 4, m * HCH:(m + 1) * HCH],
                        w.rearrange("(k p) n -> p k n", p=P)[:, 4 * u:4 * u + 4, bass.ds(cc * HCH, HCH)])
                       for u in range(2) for m, w in enumerate((wa, wg))], n=s)

        def ffn_all_loads(wa, wg):
            with nc.sync.Fori(0, NFF) as i:
                ffn_loads(i + c.loads, wa, wg, i)
            c.loads += NFF
            SP.seen.clear()

        def ffn(n, wd, after=(), last=False):
            s0, g0 = c.step, c.ff

            def load_down(i):
                at_least(AC, s_lod, g0 + i)
                K.dma_start(rawd[:, :, :], wd[bass.ds(i * HCH, HCH), :].rearrange("(k p) n -> p k n", p=P)
                            ).then_inc(s_ldd, 16)

            PE.wait(*after, products_read())
            DV.wait(*after)
            AC.wait(*after)
            load_down(0)
            for b in range(4):
                T.matmul(bank[b][:, :], zb[:, 0:P], zb[:, :], start=True, stop=False)

            def down(g, stop=False):
                at_least(PE, s_lod, g + 1)
                at_least(PE, s_htl, g + 1)
                for t in range(NT):
                    tok = slice(t * P, (t + 1) * P)
                    for k in range(2):
                        for xx, ww in ((hh, dh), (hh, dl), (hl, dh)):
                            for m in range(2):
                                mm = T.matmul(bank[2 * t + m][:, :], xx[:, k, tok], ww[:, k, m * CH:(m + 1) * CH],
                                              start=False, stop=stop and k == 1 and xx is hl)
                    if stop and t == 0:
                        first = PE.mark(mm)
                mm.then_inc(s_dn, 1)
                return first if stop else None

            def slot(i, j, first=False, cut_next=True, more=True):
                s, g, par = s0 + i, g0 + i, (s0 + j) % 2
                if cut_next:
                    cut(s + 1, 1 - par)
                multiply(s, par)
                if not first:
                    down(g - 1)
                for t in range(NT):
                    at_least(AC, s_mm, 2 * s + t + 1)
                    at_least(AC, s_ev, 2 * s - 1 + t)
                    K.activation(SG[:, t, :], bank[4 + t][:, 0:HCH], ACT.Silu).then_inc(s_si, 1)
                    at_least(DV, s_si, 2 * g + t + 1)
                    at_least(DV, s_tr, g)
                    V.scalar_tensor_tensor(HB[:, t, :], SG[:, t, :], 1.0,
                                           bank[4 + t][:, HCH:CH], ALU.mult, ALU.mult).then_inc(s_ev, 1)
                for t in range(NT):
                    at_least(PE, s_ev, 2 * s + t + 1)
                    at_least(PE, s_htl, g)
                    for k in range(2):
                        tr = T.transpose(bank[6][:, k * SEQ + t * P:k * SEQ + (t + 1) * P],
                                         HB[:, t, k * P:(k + 1) * P], ident[:, :])
                tr.then_inc(s_tr, 1)
                at_least(AC, s_ldd, 16 * (g + 1))
                at_least(AC, s_dn, g)
                K.copy(dh[:, :, :], rawd[:, :, :]).then_inc(s_hid, 1)
                at_least(DV, s_hid, g + 1)
                V.tensor_tensor(dl[:, :, :], rawd[:, :, :], dh[:, :, :].bitcast(F32), ALU.subtract).then_inc(s_lod, 1)
                at_least(AC, s_tr, g + 1)
                K.copy(hh[:, :, :], halves(6)).then_inc(s_hth, 1)
                at_least(DV, s_hth, g + 1)
                V.tensor_tensor(hl[:, :, :], halves(6), hh[:, :, :].bitcast(F32), ALU.subtract).then_inc(s_htl, 1)
                if more:
                    load_down(i + 1)

            AC.eng.preload_act_table(ACT.Silu)
            slot(0, 0, first=True)
            pairs = (n - 2) // 2
            with nc.Fori(0, pairs) as r:
                for j in range(2):
                    slot(r * 2 + (1 + j), 1 + j)
            forget()
            for i in range(1 + 2 * pairs, n):
                slot(i, i, cut_next=not (last and i == n - 1), more=i < n - 1)
            first = down(g0 + n - 1, stop=True)
            c.step += n
            c.ff += n
            return [first, (s_dn, c.ff)]

        def rsqrt(dst, src, after=()):
            return PO.run(Q.tensor_tensor, dst, src, mhalf[:, 0:src.shape[1]], ALU.pow, after=after)

        def norm_rows(g, b, after):
            return small_loads([(GR, g.partition_broadcast(P)), (BR, b.partition_broadcast(P))], after=after)

        def row_stats(t, m, after=()):
            DV.run(V.bn_stats, st[:, t, m, :], U[:, t, m * CH:(m + 1) * CH], after=after)

        def layer_norm(rows, after=()):
            DV.wait(*after)
            for t in range(NT):
                DV.run(V.bn_aggr, mv[:, t, :], st[:, t, :, :].rearrange("p a b -> p (a b)"))
                e = DV.run(V.tensor_scalar, ss[:, t:t + 1], mv[:, t, 1:2], 1e-5, None, ALU.add)
                r = rsqrt(rs[:, t:t + 1], ss[:, t:t + 1], after=[e])
                DV.run(V.tensor_scalar, H[:, t, :], U[:, t, :], mv[:, t, 0:1], rs[:, t:t + 1],
                       ALU.subtract, ALU.mult, after=[r])
                yield
                DV.run(V.tensor_tensor, H[:, t, :], H[:, t, :], GR, ALU.mult, after=[rows])
                DV.run(V.tensor_tensor, H[:, t, :], H[:, t, :], BR, ALU.add)
                yield

        def norm_and_turn(rows, after, turned=True):
            DV.wait(*after)
            for t in range(NT):
                DV.run(V.bn_aggr, mv[:, t, :], st[:, t, :, :].rearrange("p a b -> p (a b)"))
                e = DV.run(V.tensor_scalar, ss[:, t:t + 1], mv[:, t, 1:2], 1e-5, None, ALU.add)
            f = rsqrt(rs[:, 0:NT], ss[:, 0:NT], after=[e])
            for t in range(NT):
                shift = DV.run(V.scalar_tensor_tensor, ss[:, 2 + t:3 + t], mv[:, t, 0:1], -1.0, rs[:, t:t + 1],
                               ALU.mult, ALU.mult, after=[f])

            def prepare(r):
                cs = slice(2 * r * P, (2 * r + 2) * P)
                for t in range(NT):
                    a = AC.run(K.activation, H[:, t, cs], U[:, t, cs], ACT.Identity, bias=ss[:, 2 + t:3 + t],
                               scale=rs[:, t:t + 1], after=[shift])
                x = H[:, :, cs]
                DV.run(V.tensor_tensor, x, x, GR[:, cs].unsqueeze(1).to_broadcast([P, NT, 2 * P]), ALU.mult,
                       after=[a, rows])
                return [DV.run(V.tensor_tensor, x, x, BR[:, cs].unsqueeze(1).to_broadcast([P, NT, 2 * P]), ALU.add)]
            if turned:
                return turn(H, after=after, prepare=prepare)
            for r in range(KT // 2):
                done = prepare(r)
            return done

        def rms_and_turn(gain, after):
            AC.wait(*after)
            DV.wait(*after)
            for t in range(NT):
                q = AC.run(K.activation, S[:, t * D:(t + 1) * D], H[:, t, :], ACT.Square, accum_out=ss[:, t:t + 1])
            e = DV.run(V.tensor_scalar, ss[:, 0:NT], ss[:, 0:NT], 1.0 / D, 1e-6, ALU.mult, ALU.add, after=[q])
            f = rsqrt(rs[:, 0:NT], ss[:, 0:NT], after=[e])

            def prepare(r):
                cs = slice(2 * r * P, (2 * r + 2) * P)
                return [DV.run(V.tensor_scalar, U[:, 0, cs], H[:, 0, cs], rs[:, 0:1], None, ALU.mult, after=[f]),
                        AC.run(K.activation, U[:, 1, cs], H[:, 1, cs], ACT.Copy, scale=rs[:, 1:2], after=[f])]
            return turn(U, gain=gain, after=after, prepare=prepare)

        def rms_rows(x, y, width, eps, col, after=()):
            DV.run(V.tensor_tensor_reduce, S[:, 0:width], x, x, 1.0, 0.0, ALU.mult, ALU.add,
                   ss[:, col:col + 1], after=after)
            e = DV.run(V.tensor_scalar, ss[:, col:col + 1], ss[:, col:col + 1], 1.0 / width, eps, ALU.mult, ALU.add)
            r = rsqrt(rs[:, col:col + 1], ss[:, col:col + 1], after=[e])
            return DV.run(V.tensor_scalar, y, x, rs[:, col:col + 1], None, ALU.mult, after=[r])

        def head_norm(c0, heads, gains):
            n = NT * heads
            for t in range(NT):
                x = Z[:, t, c0:c0 + heads * HD]
                sq = S[:, 0:heads * HD]
                DV.run(V.tensor_tensor, sq, x, x, ALU.mult)
                DV.run(V.tensor_reduce, ss[:, t * heads:(t + 1) * heads], sq.rearrange("p (h d) -> p h d", d=HD),
                       AX.X, ALU.add)
            e = DV.run(V.tensor_scalar, ss[:, 0:n], ss[:, 0:n], 1.0 / HD, 1e-6, ALU.mult, ALU.add)
            r = rsqrt(rs[:, 0:n], ss[:, 0:n], after=[e])
            yield
            for t in range(NT):
                x = Z[:, t, c0:c0 + heads * HD].rearrange("p (h d) -> p h d", d=HD)
                f = rs[:, t * heads:(t + 1) * heads].unsqueeze(2).to_broadcast([P, heads, HD])
                DV.run(V.tensor_tensor, x, x, f, ALU.mult, after=[r])
                for h0, nh, row in gains:
                    y = x[:, h0:h0 + nh, :]
                    DV.run(V.tensor_tensor, y, y, row.unsqueeze(1).to_broadcast([P, nh, HD]), ALU.mult)

        def rotate(x, heads, half, table):
            a = S[:, 0:heads * 2 * half].rearrange("p (h d) -> p h d", h=heads)
            b = S[:, 1024:1024 + heads * 2 * half].rearrange("p (h d) -> p h d", h=heads)
            cc = table[:, 0, :].unsqueeze(1).to_broadcast([P, heads, 2 * half])
            s1 = table[:, 1, 0:half].unsqueeze(1).to_broadcast([P, heads, half])
            s2 = table[:, 1, half:2 * half].unsqueeze(1).to_broadcast([P, heads, half])
            DV.run(V.tensor_tensor, a, x[:, :, 0:2 * half], cc, ALU.mult)
            DV.run(V.tensor_tensor, b[:, :, 0:half], x[:, :, half:2 * half], s1, ALU.mult)
            DV.run(V.tensor_tensor, b[:, :, half:2 * half], x[:, :, 0:half], s2, ALU.mult)
            return DV.run(V.tensor_tensor, x[:, :, 0:2 * half], a, b, ALU.add)

        def heads3(x, c0, heads, d=HD):
            return x[:, c0:c0 + heads * d].rearrange("p (h d) -> p h d", d=d)

        def attention(heads, after, beside=()):
            for e in (PE, DV, AC):
                e.wait(*after)
            n = len(heads)
            lag = 1 if heads[0]["nk"] == 2 else 2

            def qk_at(h, k):
                return (h % 2, k) if lag == 1 else (h % 3 // 2, h % 3 % 2)
            low = []
            qkc, sc, ex, rc, ptc, ov, of = {}, {}, {}, {}, {}, {}, {}

            def turn_qk(h):
                d = heads[h]
                for k in range(d["nk"]):
                    b = 6 + (h + k) % 2
                    PE.wait(qkc.get(h - 1 if d["nk"] == 2 else h - 2))
                    if d["nk"] == 2 and k == 0:
                        PE.wait(qkc.get(h - 1))
                    dk = d["dk"]
                    for j in range(2):
                        for t in range(NT):
                            i = T.transpose(bank[b][0:dk, (2 * j + t) * P:(2 * j + t + 1) * P],
                                            (d["q"], d["k"])[j](t, k), ident[:, :])
                    turned = PE.mark(i)
                    at_ = (slice(0, dk),) + qk_at(h, k)
                    free = sc.get(h - 1 - lag)
                    cut_ = AC.run(K.copy, QKH[at_], bank[b][0:dk, :], after=[turned, free])
                    low.append((h, V.tensor_tensor, QKL[at_], bank[b][0:dk, :], QKH[at_].bitcast(F32),
                                [cut_, free]))

            def cut_low():
                for h, op, dst, src, hi, wait in low:
                    qkc[h] = DV.run(op, dst, src, hi, ALU.subtract, after=wait)
                low.clear()

            def score(h):
                d, b = heads[h], h % 2
                dk = d["dk"]
                PE.wait(qkc[h], ex.get(h - 2), rc.get(("m", h - 2)))
                for t in range(NT):
                    for k in range(d["nk"]):
                        at_ = (slice(0, dk),) + qk_at(h, k)
                        qk, kk = ([x[at_][:, c0:c0 + SEQ] for x in (QKH, QKL)] for c0 in (0, SEQ))
                        i = three(halves(b)[:, t, :], qk, kk, t, k == 0, k == d["nk"] - 1)
                sc[h] = PE.mark(i)
                x, f = halves(b), d["scale"]
                if d["bias"] is not None:
                    for t in range(NT):
                        DV.run(V.scalar_tensor_tensor, SM[:, b, t, :], halves(b)[:, t, :], f, d["bias"][:, t, :],
                               ALU.mult, ALU.add, after=[sc[h], ex.get(h - 2)])
                    x, f = SM[:, b, :, :], 1.0
                mx = ss[:, 4 * b:4 * b + 2]
                DV.run(V.tensor_reduce, mx, x, AX.X, ALU.max, after=[sc[h]])
                rc[("m", h)] = DV.run(V.tensor_scalar, rs[:, 4 * b:4 * b + 2], mx, -f, None, ALU.mult,
                                      after=[ex.get(h - 2)])
                c4 = 8 + 2 * (h % 4)
                for t in range(NT):
                    ex[h] = AC.run(K.activation, PR[:, b, t, :], x[:, t, :], ACT.Exp,
                                   bias=rs[:, 4 * b + t:4 * b + t + 1], scale=f,
                                   accum_out=ss[:, c4 + t:c4 + t + 1],
                                   after=[rc[("m", h)], ptc.get(("pe", h - 2)), rc.get(h - 4)])

            def turn_p(h):
                b = h % 2
                PE.wait(ex[h], ptc.get(h - 2))
                for k in range(NT):
                    for t in range(NT):
                        i = T.transpose(halves(2 + b)[:, k, t * P:(t + 1) * P], PR[:, b, t, k * P:(k + 1) * P],
                                        ident[:, :])
                ptc[("pe", h)] = PE.mark(i)
                ptc[h] = AC.run(K.copy, PT[:, b, :, :], halves(2 + b), after=[ptc[("pe", h)], ov.get(h - 2)])

            def value(h):
                d, b = heads[h], h % 2
                dv = d["dv"]
                PE.wait(ptc[h], of.get(h - 2))
                for t in range(NT):
                    for k in range(NT):
                        i = T.matmul(halves(4 + b)[:, t, 0:dv], PT[:, b, k, t * P:(t + 1) * P], d["v"](k),
                                     start=k == 0, stop=k == 1)
                ov[h] = PE.mark(i)
                c4 = 8 + 2 * (h % 4)
                rc[h] = DV.run(V.reciprocal, rs[:, c4:c4 + 2], ss[:, c4:c4 + 2], after=[ex[h]])
                for t in range(NT):
                    r = rs[:, c4 + t:c4 + t + 1]
                    if d["weight"] is None:
                        of[h] = DV.run(V.tensor_scalar, d["out"](t), halves(4 + b)[:, t, 0:dv], r, None, ALU.mult,
                                       after=[ov[h]])
                    else:
                        DV.run(V.tensor_tensor, r, r, d["weight"], ALU.mult)
                        of[h] = DV.run(V.scalar_tensor_tensor, d["out"](t), halves(4 + b)[:, t, 0:dv], r,
                                       d["out"](t), ALU.mult, ALU.add, after=[ov[h]])

            for i in range(n + lag + 3):
                if i < n:
                    turn_qk(i)
                if lag == 1:
                    cut_low()
                if 0 <= i - lag - 2 < n:
                    turn_p(i - lag - 2)
                if 0 <= i - lag < n:
                    score(i - lag)
                if 0 <= i - lag - 3 < n:
                    value(i - lag - 3)
                cut_low()
                if beside:
                    next(beside, None)
            return DV.last()

        def head(q, k, v, out_, scale, dk=HD, dv=HD, nk=1, bias=None, weight=None):
            return dict(q=q, k=k, v=v, out=out_, scale=scale, dk=dk, dv=dv, nk=nk, bias=bias, weight=weight)

        def zc(c0, w=HD):
            return lambda t, k=0: Z[:, t, c0 + k * w:c0 + (k + 1) * w]

        def uc(c0, w=HD):
            return lambda t: U[:, t, c0:c0 + w]

        def to_tokens(dst, widths=None):
            def evac(i, t, done):
                w = widths[i] if widths and isinstance(i, int) else CH
                at_least(DV, *done)
                V.tensor_copy(dst[:, t, bass.ds(i * CH, w)], bank[4 + t][:, 0:w]).then_inc(s_ev, 1)
            return evac

        def to_gates(i, t, done):
            at_least(AC, *done)
            K.activation(G[:, t, bass.ds(i * CH, CH)], bank[4 + t][:, :], ACT.Sigmoid).then_inc(s_ev, 1)

        def add_residual(i, t, done):
            at_least(DV, *done)
            V.scalar_tensor_tensor(U[:, t, i * CH:(i + 1) * CH], H[:, t, i * CH:(i + 1) * CH], ALPHA,
                                   bank[4 + t][:, :], ALU.mult, ALU.add).then_inc(s_ev, 1)
            row_stats(t, i, after=[(s_ev, done[1])])

        def add_to_h(i, t, done):
            at_least(DV, *done)
            V.tensor_tensor(H[:, t, i * CH:(i + 1) * CH], H[:, t, i * CH:(i + 1) * CH], bank[4 + t][:, :],
                            ALU.add).then_inc(s_ev, 1)

        def merge(i, t, done):
            at_least(DV, *done)
            cs = slice(i * CH, (i + 1) * CH)
            tmp = S[:, 2 * D:2 * D + CH]
            DV.run(V.tensor_tensor, U[:, t, cs], bank[3 * t][:, :], G[:, t, cs], ALU.mult)
            for b in (1, 2):
                DV.run(V.tensor_tensor, tmp, bank[3 * t + b][:, :], G[:, t, b * D + i * CH:b * D + (i + 1) * CH],
                       ALU.mult)
                if b == 1:
                    DV.run(V.tensor_tensor, U[:, t, cs], U[:, t, cs], tmp, ALU.add)
            DV.wait(DV.last())
            V.tensor_tensor(U[:, t, cs], U[:, t, cs], tmp, ALU.add).then_inc(s_ev, 1)

        def all_idle():
            return [e.last() for e in (PE, AC, DV, PO)] + [products_read()]

        def store_and_end(src):
            SP.wait(*all_idle())
            o = out.rearrange("a (t p) n -> p (a t) n", p=P)
            Y.dma_start(o, src).then_inc(s_out, 16)
            Y.wait_ge(s_out, 16)

        at_z, at_g = z_offset, g_offset

        def over(name, shape, offset):
            return nc.alloc_sbuf_tensor_at(name, shape, F32R, offset=offset)
        HH = over("tokens_hi", [P, NT, D], at_z)
        HL = over("tokens_lo", [P, NT, D], at_z + 4 * NT * D)
        SEL_R = over("gather", [P, 2, NT, P], at_z + 8 * NT * D)
        SEL_T = over("scatter", [P, 2, SEQ], at_z + 8 * NT * D + 2048)
        YH = over("expert_out_hi", [P, D], at_g)
        YL = over("expert_out_lo", [P, D], at_g + 4 * D)
        Gf = G[:, :, :].rearrange("p t n -> p (t n)")
        rawg2 = Gf[:, 2 * D:2 * D + KT * CH].rearrange("p (k n) -> p k n", n=CH)
        rawd2 = S[:, 3072:5120].rearrange("p (k n) -> p k n", n=D)
        RAWG, RAWD = (rawg, rawg2), (rawd, rawd2)
        before, ones = (ropeb[:, t, :, :].rearrange("p a b -> p (a b)") for t in range(NT))
        slot_no = ropec[:, :, :, :].rearrange("p t a b -> p (t a b)")
        ranks = pb[:, 256:272]
        rank = ranks.rearrange("p (t e) -> p t e", t=NT)
        chose = pb[:, 272:288].rearrange("p (t e) -> p t e", t=NT)
        g8 = pb[:, 288:304].rearrange("p (t e) -> p t e", t=NT)
        gslot = pb[:, 304:306]
        total, many = pb[:, 312:320], pb[:, 320:321]

        def router_loads(m, after):
            return small_loads([(rw[:, :, :], A["moe_router"][m].rearrange("(k p) e -> p k e", p=P)),
                                (before, C["before"]), (ones, C["ones"]), (slot_no, C["slots"])], after=after)

        def route(w):
            DV.run(V.tensor_copy, rh[:, :, :], rw[:, :, :], after=[w])
            DV.run(V.tensor_tensor, rl[:, :, :], rw[:, :, :], rh[:, :, :].bitcast(F32), ALU.subtract)
            PE.wait(DV.last())
            for t in range(NT):
                for k in range(KT):
                    i = three(bank[7][:, t * 8:(t + 1) * 8], (xh[:, k, :], xl[:, k, :]), (rh[:, k, :], rl[:, k, :]), t,
                              k == 0, k == KT - 1)
            scored = PE.mark(i)
            for t in range(NT):
                hi = AC.run(K.copy, HH[:, t, :], H[:, t, :])
                DV.run(V.tensor_scalar, U[:, t, :], H[:, t, :], ALPHA, None, ALU.mult)
                DV.run(V.tensor_tensor, HL[:, t, :], H[:, t, :], HH[:, t, :].bitcast(F32), ALU.subtract, after=[hi])
            L, top, idx, num, e, g2 = (lg[:, j, :] for j in range(6))
            for t in range(NT):
                g = g8[:, t, :]
                DV.run(V.tensor_copy, L, bank[7][:, t * 8:(t + 1) * 8], after=[scored])
                DV.run(V.max, top, L)
                DV.run(V.max_index, idx.bitcast(U32), top, L)
                DV.run(V.tensor_copy, num, idx.bitcast(U32))
                d = DV.run(V.tensor_tensor, e[:, 0:1], top[:, 1:2], top[:, 0:1], ALU.subtract)
                x = AC.run(K.activation, e[:, 1:2], e[:, 0:1], ACT.Exp, after=[d])
                DV.run(V.tensor_scalar, e[:, 2:3], e[:, 1:2], 1.0, None, ALU.add, after=[x])
                DV.run(V.reciprocal, e[:, 3:4], e[:, 2:3])
                DV.run(V.tensor_tensor, e[:, 4:5], e[:, 1:2], e[:, 3:4], ALU.mult)
                DV.run(V.tensor_scalar, g, iota[:, :], num[:, 0:1], e[:, 3:4], ALU.is_equal, ALU.mult)
                DV.run(V.tensor_scalar, g2, iota[:, :], num[:, 1:2], e[:, 4:5], ALU.is_equal, ALU.mult)
                DV.run(V.tensor_tensor, g, g, g2, ALU.add)
                DV.run(V.tensor_scalar, chose[:, t, :], iota[:, :], num[:, 0:1], None, ALU.is_equal)
                DV.run(V.tensor_scalar, g2, iota[:, :], num[:, 1:2], None, ALU.is_equal)
                DV.run(V.tensor_tensor, chose[:, t, :], chose[:, t, :], g2, ALU.add)
            PE.wait(DV.last())
            T.matmul(bank[7][:, 0:8], before, chose[:, 0, :], start=True, stop=True)
            T.matmul(bank[7][:, 8:16], ones, chose[:, 0, :], start=True, stop=False)
            T.matmul(bank[7][:, 8:16], before, chose[:, 1, :], start=False, stop=True)
            T.matmul(bank[7][:, 16:24], ones, chose[:, 0, :], start=True, stop=False)
            i = T.matmul(bank[7][:, 16:24], ones, chose[:, 1, :], start=False, stop=True)
            ranked = PE.mark(i)
            DV.run(V.tensor_copy, ranks, bank[7][:, 0:16], after=[ranked])
            DV.run(V.tensor_copy, total, bank[7][:, 16:24])
            DV.run(V.tensor_reduce, many, total, AX.X, ALU.max)
            DV.run(V.tensor_scalar, many, many, P + 0.5, None, ALU.is_gt)
            DV.run(V.tensor_copy, flag[:, :], many)

        names = ["ld00", "ld01", "ld10", "ld11", "ldd0", "ldd1", "hi", "lo", "hid", "lod", "mm", "ev", "si", "tr", "hth", "htl", "dn", "sel", "ga", "xhi",
                 "xlo", "tp", "st", "gs", "yh", "yl", "sc", "ua"]
        passes = [{x: sem(f"moe{q}_{x}") for x in names} for q in range(2)]

        def at(eng, s, value):
            if not isinstance(value, int) or value > 0:
                eng.wait_ge(s, value)

        def moe_loads(q, wgu):
            def load(e, j, f, fp):
                n = e * NFF + f
                par = (j + fp) % 2
                for u in range(2):
                    at(Y, q["lo"], 2 * n - 3 + u)
                    for m in range(2):
                        Y.dma_start(RAWG[par][:, 4 * u:4 * u + 4, m * HCH:(m + 1) * HCH],
                                    wgu[e].rearrange("(k p) n -> p k n", p=P)[:, 4 * u:4 * u + 4,
                                                                              bass.ds(f * HCH + m * DFF, HCH)]
                                    ).then_inc(q[f"ld{par}{u}"], 16)

            def expert(e, j):
                load(e, j, 0, 0)
                if isinstance(e, int) and e == 0:
                    load(e, j, 1, 1)
                    load(e, j, 2, 2)
                with nc.sync.Fori(1 if isinstance(e, int) and e == 0 else 0, NFF // 2) as r:
                    for fp in (1, 2):
                        load(e, j, r * 2 + fp, fp)
            expert(0, 0)
            expert(1, 1)
            with nc.sync.Fori(1, EXPERTS // 2) as r:
                for j in range(2):
                    expert(r * 2 + j, j)
            SP.seen.clear()

        def moe_pass(q, wd, start):
            s = q

            def load_down(n, par):
                at(K, s["lod"], n - 1)
                K.dma_start(RAWD[par][:, :, :], wd[bass.ds(n * HCH, HCH), :].rearrange("(k p) n -> p k n", p=P)
                            ).then_inc(s[f"ldd{par}"], 16)

            def cut_up(n, par):
                for u in range(2):
                    src, hi, lo = (x[:, 4 * u:4 * u + 4, :] for x in (RAWG[par], wh[:, par, :, :], wl[:, par, :, :]))
                    at(K, s[f"ld{par}{u}"], 16 * (n - par) + 32)
                    at(K, s["mm"], n - 1)
                    K.copy(hi, src).then_inc(s["hi"], 1)
                    at(V, s["hi"], 2 * n + u + 1)
                    V.tensor_tensor(lo, src, hi.bitcast(F32), ALU.subtract).then_inc(s["lo"], 1)

            def down_products(n, par, j):
                at(T, s["lod"], n + 1)
                at(T, s["htl"], n + 1)
                tok = slice(par * P, (par + 1) * P)
                for k in range(2):
                    for xx, ww in ((hh, dh), (hh, dl), (hl, dh)):
                        for m in range(2):
                            mm = T.matmul(bank[2 * j + m][:, :], xx[:, k, tok], ww[:, k, m * CH:(m + 1) * CH],
                                          start=False, stop=False, skip_group_check=True)
                mm.then_inc(s["dn"], 1)

            def slot(e, j, f, fp, prev, cut_next=True, between=(), after=()):
                n = e * NFF + f
                par = (j + fp) % 2
                if cut_next:
                    cut_up(n + 1, 1 - par)
                if fp == 0:
                    at(T, s["xlo"], 2 * e + 2)
                at(T, s["ev"], n - 1)
                for k in range(KT):
                    if k % 4 == 0:
                        at(T, s["lo"], 2 * n + k // 4 + 1)
                    mm = three(bank[4 + par][:, :], (xh[:, k, :], xl[:, k, :]), (wh[:, par, k, :], wl[:, par, k, :]), j,
                               k == 0, k == KT - 1)
                mm.then_inc(s["mm"], 1)
                if prev is not None:
                    down_products(n - 1, 1 - par, prev)
                for piece in between:
                    piece()
                at(K, s["mm"], n + 1)
                at(K, s["ev"], n - 1)
                K.activation(SG[:, par, :], bank[4 + par][:, 0:HCH], ACT.Silu).then_inc(s["si"], 1)
                at(V, s["si"], n + 1)
                at(V, s["tr"], n - 1)
                if fp == 0:
                    at(V, s["gs"], e + 1)
                V.scalar_tensor_tensor(HB[:, par, :], SG[:, par, :], gslot[:, j:j + 1], bank[4 + par][:, HCH:CH],
                                       ALU.mult, ALU.mult).then_inc(s["ev"], 1)
                at(T, s["ev"], n + 1)
                at(T, s["htl"], n)
                for k in range(2):
                    tr = T.transpose(bank[6][:, k * P:(k + 1) * P], HB[:, par, k * P:(k + 1) * P], ident[:, :])
                tr.then_inc(s["tr"], 1)
                at(K, s[f"ldd{par}"], 8 * (n - par) + 16)
                at(K, s["dn"], n)
                K.copy(dh[:, :, :], RAWD[par][:, :, :]).then_inc(s["hid"], 1)
                at(V, s["hid"], n + 1)
                V.tensor_tensor(dl[:, :, :], RAWD[par][:, :, :], dh[:, :, :].bitcast(F32), ALU.subtract
                                ).then_inc(s["lod"], 1)
                tok = slice(par * P, (par + 1) * P)
                src = bank[6][:, 0:2 * P].rearrange("p (k n) -> p k n", k=2)
                at(K, s["tr"], n + 1)
                K.copy(hh[:, :, tok], src).then_inc(s["hth"], 1)
                at(V, s["hth"], n + 1)
                V.tensor_tensor(hl[:, :, tok], src, hh[:, :, tok].bitcast(F32), ALU.subtract).then_inc(s["htl"], 1)
                for piece in after:
                    piece()
                if cut_next:
                    load_down(n + 1, 1 - par)

            def choose(e, j):
                at(V, s["tp"], e - 1)
                for t in range(NT):
                    i = V.tensor_scalar(SEL_R[:, j, t, :], slot_no, rank[:, t, bass.ds(e, 1)], chose[:, t, bass.ds(e, 1)],
                                        ALU.is_equal, ALU.mult)
                i.then_inc(s["sel"], 1)

            def gather(e, j, h):
                at(T, s["sel"], e + 1)
                at(T, s["gs"], e)
                at(T, s["xlo"], 2 * e + h)
                for kk in range(4):
                    ks = slice((4 * h + kk) * P, (4 * h + kk + 1) * P)
                    for t in range(NT):
                        for x in (HH, HL):
                            i = T.matmul(bank[7][:, kk * P:(kk + 1) * P], x[:, t, ks], SEL_R[:, j, t, :],
                                         start=t == 0 and x is HH, stop=t == 1 and x is HL)
                i.then_inc(s["ga"], 1)

            def cut_gathered(e, j, h):
                src = bank[7][:, :].rearrange("p (k n) -> p k n", n=P)
                xs = (slice(None), slice(4 * h, 4 * h + 4), slice(j * P, (j + 1) * P))
                at(K, s["ga"], 2 * e + h + 1)
                K.copy(xh[xs], src).then_inc(s["xhi"], 1)
                at(V, s["xhi"], 2 * e + h + 1)
                V.tensor_tensor(xl[xs], src, xh[xs].bitcast(F32), ALU.subtract).then_inc(s["xlo"], 1)

            def turn_choice(e, j):
                at(T, s["xlo"], 2 * e + 2)
                for t in range(NT):
                    T.transpose(bank[7][:, t * P:(t + 1) * P], SEL_R[:, j, t, :].bitcast(F32), ident[:, :])
                for t in range(NT):
                    i = T.matmul(bank[7][:, SEQ:SEQ + 1], SEL_R[:, j, t, :].bitcast(F32), g8[:, t, bass.ds(e, 1)],
                                 start=t == 0, stop=t == 1)
                i.then_inc(s["tp"], 1)

            def keep_choice(e, j):
                at(K, s["tp"], e + 1)
                at(K, s["sc"], 2 * e - 2)
                K.copy(SEL_T[:, j, :], bank[7][:, 0:SEQ]).then_inc(s["st"], 1)
                at(V, s["st"], e + 1)
                V.tensor_copy(gslot[:, j:j + 1], bank[7][:, SEQ:SEQ + 1]).then_inc(s["gs"], 1)

            def open_sums(e, j):
                at(T, s["ua"], 2 * e - 2)
                for m in range(2):
                    T.matmul(bank[2 * j + m][:, :], zb[:, 0:P], zb[:, :], start=True, stop=False,
                             skip_group_check=True)

            def cut_sums(e, j):
                for m in range(2):
                    cs = slice(m * CH, (m + 1) * CH)
                    at(K, s["dn"], e * NFF + NFF)
                    at(K, s["sc"], 2 * e)
                    K.copy(YH[:, cs], bank[2 * j + m][:, :]).then_inc(s["yh"], 1)
                    at(V, s["yh"], 2 * e + m + 1)
                    V.tensor_tensor(YL[:, cs], bank[2 * j + m][:, :], YH[:, cs].bitcast(F32), ALU.subtract
                                    ).then_inc(s["yl"], 1)

            def scatter(e, j, t):
                at(T, s["yl"], 2 * e + 2)
                at(T, s["st"], e + 1)
                at(T, s["ua"], 2 * e + t)
                for m in range(2):
                    cs = slice(m * CH, (m + 1) * CH)
                    T.matmul(bank[2 * j + m][:, :], SEL_T[:, j, t * P:(t + 1) * P], YH[:, cs], start=True, stop=False)
                    i = T.matmul(bank[2 * j + m][:, :], SEL_T[:, j, t * P:(t + 1) * P], YL[:, cs], start=False, stop=True)
                i.then_inc(s["sc"], 1)

            def add(e, j, t):
                at(V, s["sc"], 2 * e + t + 1)
                at(V, s["ua"], 2 * e + t)
                for m in range(2):
                    cs = slice(m * CH, (m + 1) * CH)
                    i = V.tensor_tensor(U[:, t, cs], U[:, t, cs], bank[2 * j + m][:, :], ALU.add)
                i.then_inc(s["ua"], 1)

            def expert(e, j, first=False, last=False):
                b, a = ([[] for _ in range(4)] for _ in range(2))
                k = 1 - j
                if not first:
                    a[0].append(lambda: cut_sums(e - 1, k))
                    for t in range(NT):
                        b[1 + t].append(lambda t=t: scatter(e - 1, k, t))
                        a[1 + t].append(lambda t=t: add(e - 1, k, t))
                if not last:
                    a[0].append(lambda: choose(e + 1, k))
                    for h in range(2):
                        b[1 + h].append(lambda h=h: gather(e + 1, k, h))
                        a[1 + h].append(lambda h=h: cut_gathered(e + 1, k, h))
                    b[3].append(lambda: turn_choice(e + 1, k))
                    a[3].append(lambda: keep_choice(e + 1, k))
                slot(e, j, 0, 0, None if first else k, after=a[0])
                open_sums(e, j)
                for f in (1, 2, 3):
                    slot(e, j, f, f, j, between=b[f], after=a[f])
                slot(e, j, 4, 4, j)
                with nc.Fori(2, NFF // 2 - (1 if last else 0)) as r:
                    for fp in (1, 2):
                        slot(e, j, r * 2 + fp, fp, j)
                if last:
                    slot(e, j, NFF - 2, 1, j)
                    slot(e, j, NFF - 1, 2, j, cut_next=False)

            load_down(0, 0)
            cut_up(0, 0)
            start()
            K.preload_act_table(ACT.Silu)
            choose(0, 0)
            for h in range(2):
                gather(0, 0, h)
                cut_gathered(0, 0, h)
            turn_choice(0, 0)
            keep_choice(0, 0)
            expert(0, 0, first=True)
            expert(1, 1)
            with nc.Fori(1, EXPERTS // 2 - 1) as r:
                for j in range(2):
                    expert(r * 2 + j, j)
            expert(EXPERTS - 2, 0)
            expert(EXPERTS - 1, 1, last=True)
            down_products(EXPERTS * NFF - 1, (EXPERTS * NFF - 1) % 2, 1)
            cut_sums(EXPERTS - 1, 1)
            for t in range(NT):
                scatter(EXPERTS - 1, 1, t)
                add(EXPERTS - 1, 1, t)

        def moe(m, g_free, router):
            wgu = A["moe_w_gu"][m]
            wd = A["moe_w_down"][m].rearrange("e f n -> (e f) n")
            everything = [(s, v) for q in passes for s, v in ((q["ua"], 2 * EXPERTS), (q["dn"], EXPERTS * NFF))]
            SP.wait((s_lo, 2 * c.loads), *g_free)
            moe_loads(passes[0], wgu)
            for e in (PE, DV, AC):
                e.wait(*all_idle())

            def first_start():
                route(router)
                for e in (PE, DV, AC):
                    e.wait(*all_idle())
            moe_pass(passes[0], wd, first_start)
            for e in (PE, DV, AC, SP, PO):
                for x, v in everything[:2]:
                    e.eng.wait_ge(x, v)
                e.wait(*all_idle())
            again = nc.values_load(flag[0:1, 0:1], min_val=0, max_val=1)
            with nc.If(again > 0):
                V.tensor_scalar(ranks, ranks, -float(P), None, ALU.add).then_inc(s_again, 1)
                for e in (V, T, K, Y, Q):
                    e.wait_ge(s_again, 1)
                moe_loads(passes[1], wgu)
                moe_pass(passes[1], wd, lambda: None)
                for e in (PE, DV, AC, SP, PO):
                    for x, v in everything[2:]:
                        e.eng.wait_ge(x, v)
            forget()

        def angles():
            load = small_loads([(pos[:, :], A["positions_2"].rearrange("a (t p) -> p (a t)", p=P)),
                                (invf[:, :], C["inv_freq"])], after=[DV.last()])
            n = NT * ROT2 // 2
            x, k, y, z = (S[:, 1700 + j * n:1700 + (j + 1) * n] for j in range(4))
            pf = lam[:, 0:NT]
            two_pi = 2 * np.pi
            c1 = 6.28125
            c2 = float(np.round((two_pi - c1) * 2 ** 20) / 2 ** 20)
            c3 = float(two_pi - c1 - c2)
            magic = 1.5 * 2.0 ** 23
            DV.run(V.tensor_copy, pf, pos[:, :], after=[load])
            for t in range(NT):
                DV.run(V.tensor_scalar, x[:, t * 8:(t + 1) * 8], invf[:, :], pf[:, t:t + 1], None, ALU.mult)
            DV.run(V.tensor_scalar, k, x, 1.0 / two_pi, magic, ALU.mult, ALU.add)
            DV.run(V.tensor_scalar, k, k, -magic, None, ALU.add)
            for part in (c1, c2, c3):
                DV.run(V.scalar_tensor_tensor, x, k, -part, x, ALU.mult, ALU.add)
            DV.run(V.tensor_scalar, y, x, float(np.pi / 2), None, ALU.add)
            DV.run(V.tensor_scalar, z, y, float(np.pi), None, ALU.is_gt)
            DV.run(V.scalar_tensor_tensor, y, z, -two_pi, y, ALU.mult, ALU.add)
            lim = 3.1415925
            for v in (x, y):
                DV.run(V.tensor_scalar, v, v, lim, -lim, ALU.min, ALU.max)
            AC.run(K.activation, k, x, ACT.Sin, after=[DV.last()])
            sc_ = AC.run(K.activation, z, y, ACT.Sin)
            for t in range(NT):
                sn, cs = k[:, t * 8:(t + 1) * 8], z[:, t * 8:(t + 1) * 8]
                DV.run(V.tensor_copy, rope2[:, t, 0, 0:8], cs, after=[sc_])
                DV.run(V.tensor_copy, rope2[:, t, 0, 8:16], cs)
                DV.run(V.tensor_scalar, rope2[:, t, 1, 0:8], sn, -1.0, None, ALU.mult)
                DV.run(V.tensor_copy, rope2[:, t, 1, 8:16], sn)

        def half_ffn_loads(l, j):
            ffn_all_loads(A["ffn_w_gate_2"][l, j], A["ffn_w_up_2"][l, j])

        def half_ffn(l, j, last=False):
            PE.wait(rms_and_turn(cols[:, (3 * l + 2 * j) * KT:(3 * l + 2 * j + 1) * KT], all_idle()))
            done = ffn(NFF, A["ffn_w_down_2"][l, j], after=all_idle(), last=last)
            for t in range(NT):
                for m in range(2):
                    cs = slice(m * CH, (m + 1) * CH)
                    DV.run(V.scalar_tensor_tensor, H[:, t, cs], bank[2 * t + m][:, :], 0.5, H[:, t, cs],
                           ALU.mult, ALU.add, after=[done[t]])

        def score_keys():
            for e in (PE, DV, AC):
                e.wait(*all_idle())
            turned, scored, relu, used = {}, {}, {}, {}
            DV.run(V.tensor_copy, ISC[:, :, :], cmask[:, :, :])
            for i in range(IDX_HEADS + 1):
                if i < IDX_HEADS:
                    PE.wait(turned.get(i - 2))
                    for j in range(2):
                        for t in range(NT):
                            c0 = IQ + i * HD if j == 0 else IK
                            tr = T.transpose(bank[6 + i % 2][0:HD, (2 * j + t) * P:(2 * j + t + 1) * P],
                                             Z[:, t, c0:c0 + HD], ident[:, :])
                    m = PE.mark(tr)
                    hi = QKH[0:HD, i % 2, 0, :]
                    cut_ = AC.run(K.copy, hi, bank[6 + i % 2][0:HD, :], after=[m, scored.get(i - 2)])
                    turned[i] = DV.run(V.tensor_tensor, QKL[0:HD, i % 2, 0, :], bank[6 + i % 2][0:HD, :],
                                       hi.bitcast(F32), ALU.subtract, after=[cut_, scored.get(i - 2)])
                h = i - 1
                if h >= 0:
                    b = h % 2
                    PE.wait(turned[h], relu.get(h - 2))
                    for t in range(NT):
                        qk, kk = ([x[0:HD, b, 0, c0:c1] for x in (QKH, QKL)] for c0, c1 in ((0, SEQ), (SEQ, 2 * SEQ)))
                        mm = three(halves(b)[:, t, :], qk, kk, t, True, True)
                    scored[h] = PE.mark(mm)
                    relu[h] = AC.run(K.activation, PR[:, b, :, :], halves(b), ACT.Relu,
                                     after=[scored[h], used.get(h - 2)])
                    for t in range(NT):
                        used[h] = DV.run(V.scalar_tensor_tensor, ISC[:, t, :], PR[:, b, t, :],
                                         Z[:, t, IW + h:IW + h + 1], ISC[:, t, :], ALU.mult, ALU.add,
                                         after=[relu[h]])

        def take_largest():
            for r in range(TOPK // 8):
                for t in range(NT):
                    top = ss[:, 32 + 8 * t:40 + 8 * t]
                    DV.run(V.max, top, ISC[:, t, :])
                    DV.run(V.match_replace, ISC[:, t, :], top, ISC[:, t, :], GONE)
                yield
            DV.run(V.tensor_scalar, SEL, ISC, GONE / 2, NEG, ALU.is_gt, ALU.mult)
            DV.run(V.tensor_tensor, SEL, SEL, cmask[:, :, :], ALU.add)


        DV.run(V.memset, mhalf[:, :], -0.5)
        DV.run(V.memset, zb[:, :], 0.0)
        consts = small_loads([(ident[:, :], C["ident"]), (cmask[:, :, :], C["causal"]),
                              (ropeb[:, :, :, :], C["rope_b"]), (ropec[:, :, :, :], C["rope_c"]),
                              (iota[:, :], C["iota"])])
        crow = G[:, 0, 0:P]
        crows = small_loads([
            (G[0:48, 0, 0:P], A["norm_g_2"].rearrange("l j (k p) -> (l j k) p", p=P)),
            (G[48:52, 0, 0:P], A["mla_q_norm"].rearrange("l (k p) -> (l k) p", p=P)),
            (G[52:54, 0, 0:P], A["mla_kv_norm"])])
        xin = small_loads([(U[:, :, :], A["x"].rearrange("a (t p) n -> p (a t) n", p=P))])
        ROW_LN, ROW_Q, ROW_KV = 0, 48, 52


        W1 = [CH, CH, CH, MAIN1 - 3 * CH]
        W2 = [CH] * 6 + [MAIN2 - 6 * CH]

        def stream(w, c0, widths, skip=0):
            for i, width in enumerate(widths):
                if i >= skip:
                    linear_loads(w, c0, width)
                c0 += width

        def stream_branches(wa, wb, wc):
            for m in range(2):
                cs = slice(m * CH, (m + 1) * CH)
                load_step([(rawg[:, k0:k1, :], w[(k0 - r) * P:(k1 - r) * P, cs].rearrange("(k p) n -> p k n", p=P))
                           for w, k0, k1, r in ((wa, 0, 2, 0), (wb, 2, 4, 2), (wb, 4, 6, 2), (wc, 6, 8, 6))])

        BRANCHES1 = [(0, 3, range(0, 2)), (1, 4, range(2, 6)), (2, 5, range(6, 8))]
        BRANCHES2 = [(0, 3, range(0, 2)), (1, 4, range(2, 4)), (2, 5, range(4, 8))]

        linear_loads(A["w_in"][0], 0, CH)
        cut(0, 0)
        PE.wait(crows, consts)
        turned = PE.mark(T.transpose(bank[0][:, 0:54], G[0:54, 0, 0:P], ident[0:54, 0:54]))
        DV.run(V.tensor_copy, cols[:, :], bank[0][:, 0:54], after=[turned])
        rows = norm_rows(A["emb_ln_g"], A["emb_ln_b"], ())
        for t in range(NT):
            for m in range(2):
                row_stats(t, m, after=[xin])
        normed = norm_and_turn(rows, after=[xin, turned])

        QC, KVC, KF = MAIN1, MAIN1 + 384, MAIN1 + 384 + 512

        def prepare_1(l, rowp, biases, latw, wmask, flip, WUQ, WUKV):
            if l == 0:
                angles()
            PE.wait(biases)
            for t in range(NT):
                for j in range(2):
                    pair = nab[:, t, 2 * j:2 * j + 2, :]
                    m = PE.mark(T.matmul(halves(2 * t + j), flip, pair, start=True, stop=True))
                    DV.run(V.tensor_tensor, pair, halves(2 * t + j), wmask.unsqueeze(1).to_broadcast([P, 2, SEQ]),
                           ALU.add, after=[m])
            DV.wait(rowp)
            yield from head_norm(BQ, GQA_HEADS + GQA_KV, [(0, GQA_HEADS, pb[:, 0:HD]), (GQA_HEADS, GQA_KV, pb[:, HD:2 * HD])])
            yield
            for t in range(NT):
                rotate(heads3(Z[:, t, :], BQ, GQA_HEADS + GQA_KV), GQA_HEADS + GQA_KV, HD // 2, ropeb[:, t, :, :])
            for t in range(NT):
                rms_rows(Z[:, t, CDQ:CDQ + QR], Z[:, t, CDQ:CDQ + QR], QR, 1e-6, t)
                rms_rows(Z[:, t, CDKV:CDKV + KVR], Z[:, t, CDKV:CDKV + KVR], KVR, 1e-6, t)
            yield
            PE.wait(DV.last())
            CQT = S[:, 2048:2560].rearrange("p (k n) -> p k n", k=2)
            CKT = S[:, 2560:2816]
            for t in range(NT):
                for k in range(2):
                    T.transpose(halves(6)[:, k, t * P:(t + 1) * P], Z[:, t, CDQ + k * P:CDQ + (k + 1) * P], ident[:, :])
                i = T.transpose(halves(7)[:, 0, t * P:(t + 1) * P], Z[:, t, CDKV:CDKV + P], ident[:, :])
            turned = PE.mark(i)
            for k in range(2):
                DV.run(V.tensor_scalar, CQT[:, k, :], halves(6)[:, k, :],
                       cols[:, ROW_Q + 2 * l + k:ROW_Q + 2 * l + k + 1], None, ALU.mult, after=[turned])
            DV.run(V.tensor_scalar, CKT, halves(7)[:, 0, :], cols[:, ROW_KV + l:ROW_KV + l + 1], None, ALU.mult)
            yield
            PE.wait(DV.last(), latw)
            for t in range(NT):
                for k in range(2):
                    T.matmul(bank[t][:, 0:384], CQT[:, k, t * P:(t + 1) * P], WUQ[:, k, :], start=k == 0, stop=k == 1)
                i = T.matmul(bank[2 + t][:, :], CKT[:, t * P:(t + 1) * P], WUKV, start=True, stop=True)
            up = PE.mark(i)
            for t in range(NT):
                DV.run(V.tensor_copy, Z[:, t, QC:QC + 384], bank[t][:, 0:384], after=[up])
                DV.run(V.tensor_copy, Z[:, t, KVC:KVC + 512], bank[2 + t][:, :])
                rotate(heads3(Z[:, t, :], QC, MLA_HEADS, 96)[:, :, NOPE:], MLA_HEADS, ROPE_C // 2, ropec[:, t, :, :])
                rotate(heads3(Z[:, t, :], CKR, 1, ROPE_C), 1, ROPE_C // 2, ropec[:, t, :, :])
                kf = heads3(Z[:, t, :], KF, MLA_HEADS, 96)
                DV.run(V.tensor_copy, kf[:, :, 0:NOPE], heads3(Z[:, t, :], KVC, MLA_HEADS, 128)[:, :, 0:NOPE])
                DV.run(V.tensor_copy, kf[:, :, NOPE:],
                       heads3(Z[:, t, :], CKR, 1, ROPE_C).to_broadcast([P, MLA_HEADS, ROPE_C]))

        def prepare_2(rowp):
            def gain(j):
                return pb[:, j * HD:(j + 1) * HD]
            DV.wait(rowp)
            yield from head_norm(A2Q, 5, [(0, 4, gain(0)), (4, 1, gain(1))])
            yield from head_norm(B2Q, 8, [(0, 4, gain(2)), (4, 4, gain(3))])
            yield
            yield from head_norm(C2Q, 16, [(0, 8, gain(4)), (8, 8, gain(5))])
            for t in range(NT):
                yield
                for c0, nh in ((A2Q, 5), (IQ, 9), (B2Q, 8), (C2Q, 16)):
                    rotate(heads3(Z[:, t, :], c0, nh), nh, ROT2 // 2, rope2[:, t, :, :])
                DV.run(V.tensor_scalar, Z[:, t, IW:IW + IDX_HEADS], Z[:, t, IW:IW + IDX_HEADS],
                       (IDX_HEADS * HD) ** -0.5, None, ALU.mult)

        for l in range(DEPTH):
            idle = all_idle()
            rowp = small_loads([(pb[:, 0:HD], A["gqa_q_norm"][l].partition_broadcast(P)),
                                (pb[:, HD:2 * HD], A["gqa_k_norm"][l].partition_broadcast(P))], after=idle)
            loads = []
            for t in range(NT):
                for half in range(2):
                    r = 2 * t + half
                    w = 2 * NA_COLS - 1
                    src = A["na_rpb"]
                    off = (l * NA_HEADS * (2 * NA_ROWS - 1) + NA_ROWS - 1 - r) * w + NA_COLS - GRID_W
                    for h in range(NA_HEADS):
                        loads.append((nab[half * 64:(half + 1) * 64, t, h, :].rearrange("p (r c) -> p r c", c=GRID_W),
                                      bass.AP(src.tensor, off + h * (2 * NA_ROWS - 1) * w,
                                              [[1, GRID_W], [w, ROWS], [1, GRID_W]])))
            wmask = S[:, 4096:4096 + SEQ]
            flip = S[:, 4096 + SEQ:4096 + SEQ + P]
            loads += [(wmask, C["window"]), (flip, C["flip"])]
            biases = small_loads(loads, after=idle + ([(s_lod, c.ff)] if c.ff else []))
            WUQ = S[:, 2816:3584].rearrange("p (k n) -> p k n", k=2)
            WUKV = S[:, 3584:4096]
            latw = small_loads([(WUQ, A["mla_w_uq"][l].rearrange("(k p) n -> p k n", p=P)),
                                (WUKV, A["mla_w_ukv"][l])], after=idle)
            stream(A["w_in"][l], 0, W1, skip=1 if l == 0 else 0)
            stream(A["w_in"][l], MAIN1, [CH] * 6)
            stream_branches(A["w_proj_a"][l], A["w_proj_b"][l], A["w_proj_c"][l])
            stream(A["w_out"][l], 0, [CH] * 2)
            stream(A["mem_wkv"][l], 0, [CH] * 4)
            stream(A["mem_wq"][l], 0, [CH] * 2)
            stream(A["mem_wo"][l], 0, [CH] * 2)

            PE.wait(normed)
            linear(4, to_tokens(Z, W1), widths=W1)
            AC.eng.preload_act_table(ACT.Sigmoid)
            linear(6, to_gates, beside=prepare_1(l, rowp, biases, latw, wmask, flip, WUQ, WUKV))
            hs = [head(zc(AQ + h * HD), zc(AK + h * HD), zc(AV + h * HD), uc(h * HD), HD ** -0.5,
                       bias=nab[:, :, h, :]) for h in range(NA_HEADS)]
            hs += [head(zc(BQ + h * HD), zc(BK + h // 4 * HD), zc(BV + h // 4 * HD), uc(256 + h * HD), HD ** -0.5)
                   for h in range(GQA_HEADS)]
            hs += [head(zc(QC + h * 96, 96), zc(KF + h * 96, 96), zc(KVC + h * 128 + NOPE), uc(768 + h * VC),
                        (NOPE + ROPE_C) ** -0.5, dk=96) for h in range(MLA_HEADS)]
            idle = all_idle()
            attention(hs, after=idle)
            rows = norm_rows(A["ln_g"][l, 0], A["ln_b"][l, 0], after=idle)
            if l % 2 == 0:
                ffn_all_loads(*(A["ffn_w_gu"][l // 2][:, m * DFF:(m + 1) * DFF] for m in range(2)))

            PE.wait(turn(U, after=all_idle()))
            linear(2, merge, groups=BRANCHES1)
            PE.wait(turn(U, after=all_idle()))
            mem = small_loads([(MEM, A["mem"].rearrange("a (t p) n -> p (a t) n", p=P))], after=all_idle())
            linear(2, add_residual)

            PE.wait(turn(MEM, after=[mem] + all_idle()))
            linear(4, to_tokens(Z), beside=layer_norm(rows, after=all_idle()))
            rows = norm_rows(A["ln_g"][l, 1], A["ln_b"][l, 1], after=all_idle())
            PE.wait(turn(H, after=all_idle()))
            linear(2, to_tokens(G))
            w = D // MEM_HEADS

            def mem_head(h):
                return head(lambda t, k: G[:, t, h * w + k * P:h * w + (k + 1) * P],
                            lambda t, k: Z[:, t, h * w + k * P:h * w + (k + 1) * P],
                            lambda t: Z[:, t, D + h * w:D + (h + 1) * w], uc(h * w, w), w ** -0.5, dk=P, dv=w, nk=2)
            if l % 2 == 1:
                router = router_loads(l // 2, all_idle())
            attention([mem_head(h) for h in range(MEM_HEADS)], after=all_idle())
            g_free = all_idle()
            PE.wait(turn(U, after=all_idle()))
            linear(2, add_residual, last=l % 2 == 1)
            normed = norm_and_turn(rows, after=all_idle())

            PE.wait(normed)
            rows = norm_rows(A["ln_g"][l, 2], A["ln_b"][l, 2], after=all_idle())
            if l % 2 == 0:
                done = ffn(NFF, A["ffn_w_down"][l // 2], after=all_idle())
                for t in range(NT):
                    for m in range(2):
                        cs = slice(m * CH, (m + 1) * CH)
                        DV.run(V.scalar_tensor_tensor, U[:, t, cs], H[:, t, cs], ALPHA, bank[2 * t + m][:, :],
                               ALU.mult, ALU.add, after=[done[t]])
                        row_stats(t, m)
            else:
                moe(l // 2, g_free, router)
                half_ffn_loads(0, 0)
                for t in range(NT):
                    for m in range(2):
                        row_stats(t, m)
            normed = norm_and_turn(rows, after=all_idle(), turned=l < DEPTH - 1)
            if l == DEPTH - 1:
                cut(c.step, c.step % 2)

        for l in range(DEPTH):
            last = l == DEPTH - 1
            if l > 0:
                half_ffn_loads(l, 0)
            half_ffn(l, 0)
            idle = all_idle()
            rowp = small_loads([(pb[:, 0:6 * HD], A["qk_norm_g_2"][l].rearrange("a b -> (a b)").partition_broadcast(P)),
                                (pb[:, 384:512], A["diff_subln_g_2"][l].partition_broadcast(P)),
                                (pb[:, 512:768], A["lambda_params_2"][l].rearrange("a b -> (a b)").partition_broadcast(P))],
                               after=idle)
            stream(A["w_in_2"][l], 0, W2)
            stream(A["w_in_2"][l], MAIN2, [CH] * 6)
            stream(A["w_branch_2"][l], 0, [CH] * 2)
            stream(A["w_out_2"][l], 0, [CH] * 2)
            PE.wait(rms_and_turn(cols[:, (3 * l + 1) * KT:(3 * l + 2) * KT], all_idle()))
            linear(7, to_tokens(Z, W2), widths=W2)
            AC.eng.preload_act_table(ACT.Sigmoid)
            linear(6, to_gates, beside=prepare_2(rowp))
            init = 0.8 - 0.6 * float(np.exp(-0.3 * l))
            for j in range(2):
                DV.run(V.tensor_tensor_reduce, S[:, 0:HD], pb[:, 512 + 2 * j * HD:512 + (2 * j + 1) * HD],
                       pb[:, 512 + (2 * j + 1) * HD:512 + (2 * j + 2) * HD], 1.0, 0.0, ALU.mult, ALU.add,
                       lam[:, j:j + 1])
            e = AC.run(K.activation, lam[:, 2:4], lam[:, 0:2], ACT.Exp, after=[DV.last()])
            DV.run(V.tensor_tensor, lam[:, 4:5], lam[:, 3:4], lam[:, 2:3], ALU.subtract, after=[e])
            DV.run(V.tensor_scalar, lam[:, 4:5], lam[:, 4:5], -init, None, ALU.add)
            score_keys()
            hs = [head(zc(B2Q + h * HD), zc(B2K + h * HD), zc(B2V + h * HD), uc(256 + h * HD), HD ** -0.5,
                        bias=cmask) for h in range(4)]
            hs += [head(zc(C2Q + (2 * h + j) * HD), zc(C2K + (2 * h + j) * HD), zc(C2V + h * P, P),
                        uc(512 + h * P, P), HD ** -0.5, dv=P, bias=cmask, weight=lam[:, 4:5] if j else None)
                   for h in range(4) for j in range(2)]
            hs += [head(zc(A2Q + h * HD), zc(A2K), zc(A2V), uc(h * HD), HD ** -0.5, bias=SEL) for h in range(4)]
            attention(hs, after=all_idle(), beside=take_largest())
            half_ffn_loads(l, 1)

            def own_norm(r):
                if r == 0:
                    for t in range(NT):
                        sq = S[:, 0:D // 2]
                        DV.run(V.tensor_tensor, sq, U[:, t, D // 2:], U[:, t, D // 2:], ALU.mult)
                        DV.run(V.tensor_reduce, ss[:, 4 * t:4 * t + 4], sq.rearrange("p (h d) -> p h d", d=P),
                               AX.X, ALU.add)
                    e = DV.run(V.tensor_scalar, ss[:, 0:8], ss[:, 0:8], 1.0 / P, 1e-6, ALU.mult, ALU.add)
                    rsqrt(rs[:, 0:8], ss[:, 0:8], after=[e])
                    DV.run(V.tensor_scalar, pb[:, 384:512], pb[:, 384:512], 1.0 - init, None, ALU.mult)
                if r < 2:
                    return []
                for t in range(NT):
                    h = 2 * (r - 2)
                    x = U[:, t, 2 * r * P:(2 * r + 2) * P].rearrange("p (h d) -> p h d", d=P)
                    DV.run(V.tensor_tensor, x, x, rs[:, 4 * t + h:4 * t + h + 2].unsqueeze(2).to_broadcast([P, 2, P]),
                           ALU.mult, after=[PO.last()])
                    DV.run(V.tensor_tensor, x, x, pb[:, 384:512].unsqueeze(1).to_broadcast([P, 2, P]), ALU.mult)
                return [DV.last()]
            PE.wait(turn(U, after=all_idle(), prepare=own_norm))
            linear(2, merge, groups=BRANCHES2)
            PE.wait(turn(U, after=all_idle()))
            linear(2, add_to_h)
            half_ffn(l, 1, last=last)
        store_and_end(H[:, :, :])


INPUTS = ["x", "mem", "emb_ln_g", "emb_ln_b", "w_in", "na_rpb", "gqa_q_norm", "gqa_k_norm", "mla_q_norm",
          "mla_kv_norm", "mla_w_uq", "mla_w_ukv", "w_proj_a", "w_proj_b", "w_proj_c", "w_out", "mem_wq", "mem_wkv",
          "mem_wo", "ln_g", "ln_b", "ffn_w_gu", "ffn_w_down", "moe_router", "moe_w_gu", "moe_w_down",
          "positions_2", "norm_g_2", "w_in_2", "qk_norm_g_2", "lambda_params_2", "diff_subln_g_2", "w_branch_2",
          "w_out_2", "ffn_w_gate_2", "ffn_w_up_2", "ffn_w_down_2"]


def shape_constants():
    f = np.float32
    t = np.arange(SEQ)
    row, col = (t // GRID_W).astype(f), (t % GRID_W).astype(f)

    def axial(dim):
        n = dim // 4
        inv = (f(10000.0) ** (-np.arange(n, dtype=f) / f(n))).astype(f)
        ang = np.concatenate([row[:, None] * inv, col[:, None] * inv], axis=1)
        c, s = np.cos(ang).astype(f), np.sin(ang).astype(f)
        tab = np.stack([np.concatenate([c, c], 1), np.concatenate([-s, s], 1)], axis=1)
        return np.ascontiguousarray(tab.reshape(NT, P, 2, dim).transpose(1, 0, 2, 3))
    causal = np.where(t[None, :] <= t[:, None], 0.0, NEG).astype(f).reshape(NT, P, SEQ).transpose(1, 0, 2)
    c = np.arange(GRID_W)
    first = np.clip(c - NA_COLS // 2, 0, GRID_W - NA_COLS)[:, None]
    window = np.where((c[None, :] >= first) & (c[None, :] < first + NA_COLS), 0.0, NEG).astype(f)
    inv2 = (500000.0 ** (-np.arange(0, ROT2, 2) / ROT2)).astype(f)
    return {"ident": np.eye(P, dtype=f), "causal": np.ascontiguousarray(causal), "rope_b": axial(HD),
            "rope_c": axial(ROPE_C), "flip": np.kron(np.eye(P // GRID_W, dtype=f), np.eye(GRID_W, dtype=f)[::-1]),
            "window": np.tile(window, (P // GRID_W, ROWS)),
            "inv_freq": np.tile(inv2, (P, 1)), "before": np.triu(np.ones((P, P), f), 1), "ones": np.ones((P, P), f),
            "slots": np.tile(np.arange(P, dtype=f), (P, 1)), "iota": np.tile(np.arange(EXPERTS, dtype=f), (P, 1))}


def kernel(**inputs):
    import concourse.bacc as bacc
    from concourse.bass_utils import run_bass_kernel_spmd
    nc = bacc.Bacc("TRN2", target_bir_lowering=False, num_devices=1, dynamic_dma_scratch_size=4096)
    arrays = {}

    def given(name, a):
        a = np.ascontiguousarray(a)
        arrays[name] = a
        return nc.dram_tensor(name, a.shape, mybir.dt.from_np(a.dtype), kind="ExternalInput").ap()
    A = {name: given(f"in_{name}", inputs[name]) for name in INPUTS}
    C = {name: given(f"const_{name}", a) for name, a in shape_constants().items()}
    out = nc.dram_tensor("out", (1, SEQ, D), F32, kind="ExternalOutput").ap()
    program(nc, A, C, out)
    return run_bass_kernel_spmd(nc, [arrays], core_ids=[0]).results[0]["out"]
```
